# Optimizing a Trainium2 kernel written in Bass

```python
import math
import jax, jax.numpy as jnp
from jax import lax
import numpy as np

D_MODEL = 1024
BATCH = 1
SEQ = 256
DEPTH = 1

GRID_W = 64
CTX_LEN = 256
NORM_EPS = 1e-6
ROPE_BASE = 10000.0
MASK_VALUE = -1e30

DA_HEADS = 4
DA_HEAD_DIM = 64
Q_BLOCK = 128
WA_HEADS = 8
WA_KV_HEADS = 2
WA_GROUP = WA_HEADS // WA_KV_HEADS
WA_HEAD_DIM = 64
WINDOW = 128
BAND_BLOCK = WINDOW

QA_COLS = DA_HEADS * 2 * DA_HEAD_DIM
KA_COLS = DA_HEADS * 2 * DA_HEAD_DIM
VA_COLS = DA_HEADS * 2 * DA_HEAD_DIM
QB_COLS = WA_HEADS * WA_HEAD_DIM
KB_COLS = WA_KV_HEADS * WA_HEAD_DIM
VB_COLS = WA_KV_HEADS * WA_HEAD_DIM
IN_COLS = QA_COLS + KA_COLS + VA_COLS + QB_COLS + KB_COLS + VB_COLS
SPLIT_POINTS = [QA_COLS, QA_COLS + KA_COLS, QA_COLS + KA_COLS + VA_COLS,
                QA_COLS + KA_COLS + VA_COLS + QB_COLS,
                QA_COLS + KA_COLS + VA_COLS + QB_COLS + KB_COLS]
DA_OUT = DA_HEADS * 2 * DA_HEAD_DIM
WA_OUT = WA_HEADS * WA_HEAD_DIM
MIX_WIDTH = DA_OUT + WA_OUT

N_EXPERTS = 32
TOP_K = 4
D_EXPERT = 1024
SWIGLU_LIMIT = 7.0
SWIGLU_ALPHA = 1.702
EXPERT_BLOCK = 128


def rmsnorm(x, g):
    xf = x.astype(jnp.float32)
    y = xf * lax.rsqrt(jnp.mean(xf * xf, axis=-1, keepdims=True) + NORM_EPS)
    return (y * g.astype(jnp.float32)).astype(x.dtype)

def adaln(cvec, w_mod, b_mod):
    mod = jax.nn.silu(cvec) @ w_mod + b_mod
    return jnp.split(mod, 6, axis=-1)

def modulate(h, shift, scale):
    return h * (1.0 + scale) + shift

def rope_tables(n_tok, head_dim):
    rows_count = n_tok // GRID_W
    rows = jnp.repeat(jnp.arange(rows_count), GRID_W).astype(jnp.float32)
    cols = jnp.tile(jnp.arange(GRID_W), rows_count).astype(jnp.float32)
    nf = head_dim // 4
    inv = ROPE_BASE ** (-jnp.arange(nf, dtype=jnp.float32) / nf)
    ang_r = rows[:, None] * inv
    ang_c = cols[:, None] * inv
    return (jnp.cos(ang_r), jnp.sin(ang_r), jnp.cos(ang_c), jnp.sin(ang_c))

def _rotate(xh, cos, sin):
    nf = xh.shape[-1] // 2
    x1, x2 = xh[..., :nf], xh[..., nf:]
    return jnp.concatenate([x1 * cos - x2 * sin, x2 * cos + x1 * sin], axis=-1)

def axial_rope(x, tabs):
    d = x.shape[-1]
    da = d // 2
    shape = (1, x.shape[1]) + (1,) * (x.ndim - 3) + (da // 2,)
    cr, sr, cc, sc = [t.reshape(shape).astype(x.dtype) for t in tabs]
    return jnp.concatenate([_rotate(x[..., :da], cr, sr), _rotate(x[..., da:], cc, sc)], axis=-1)

def split_proj(p):
    B, N, _ = p.shape
    qa, ka, va, qb, kb, vb = jnp.split(p, SPLIT_POINTS, axis=-1)
    qa = qa.reshape(B, N, DA_HEADS, 2, DA_HEAD_DIM)
    ka = ka.reshape(B, N, DA_HEADS, 2, DA_HEAD_DIM)
    va = va.reshape(B, N, DA_HEADS, 2 * DA_HEAD_DIM)
    qb = qb.reshape(B, N, WA_KV_HEADS, WA_GROUP, WA_HEAD_DIM)
    kb = kb.reshape(B, N, WA_KV_HEADS, WA_HEAD_DIM)
    vb = vb.reshape(B, N, WA_KV_HEADS, WA_HEAD_DIM)
    return qa, ka, va, qb, kb, vb

def diff_attend(q, k, v, lam):
    s = jnp.einsum('bqhcd,bkhcd->bhcqk', q, k).astype(jnp.float32)
    p = jax.nn.softmax(s, axis=-1)
    a = p[:, :, 0] - lam * p[:, :, 1]
    return jnp.einsum('bhqk,bkhe->bqhe', a.astype(v.dtype), v)

def diff_attend_latent(q, k_all, v_all, lam):
    B, S, H, _, d = q.shape
    nqb = S // Q_BLOCK
    qb = jnp.moveaxis(q.reshape(B, nqb, Q_BLOCK, H, 2, d), 1, 0)
    out = lax.map(lambda qq: diff_attend(qq, k_all, v_all, lam), qb)
    return jnp.moveaxis(out, 0, 1).reshape(B, S, H, 2 * d)

def diff_post(o, subln_g, lam_init):
    B, N = o.shape[:2]
    return (rmsnorm(o, subln_g) * (1.0 - lam_init)).reshape(B, N, DA_OUT)

def window_gqa_latent(q, k, v, k_ctx, v_ctx, sink):
    B, S, KV, G, d = q.shape
    W = BAND_BLOCK
    nb = S // W
    pad = ((0, 0), (W, W), (0, 0), (0, 0))
    kp = jnp.pad(k, pad).reshape(B, nb + 2, W, KV, d)
    vp = jnp.pad(v, pad).reshape(B, nb + 2, W, KV, d)
    kband = jnp.concatenate([kp[:, :-2], kp[:, 1:-1], kp[:, 2:]], axis=2)
    vband = jnp.concatenate([vp[:, :-2], vp[:, 1:-1], vp[:, 2:]], axis=2)
    qbk = q.reshape(B, nb, W, KV, G, d)
    s_loc = jnp.einsum('bnqkgd,bnjkd->bnkgqj', qbk, kband).astype(jnp.float32)
    s_ctx = jnp.einsum('bnqkgd,bjkd->bnkgqj', qbk, k_ctx).astype(jnp.float32)
    n_i = jnp.arange(nb)[:, None, None]
    q_i = jnp.arange(W)[None, :, None]
    k_j = jnp.arange(3 * W)[None, None, :]
    kpos = (n_i - 1) * W + k_j
    rel = k_j - W - q_i
    valid = (jnp.abs(rel) <= WINDOW) & (kpos >= 0) & (kpos < S)
    s_loc = jnp.where(valid[None, :, None, None], s_loc, MASK_VALUE)
    sink_col = jnp.broadcast_to(sink.astype(jnp.float32).reshape(1, 1, KV, G, 1, 1),
                                s_loc.shape[:-1] + (1,))
    p = jax.nn.softmax(jnp.concatenate([s_loc, s_ctx, sink_col], axis=-1), axis=-1)
    p_loc = p[..., :3 * W].astype(v.dtype)
    p_ctx = p[..., 3 * W:-1].astype(v.dtype)
    o = (jnp.einsum('bnkgqj,bnjkd->bnqkgd', p_loc, vband)
         + jnp.einsum('bnkgqj,bjkd->bnqkgd', p_ctx, v_ctx))
    return o.reshape(B, S, WA_OUT)

def sink_attend_ctx(q, k, v, sink):
    B, C, KV, G, d = q.shape
    s = jnp.einsum('bqkgd,bjkd->bkgqj', q, k).astype(jnp.float32)
    sink_col = jnp.broadcast_to(sink.astype(jnp.float32).reshape(1, KV, G, 1, 1), s.shape[:-1] + (1,))
    p = jax.nn.softmax(jnp.concatenate([s, sink_col], axis=-1), axis=-1)[..., :-1]
    o = jnp.einsum('bkgqj,bjkd->bqkgd', p.astype(v.dtype), v)
    return o.reshape(B, C, WA_OUT)

def moe(x2d, w_r, b_r, w_gu, b_gu, w_dn, b_dn):
    T, D = x2d.shape
    logits = (x2d @ w_r + b_r).astype(jnp.float32)
    top_v, top_i = lax.top_k(logits, TOP_K)
    gates = jax.nn.softmax(top_v, axis=-1)
    flat_e = top_i.reshape(-1).astype(jnp.int32)
    n_assign = T * TOP_K
    order = jnp.argsort(flat_e)
    sorted_e = flat_e[order]
    counts = jnp.zeros((N_EXPERTS,), jnp.int32).at[flat_e].add(1)
    padded = ((counts + EXPERT_BLOCK - 1) // EXPERT_BLOCK) * EXPERT_BLOCK
    start = jnp.cumsum(counts) - counts
    pend = jnp.cumsum(padded)
    pstart = pend - padded
    rank = jnp.arange(n_assign, dtype=jnp.int32) - start[sorted_e]
    dest_sorted = (pstart[sorted_e] + rank).astype(jnp.int32)
    n_rows = n_assign + N_EXPERTS * EXPERT_BLOCK
    n_blocks = n_rows // EXPERT_BLOCK
    row_tok = jnp.full((n_rows,), T, jnp.int32).at[dest_sorted].set((order // TOP_K).astype(jnp.int32))
    block_start = jnp.arange(n_blocks, dtype=jnp.int32) * EXPERT_BLOCK
    block_exp = jnp.clip(jnp.searchsorted(pend, block_start, side='right'), 0, N_EXPERTS - 1)
    x_pad = jnp.concatenate([x2d, jnp.zeros((1, D), x2d.dtype)], axis=0)

    def expert_block(args):
        tok, e = args
        xb = x_pad[tok]
        h = xb @ w_gu[e] + b_gu[e]
        g = jnp.minimum(h[:, ::2], SWIGLU_LIMIT)
        lin = jnp.clip(h[:, 1::2], -SWIGLU_LIMIT, SWIGLU_LIMIT)
        a = g * jax.nn.sigmoid(SWIGLU_ALPHA * g) * (lin + 1.0)
        return a @ w_dn[e] + b_dn[e]

    rows = lax.map(expert_block, (row_tok.reshape(n_blocks, EXPERT_BLOCK), block_exp))
    rows = rows.reshape(n_rows, D)
    dest = jnp.zeros((n_assign,), jnp.int32).at[order].set(dest_sorted)
    y = rows[dest].reshape(T, TOP_K, D)
    return jnp.einsum('tk,tkd->td', gates.astype(y.dtype), y)

def first_inputs(seed: int = 0) -> dict:
    key = jax.random.key(seed)
    ks = jax.random.split(key, 24)
    D, L, E, F = D_MODEL, DEPTH, N_EXPERTS, D_EXPERT
    nrm = lambda k, s: jax.random.normal(k, s, jnp.float32)
    return {
        "x": nrm(ks[0], (BATCH, SEQ, D)),
        "c": nrm(ks[1], (BATCH, D)),
        "ctx": nrm(ks[2], (BATCH, CTX_LEN, D)),
        "c_ctx": nrm(ks[3], (D,)),
        "w_mod": nrm(ks[4], (L, D, 6 * D)) * (0.5 * D ** -0.5),
        "b_mod": nrm(ks[5], (L, 6 * D)) * 0.02,
        "norm1_g": 1.0 + 0.05 * nrm(ks[6], (L, D)),
        "w_in": nrm(ks[7], (L, D, IN_COLS)) * D ** -0.5,
        "lam_q1": 0.1 * nrm(ks[8], (L, DA_HEAD_DIM)),
        "lam_k1": 0.1 * nrm(ks[9], (L, DA_HEAD_DIM)),
        "lam_q2": 0.1 * nrm(ks[10], (L, DA_HEAD_DIM)),
        "lam_k2": 0.1 * nrm(ks[11], (L, DA_HEAD_DIM)),
        "subln_g": 1.0 + 0.05 * nrm(ks[12], (L, 2 * DA_HEAD_DIM)),
        "sink": 0.5 * nrm(ks[13], (L, WA_HEADS)),
        "w_out": nrm(ks[14], (L, MIX_WIDTH, D)) * MIX_WIDTH ** -0.5,
        "norm2_g": 1.0 + 0.05 * nrm(ks[15], (L, D)),
        "w_router": nrm(ks[16], (L, D, E)) * D ** -0.5,
        "b_router": 0.01 * nrm(ks[17], (L, E)),
        "w_gate_up": nrm(ks[18], (L, E, D, 2 * F)) * D ** -0.5,
        "b_gate_up": 0.01 * nrm(ks[19], (L, E, 2 * F)),
        "w_down": nrm(ks[20], (L, E, F, D)) * F ** -0.5,
        "b_down": 0.01 * nrm(ks[21], (L, E, D)),
        "final_g": 1.0 + 0.05 * nrm(ks[22], (D,)),
    }

def first_block(x, c, ctx, c_ctx, w_mod, b_mod, norm1_g, w_in, lam_q1, lam_k1, lam_q2, lam_k2,
              subln_g, sink, w_out, norm2_g, w_router, b_router, w_gate_up, b_gate_up,
              w_down, b_down, final_g):
    B, S, D = x.shape
    C = ctx.shape[1]
    ROWS = S // GRID_W
    tabs = rope_tables(ROWS * GRID_W, DA_HEAD_DIM)
    scale_a = DA_HEAD_DIM ** -0.5
    scale_b = WA_HEAD_DIM ** -0.5
    cs = ctx
    for l in range(DEPTH):
        lam_init = 0.8 - 0.6 * math.exp(-0.3 * l)
        sh1, sc1, g1, sh2, sc2, g2 = [m[:, None, :] for m in adaln(c, w_mod[l], b_mod[l])]
        csh1, csc1, cg1, csh2, csc2, cg2 = [m[None, None, :] for m in adaln(c_ctx, w_mod[l], b_mod[l])]

        hx = modulate(rmsnorm(x, norm1_g[l]), sh1, sc1)
        hc = modulate(rmsnorm(cs, norm1_g[l]), csh1, csc1)
        qa, ka, va, qb, kb, vb = split_proj(hx @ w_in[l])
        qac, kac, vac, qbc, kbc, vbc = split_proj(hc @ w_in[l])
        qa = axial_rope(qa * scale_a, tabs)
        ka = axial_rope(ka, tabs)
        qb = axial_rope(qb * scale_b, tabs)
        kb = axial_rope(kb, tabs)
        lam = (jnp.exp(jnp.sum(lam_q1[l].astype(jnp.float32) * lam_k1[l].astype(jnp.float32)))
               - jnp.exp(jnp.sum(lam_q2[l].astype(jnp.float32) * lam_k2[l].astype(jnp.float32)))
               + lam_init)
        ya = diff_attend_latent(qa, jnp.concatenate([ka, kac], axis=1),
                                jnp.concatenate([va, vac], axis=1), lam)
        ya = diff_post(ya, subln_g[l], lam_init)
        yb = window_gqa_latent(qb, kb, vb, kbc, vbc, sink[l])
        x = x + g1 * (jnp.concatenate([ya, yb], axis=-1) @ w_out[l])
        if l < DEPTH - 1:
            yac = diff_post(diff_attend(qac * scale_a, kac, vac, lam), subln_g[l], lam_init)
            ybc = sink_attend_ctx(qbc * scale_b, kbc, vbc, sink[l])
            cs = cs + cg1 * (jnp.concatenate([yac, ybc], axis=-1) @ w_out[l])

        hx2 = modulate(rmsnorm(x, norm2_g[l]), sh2, sc2)
        x = x + g2 * moe(hx2.reshape(B * S, D), w_router[l], b_router[l], w_gate_up[l],
                         b_gate_up[l], w_down[l], b_down[l]).reshape(B, S, D)
        if l < DEPTH - 1:
            hc2 = modulate(rmsnorm(cs, norm2_g[l]), csh2, csc2)
            cs = cs + cg2 * moe(hc2.reshape(B * C, D), w_router[l], b_router[l], w_gate_up[l],
                                b_gate_up[l], w_down[l], b_down[l]).reshape(B, C, D)
    return rmsnorm(x, final_g)


MOBA_HEADS = 8
MOBA_HEAD_DIM = 64
MOBA_BLOCK = 256
MOBA_TOPK = 3
MOBA_QCHUNK = 64
SWA_Q_HEADS = 8
SWA_KV_HEADS = 2
SWA_HEAD_DIM = 64
SWA_WINDOW = 128
SWA_BLOCK = 128
MEM_HEADS = 4
MEM_HEAD_DIM = 128
MEM_LEN = 256
NUM_BUCKETS = 32
MAX_EXACT = NUM_BUCKETS // 2
REL_MAX_DISTANCE = 128
N_SELF_HEADS = MOBA_HEADS + SWA_Q_HEADS
FFN_HIDDEN = 2816
CONV_WIDTH = 3
RMS_EPS = 1e-6
MOBA_W = MOBA_HEADS * MOBA_HEAD_DIM
SWA_QW = SWA_Q_HEADS * SWA_HEAD_DIM
SWA_KVW = SWA_KV_HEADS * SWA_HEAD_DIM
MEM_W = MEM_HEADS * MEM_HEAD_DIM
IN_SPLITS = (MOBA_W, MOBA_W, MOBA_W, SWA_QW, SWA_KVW, SWA_KVW, MEM_W, D_MODEL, D_MODEL, D_MODEL)
IN_WIDTH = 3 * MOBA_W + SWA_QW + 2 * SWA_KVW + MEM_W + 3 * D_MODEL


def rmsnorm_2(x, g):
    xf = x.astype(jnp.float32)
    r = lax.rsqrt(jnp.mean(xf * xf, axis=-1, keepdims=True) + RMS_EPS)
    return (xf * r * g.astype(jnp.float32)).astype(x.dtype)

def t5_bucket(dist):
    n = jnp.maximum(dist, 0)
    nf = jnp.maximum(n, 1).astype(jnp.float32)
    large = MAX_EXACT + (jnp.log(nf / MAX_EXACT) / math.log(REL_MAX_DISTANCE / MAX_EXACT)
                         * (NUM_BUCKETS - MAX_EXACT)).astype(jnp.int32)
    large = jnp.minimum(large, NUM_BUCKETS - 1)
    return jnp.where(n < MAX_EXACT, n, large)

def moba_attention(q, k, v, bias_table):
    B_, S_, H, dh = q.shape
    Sp = -(-S_ // MOBA_BLOCK) * MOBA_BLOCK
    pad = Sp - S_
    if pad:
        padw = ((0, 0), (0, pad), (0, 0), (0, 0))
        q, k, v = jnp.pad(q, padw), jnp.pad(k, padw), jnp.pad(v, padw)
    NB = Sp // MOBA_BLOCK
    scale = 1.0 / math.sqrt(dh)
    qh = q.transpose(0, 2, 1, 3)
    kb = k.reshape(B_, NB, MOBA_BLOCK, H, dh).transpose(0, 3, 1, 2, 4)
    vb = v.reshape(B_, NB, MOBA_BLOCK, H, dh).transpose(0, 3, 1, 2, 4)
    kmean = jnp.mean(kb.astype(jnp.float32), axis=3)
    gate = jnp.einsum('bhsd,bhnd->bhsn', qh.astype(jnp.float32), kmean)
    qblk = jnp.arange(Sp) // MOBA_BLOCK
    past = jnp.arange(NB)[None, :] < qblk[:, None]
    gate = jnp.where(past, gate, -jnp.inf)
    k_sel = min(MOBA_TOPK, NB)
    _, sel = lax.top_k(gate, k_sel)
    sel_valid = jnp.arange(k_sel)[None, :] < qblk[:, None]
    bi = jnp.arange(B_)[:, None, None, None]
    hi = jnp.arange(H)[None, :, None, None]
    hb = jnp.arange(H)[None, :, None, None, None]
    kpos_in = jnp.arange(MOBA_BLOCK)

    def chunk(i):
        q0 = i * MOBA_QCHUNK
        qc = lax.dynamic_slice_in_dim(qh, q0, MOBA_QCHUNK, axis=2)
        selc = lax.dynamic_slice_in_dim(sel, q0, MOBA_QCHUNK, axis=2)
        validc = lax.dynamic_slice_in_dim(sel_valid, q0, MOBA_QCHUNK, axis=0)
        c = q0 // MOBA_BLOCK
        kg = kb[bi, hi, selc]
        vg = vb[bi, hi, selc]
        k_own = lax.dynamic_index_in_dim(kb, c, axis=2, keepdims=False)
        v_own = lax.dynamic_index_in_dim(vb, c, axis=2, keepdims=False)
        qpos = q0 + jnp.arange(MOBA_QCHUNK)
        kpos_sel = selc[..., None] * MOBA_BLOCK + kpos_in
        s_sel = (jnp.einsum('bhqd,bhqnkd->bhqnk', qc, kg).astype(jnp.float32) * scale
                 + bias_table[hb, t5_bucket(qpos[:, None, None] - kpos_sel)].astype(jnp.float32))
        s_sel = jnp.where(validc[:, :, None], s_sel, -jnp.inf)
        dist_own = qpos[:, None] - (c * MOBA_BLOCK + kpos_in)[None, :]
        s_own = (jnp.einsum('bhqd,bhkd->bhqk', qc, k_own).astype(jnp.float32) * scale
                 + bias_table[:, t5_bucket(dist_own)].astype(jnp.float32))
        s_own = jnp.where(dist_own >= 0, s_own, -jnp.inf)
        s_all = jnp.concatenate(
            [s_sel.reshape(B_, H, MOBA_QCHUNK, k_sel * MOBA_BLOCK), s_own], axis=-1)
        p = jax.nn.softmax(s_all, axis=-1).astype(v.dtype)
        p_sel = p[..., :k_sel * MOBA_BLOCK].reshape(B_, H, MOBA_QCHUNK, k_sel, MOBA_BLOCK)
        p_own = p[..., k_sel * MOBA_BLOCK:]
        return (jnp.einsum('bhqnk,bhqnkd->bhqd', p_sel, vg)
                + jnp.einsum('bhqk,bhkd->bhqd', p_own, v_own))

    outs = lax.map(chunk, jnp.arange(Sp // MOBA_QCHUNK))
    out = outs.transpose(1, 0, 3, 2, 4).reshape(B_, Sp, H, dh)
    return out[:, :S_]

def swa_attention(q, k, v, sinks, bias_table):
    B_, S_, HQ, dh = q.shape
    HKV = k.shape[2]
    G = HQ // HKV
    QB = SWA_BLOCK
    nblk = S_ // QB
    scale = 1.0 / math.sqrt(dh)
    qb = q.reshape(B_, nblk, QB, HKV, G, dh)
    kb = k.reshape(B_, nblk, QB, HKV, dh)
    vb = v.reshape(B_, nblk, QB, HKV, dh)
    padw = ((0, 0), (1, 0), (0, 0), (0, 0), (0, 0))
    kband = jnp.concatenate([jnp.pad(kb, padw)[:, :-1], kb], axis=2)
    vband = jnp.concatenate([jnp.pad(vb, padw)[:, :-1], vb], axis=2)
    s = jnp.einsum('bnqhgd,bnkhd->bhgnqk', qb, kband).astype(jnp.float32) * scale
    dist = QB + jnp.arange(QB)[:, None] - jnp.arange(2 * QB)[None, :]
    bias = bias_table[:, t5_bucket(dist)].astype(jnp.float32).reshape(HKV, G, 1, QB, 2 * QB)
    s = s + bias
    kpos = (jnp.arange(nblk)[:, None] - 1) * QB + jnp.arange(2 * QB)[None, :]
    allowed = ((dist >= 0) & (dist < SWA_WINDOW))[None] & (kpos >= 0)[:, None, :]
    s = jnp.where(allowed, s, -jnp.inf)
    sink = sinks.astype(jnp.float32).reshape(HKV, G, 1, 1, 1)
    m = jnp.maximum(jnp.max(s, axis=-1, keepdims=True), sink)
    p = jnp.exp(s - m)
    denom = jnp.sum(p, axis=-1, keepdims=True) + jnp.exp(sink - m)
    p = (p / denom).astype(v.dtype)
    o = jnp.einsum('bhgnqk,bnkhd->bnqhgd', p, vband)
    return o.reshape(B_, S_, HQ * dh)

def memory_attention(q, km, vm):
    B_, S_, Hm, dm = q.shape
    s = jnp.einsum('bshd,bmhd->bhsm', q, km).astype(jnp.float32) * (1.0 / math.sqrt(dm))
    p = jax.nn.softmax(s, axis=-1).astype(vm.dtype)
    return jnp.einsum('bhsm,bmhd->bshd', p, vm).reshape(B_, S_, Hm * dm)

def causal_depthwise_conv(u, w, b):
    S_ = u.shape[1]
    up = jnp.pad(u, ((0, 0), (CONV_WIDTH - 1, 0), (0, 0)))
    out = b.astype(u.dtype)
    for t in range(CONV_WIDTH):
        out = out + w[t].astype(u.dtype) * up[:, t:t + S_]
    return out

def _normal(k, shape, scale):
    return jax.random.normal(k, shape, jnp.float32) * scale

def second_inputs(seed: int = 0) -> dict:
    key = jax.random.key(seed)
    ks = jax.random.split(key, 20)
    L, D, F = DEPTH, D_MODEL, FFN_HIDDEN
    return {
        "x": _normal(ks[0], (BATCH, SEQ, D), 1.0),
        "mem": _normal(ks[1], (BATCH, MEM_LEN, D), 1.0),
        "norm_mix_pre": 1.0 + _normal(ks[2], (L, D), 0.05),
        "norm_mix_post": 1.0 + _normal(ks[3], (L, D), 0.05),
        "norm_ffn_pre": 1.0 + _normal(ks[4], (L, D), 0.05),
        "norm_ffn_post": 1.0 + _normal(ks[5], (L, D), 0.05),
        "norm_mem": 1.0 + _normal(ks[6], (L, D), 0.05),
        "w_in": _normal(ks[7], (L, D, IN_WIDTH), D ** -0.5),
        "rel_bias": _normal(ks[8], (NUM_BUCKETS, N_SELF_HEADS), 0.3),
        "swa_sinks": _normal(ks[9], (L, SWA_Q_HEADS), 1.0),
        "w_mem_kv": _normal(ks[10], (L, D, 2 * MEM_W), D ** -0.5),
        "w_branch_moba": _normal(ks[11], (L, MOBA_W, D), MOBA_W ** -0.5),
        "w_branch_swa": _normal(ks[12], (L, SWA_QW, D), SWA_QW ** -0.5),
        "w_branch_mem": _normal(ks[13], (L, MEM_W, D), MEM_W ** -0.5),
        "w_out": _normal(ks[14], (L, D, D), D ** -0.5),
        "w_ffn_up": _normal(ks[15], (L, D, 2 * F), D ** -0.5),
        "ffn_conv_w": _normal(ks[16], (L, CONV_WIDTH, 2 * F), CONV_WIDTH ** -0.5),
        "ffn_conv_b": _normal(ks[17], (L, 2 * F), 0.02),
        "w_ffn_down": _normal(ks[18], (L, F, D), F ** -0.5),
    }

def second_block(x, mem, norm_mix_pre, norm_mix_post, norm_ffn_pre, norm_ffn_post, norm_mem,
              w_in, rel_bias, swa_sinks, w_mem_kv, w_branch_moba, w_branch_swa, w_branch_mem,
              w_out, w_ffn_up, ffn_conv_w, ffn_conv_b, w_ffn_down):
    B_, S_, _ = x.shape
    cuts = []
    acc = 0
    for width in IN_SPLITS[:-1]:
        acc += width
        cuts.append(acc)
    bias_moba = rel_bias[:, :MOBA_HEADS].T
    bias_swa = rel_bias[:, MOBA_HEADS:].T
    for l in range(DEPTH):
        h = rmsnorm_2(x, norm_mix_pre[l])
        proj = h @ w_in[l]
        (q_mb, k_mb, v_mb, q_sw, k_sw, v_sw, q_me,
         g_mb, g_sw, g_me) = jnp.split(proj, cuts, axis=-1)
        o_mb = moba_attention(
            q_mb.reshape(B_, S_, MOBA_HEADS, MOBA_HEAD_DIM),
            k_mb.reshape(B_, S_, MOBA_HEADS, MOBA_HEAD_DIM),
            v_mb.reshape(B_, S_, MOBA_HEADS, MOBA_HEAD_DIM), bias_moba).reshape(B_, S_, MOBA_W)
        o_sw = swa_attention(
            q_sw.reshape(B_, S_, SWA_Q_HEADS, SWA_HEAD_DIM),
            k_sw.reshape(B_, S_, SWA_KV_HEADS, SWA_HEAD_DIM),
            v_sw.reshape(B_, S_, SWA_KV_HEADS, SWA_HEAD_DIM), swa_sinks[l], bias_swa)
        kv_me = rmsnorm_2(mem, norm_mem[l]) @ w_mem_kv[l]
        M_ = mem.shape[1]
        k_me = kv_me[..., :MEM_W].reshape(B_, M_, MEM_HEADS, MEM_HEAD_DIM)
        v_me = kv_me[..., MEM_W:].reshape(B_, M_, MEM_HEADS, MEM_HEAD_DIM)
        o_me = memory_attention(q_me.reshape(B_, S_, MEM_HEADS, MEM_HEAD_DIM), k_me, v_me)
        merged = (jax.nn.sigmoid(g_mb) * (o_mb @ w_branch_moba[l])
                  + jax.nn.sigmoid(g_sw) * (o_sw @ w_branch_swa[l])
                  + jax.nn.sigmoid(g_me) * (o_me @ w_branch_mem[l]))
        x = x + rmsnorm_2(merged @ w_out[l], norm_mix_post[l])
        h = rmsnorm_2(x, norm_ffn_pre[l])
        u = causal_depthwise_conv(h @ w_ffn_up[l], ffn_conv_w[l], ffn_conv_b[l])
        u_gate, u_val = jnp.split(u, 2, axis=-1)
        y = (jax.nn.gelu(u_gate, approximate=True) * u_val) @ w_ffn_down[l]
        x = x + rmsnorm_2(y, norm_ffn_post[l])
    return x


def setup_inputs(seed=0):
    out = dict(first_inputs(seed))
    for name, value in second_inputs(seed + 1).items():
        if name != "x":
            out[name + "_2"] = value
    return out


def reference(
    x, c, ctx, c_ctx, w_mod, b_mod, norm1_g, w_in, lam_q1, lam_k1, lam_q2, lam_k2, subln_g,
    sink, w_out, norm2_g, w_router, b_router, w_gate_up, b_gate_up, w_down, b_down, final_g,
    mem_2, norm_mix_pre_2, norm_mix_post_2, norm_ffn_pre_2, norm_ffn_post_2, norm_mem_2, w_in_2,
    rel_bias_2, swa_sinks_2, w_mem_kv_2, w_branch_moba_2, w_branch_swa_2, w_branch_mem_2,
    w_out_2, w_ffn_up_2, ffn_conv_w_2, ffn_conv_b_2, w_ffn_down_2,
):
    x = first_block(
        x, c, ctx, c_ctx, w_mod, b_mod, norm1_g, w_in, lam_q1, lam_k1, lam_q2, lam_k2, subln_g,
        sink, w_out, norm2_g, w_router, b_router, w_gate_up, b_gate_up, w_down, b_down, final_g,
    )
    return second_block(
        x, mem_2, norm_mix_pre_2, norm_mix_post_2, norm_ffn_pre_2, norm_ffn_post_2, norm_mem_2,
        w_in_2, rel_bias_2, swa_sinks_2, w_mem_kv_2, w_branch_moba_2, w_branch_swa_2,
        w_branch_mem_2, w_out_2, w_ffn_up_2, ffn_conv_w_2, ffn_conv_b_2, w_ffn_down_2,
    )


_drawn_inputs = setup_inputs


def setup_inputs(seed=0):
    import zlib

    import numpy as np

    out = dict(_drawn_inputs(seed))
    spreads = {}
    factors = {'norm1_g': 2.961,
     'lam_k1': 8.0,
     'lam_q2': 8.0,
     'sink': 64.0,
     'b_router': 3.815,
     'b_gate_up': 8.0,
     'b_down': 22.104,
     'norm_mem_2': 3.091,
     'ffn_conv_b_2': 3.446,
     'subln_g': 3.0,
     'swa_sinks_2': 4.478}
    for name, (base, spread) in spreads.items():
        noise = np.random.default_rng([zlib.crc32(name.encode()), seed]).standard_normal(out[name].shape)
        drawn = base * np.exp(spread * noise) if base else spread * noise
        out[name] = __import__('jax').numpy.asarray(drawn.astype(out[name].dtype))
    for name, factor in factors.items():
        out[name] = (out[name] * factor).astype(out[name].dtype)
    return out
```

```python
from contextlib import ExitStack

import numpy as np
import concourse.bass as bass
from concourse import mybir

F32 = mybir.dt.float32
F32R = mybir.dt.float32r
I32 = mybir.dt.int32
U32 = mybir.dt.uint32
ALU = mybir.AluOpType
ACT = mybir.ActivationFunctionType
AX = mybir.AxisListType

P = 128
D = 1024
KC = D // P
T = 256
TT = T // P
GRID_W = 64
EPS = 1e-6
HD = 64
QK_SCALE = HD ** -0.5
MEM_SCALE = P ** -0.5
MASKED = -1e30
LAM_INIT = 0.2
N_EXPERTS = 32
TOP_K = 4
SLOTS = 64
ROUNDS_MORE = T // SLOTS - 1
D_EXPERT = 1024
FFN = 2816
FC = FFN // P
SWIGLU_LIMIT = 7.0
SWIGLU_ALPHA = 1.702
NUM_BUCKETS = 32

RING = 6
SLOT = 4096
RING2 = RING - 1
PART = 1024
HI_PARTS = SLOT // PART
UNITS_EXPERT = 6

SMALL = [("ident", 128), ("tri", 128), ("cos", T), ("sin", T), ("wmask", 2 * P), ("iota_slot", 128),
         ("iota_expert", 32), ("b_mod", 48), ("norm1_g", 8), ("norm2_g", 8), ("final_g", 8),
         ("mix_pre", 8), ("mix_post", 8), ("ffn_pre", 8), ("ffn_post", 8), ("mem_g", 8), ("subln", 1),
         ("conv_w", 132), ("conv_b", 44), ("cvec", 16), ("w_router", 256), ("lam", 256), ("sink", 8),
         ("swa_sink", 8), ("b_router", 32)]
SMALL_AT = {}
SMALL_N = 0
for _name, _width in SMALL:
    SMALL_AT[_name] = (SMALL_N, _width)
    SMALL_N += _width

AT_X = 0
AT_HX = 2048
AT_YT = 6144
AT_QA, AT_KA, AT_QB, AT_KB, AT_VA, AT_VB = 8192, 9216, 11264, 12288, 13312, 15360
AT_CS, AT_ROW = 15872, 16128
AT_SQ, AT_R, AT_SH, AT_T1 = 16384, 17408, 17920, 18432
AT_E, AT_MEM, AT_PT = 18944, 20992, 23040
AT_BUCKET, AT_BROW = 18944, 23552
AT_HX2, AT_HX2TM = 2048, 8192
AT_XG, AT_SGT, AT_S, AT_SG, AT_SEL = 6144, 7168, 7424, 7680, 7936
AT_KME, AT_VME, AT_BIAS, AT_BGU, AT_BDN = 4096, 5120, 10240, 13312, 15360
AT_G, AT_LIN, AT_SIGM, AT_U, AT_A, AT_AT, AT_Y = 16384, 16896, 17408, 17920, 18432, 18944, 19456
AT_PICK, AT_GT, AT_LAM = 19968, 20224, 23040
AT_SQ2 = 24320
AT_H, AT_QMB, AT_KMB = 2048, 6144, 7168
AT_VMB, AT_VSW, AT_KSW, AT_QSW, AT_QME = 13312, 14336, 14592, 15104, 16128
AT_S2, AT_E2, AT_PT2, AT_HI = 17152, 18176, 19200, 20224
AT_GMB, AT_GSW, AT_GME = 8192, 22272, 4096
AT_MERGED, AT_MIX, AT_SQ3 = 10240, 15360, 17408
AT_FT, AT_UB, AT_GELU, AT_SQ4, AT_FHI = 4096, 9728, 11776, 12288, 13312
ARENA = 25088


def build(nc, io, out):
    ctx = ExitStack()
    with ctx:
        def sb(name, shape, dt=F32):
            return ctx.enter_context(nc.sbuf_tensor(name, shape, dt))

        def sem(name):
            return ctx.enter_context(nc.semaphore(name))

        with nc.sbuf_tensor("ring", [P, RING, SLOT], F32) as ring:
            pass
        ring_r = sb("ring_r", [P, RING, SLOT], F32R)
        with nc.sbuf_tensor("arena", [P, ARENA], F32) as arena:
            pass
        arena_r = sb("arena_r", [P, ARENA], F32R)
        small = sb("small", [P, SMALL_N])
        ones = sb("ones", [P, P])
        modcol = sb("modcol", [P, 48, 2])
        scale1 = sb("scale1", [P, KC, 2])
        scale2 = sb("scale2", [P, KC])
        csig = sb("csig", [P, 16])
        both_g = sb("both_g", [P, KC])
        lamv = sb("lamv", [P, 4])
        subln_s = sb("subln_s", [P, 1])
        mx = sb("mx", [P, 2, 2])
        negm = sb("negm", [P, 2, 2])
        esum = sb("esum", [P, 2, 2])
        esink = sb("esink", [P, 2, 2])
        tot = sb("tot", [P, 2])
        rsum = sb("rsum", [P, 2, 2])
        fneg = sb("fneg", [P, 1])
        oss = sb("oss", [P, 4])
        nrm = sb("nrm", [P, 2, T])
        logits = sb("logits", [P, TT, N_EXPERTS])
        top_v = sb("top_v", [P, TT, 8])
        top_i = sb("top_i", [P, TT, 8], U32)
        top_f = sb("top_f", [P, TT, 8])
        top_e = sb("top_e", [P, TT, TOP_K])
        top_n = sb("top_n", [P, TT])
        top_s = sb("top_s", [P, TT])
        chosen = sb("chosen", [P, TT, N_EXPERTS])
        gates = sb("gates", [P, TT, N_EXPERTS + 2])
        rank = sb("rank", [P, TT, N_EXPERTS + 2])
        most = sb("most", [P, 1])
        unread = sb("unread", [1, 16])
        most_i = sb("most_i", [P, 1], I32)
        ps = ctx.enter_context(nc.psum_tensor("ps", [P, 8, 512], F32))
        bias_rows = nc.dram_tensor("bias_rows", [16, 512], F32)

        def col(name):
            at, width = SMALL_AT[name]
            return small[:, at:at + width]

        def buf(at, *shape, of=arena):
            n = 1
            for s in shape:
                n *= s
            v = of[:, at:at + n]
            if len(shape) == 2:
                return v.rearrange("p (a b) -> p a b", a=shape[0])
            if len(shape) == 3:
                return v.rearrange("p (a b c) -> p a b c", a=shape[0], b=shape[1])
            return v

        def slot(u, a):
            return ring[:, u % RING, :].rearrange("p (a n) -> p a n", a=a)

        ident = col("ident")
        cos, sin = col("cos"), col("sin")
        xT = buf(AT_X, KC, T)
        hx = buf(AT_HX, KC, 2 * T)
        yT = buf(AT_YT, KC, T)
        qa, ka = buf(AT_QA, 4, T), buf(AT_KA, 4, 2 * T)
        qb, kb = buf(AT_QB, 4, T), buf(AT_KB, 2, 2 * T)
        va, vb = buf(AT_VA, 4, 512), buf(AT_VB, 4, P)
        cs, modrow = buf(AT_CS, KC, 32), buf(AT_ROW, 2, P)
        sq, r1 = buf(AT_SQ, 2, 512), buf(AT_R, 512)
        shuf, rope1 = buf(AT_SH, 512), buf(AT_T1, 512)
        e_a = buf(AT_E, 2, 2, 512)
        pT_a = [buf(AT_PT + 1024 * b, 2, 4, P) for b in range(2)]
        o_sq, y_da = buf(AT_SQ, 512), buf(AT_SQ + 512, 512)
        buckets, brow = buf(AT_BUCKET, 1040), buf(AT_BROW, 2, 512)
        lamw = buf(AT_LAM, 2, HD)
        pick = arena[:, AT_PICK:AT_PICK + TT * TOP_K * N_EXPERTS].rearrange("p (a b c) -> p a b c", a=TT, b=TOP_K)
        gates_t = arena[0:N_EXPERTS, AT_GT:AT_GT + T]
        hx2, hx2tm = buf(AT_HX2, KC, T), buf(AT_HX2TM, TT, D)
        xg, sgt, s_hot = buf(AT_XG, KC, 2 * SLOTS), buf(AT_SGT, T), buf(AT_S, TT, 2, SLOTS)
        sg_hot, esel = buf(AT_SG, TT, 2 * SLOTS), buf(AT_SEL, SLOTS)
        memT, bias = buf(AT_MEM, KC, T), buf(AT_BIAS, 8, 384)
        b_gu, b_dn = buf(AT_BGU, 2 * D_EXPERT), buf(AT_BDN, D)
        g_e, lin_e, sig_e, u_e, a_e = (buf(x, 512) for x in (AT_G, AT_LIN, AT_SIGM, AT_U, AT_A))
        aT_e, y_e = buf(AT_AT, 4, P), buf(AT_Y, 512)
        sq_m = buf(AT_PT + 1536, 2, T)
        sq2, sq3, sq4 = buf(AT_SQ2, 2, T), buf(AT_SQ3, 2, T), buf(AT_SQ4, 2, T)
        h, k_me, v_me = buf(AT_H, KC, T), buf(AT_KME, 4, T), buf(AT_VME, TT, 512)
        q_mb, k_mb, v_mb = buf(AT_QMB, 4, T), buf(AT_KMB, 4, T), buf(AT_VMB, TT, 512)
        q_sw, k_sw, v_sw = buf(AT_QSW, 4, T), buf(AT_KSW, 2, T), buf(AT_VSW, TT, P)
        q_me = buf(AT_QME, 4, T)
        s_c, e_c = buf(AT_S2, 2, 2, T), buf(AT_E2, 2, 2, T)
        pT_c = [buf(AT_PT2 + 512 * b, 2, 2, P) for b in range(2)]
        oT = [q_mb, q_sw, q_me]
        gate = [buf(AT_GMB, KC, T), buf(AT_GSW, KC, T), buf(AT_GME, KC, T)]
        sq_mix, fin = buf(AT_S2, 2, 2 * T), buf(AT_E2, 2, T)
        merged, mix = buf(AT_MERGED, KC, T), buf(AT_MIX, KC, T)
        fT = buf(AT_FT, FC, T)
        x_hi, h_lo = buf(AT_HI, KC, T, of=arena_r), buf(AT_H, KC, T, of=arena_r)
        merged_lo = buf(AT_MERGED, KC, T, of=arena_r)
        f_hi, f_lo = buf(AT_FHI, FC, T, of=arena_r), buf(AT_FT, FC, T, of=arena_r)
        u_gate = [buf(AT_UB + 1024 * b, 2, T) for b in range(2)]
        u_val = [buf(AT_UB + 1024 * b + 512, 2, T) for b in range(2)]
        gelu = buf(AT_GELU, 2, T)

        small_in, x_in, ctx_in, bucket_in = sem("small_in"), sem("x_in"), sem("ctx_in"), sem("bucket_in")
        slot_full = [sem(f"slot_full{i}") for i in range(RING)]
        ada_mm, moe_units, more_units = sem("ada_mm"), sem("moe_units"), sem("more_units")
        mem_in, bgu_in, bdn_in = sem("mem_in"), sem("bgu_in"), sem("bdn_in")
        bias_out, bias_in, sw_bias_in = sem("bias_out"), sem("bias_in"), sem("sw_bias_in")
        dve_chain = sem("dve_chain")
        ones_set, cs_zero, csig_set, cs_set, bgu_zero = (sem("ones_set"), sem("cs_zero"), sem("csig_set"),
                                                         sem("cs_set"), sem("bgu_zero"))
        brow_mm, brow_set = sem("brow_mm"), sem("brow_set")
        sq_set, sq_used = sem("sq_set"), sem("sq_used")
        ms_set, root_set = sem("ms_set"), sem("root_set")
        lam_set, lame_set, subln_set = sem("lam_set"), sem("lame_set"), sem("subln_set")
        ada_row, ada_t, ada_col = sem("ada_row"), sem("ada_t"), sem("ada_col")
        hx_x, hx_c, scaled1 = sem("hx_x"), sem("hx_c"), sem("scaled1")
        proj_mm, proj_dve, proj_act = sem("proj_mm"), sem("proj_dve"), sem("proj_act")
        sc_mm, max_set, exp_set, p_set = sem("sc_mm"), sem("max_set"), sem("exp_set"), sem("p_set")
        sinkexp_set = sem("sinkexp_set")
        pt_mm, pt_set, pv_mm, pv_set = sem("pt_mm"), sem("pt_set"), sem("pv_mm"), sem("pv_set")
        ov_set, osq_set, oms_set, oroot_set, yda_set = (sem("ov_set"), sem("osq_set"), sem("oms_set"),
                                                        sem("oroot_set"), sem("yda_set"))
        out_mm, x1_set = sem("out_mm"), sem("x1_set")
        hx2_pre, hx2_set = sem("hx2_pre"), sem("hx2_set")
        log_mm, log_set, top_set, tope_set, route_set = (sem("log_mm"), sem("log_set"), sem("top_set"),
                                                         sem("tope_set"), sem("route_set"))
        tm_mm, tm_set = sem("tm_mm"), sem("tm_set")
        rank_mm, most_set = sem("rank_mm"), sem("most_set")
        gt_mm, gt_set, mem_set = sem("gt_mm"), sem("gt_set"), sem("mem_set")
        x2_pre, h_set = sem("x2_pre"), sem("h_set")
        fin_ms, fin_root = sem("fin_ms"), sem("fin_root")
        w_hi_set, w_lo_set, part_mm, c_act = sem("w_hi_set"), sem("w_lo_set"), sem("part_mm"), sem("c_act")
        h_hi_set, h_lo_set = sem("h_hi_set"), sem("h_lo_set")
        mg_hi_set, mg_lo_set, f_hi_set, f_lo_set = (sem("mg_hi_set"), sem("mg_lo_set"), sem("f_hi_set"),
                                                    sem("f_lo_set"))
        kv_mm, kv_act = sem("kv_mm"), sem("kv_act")
        c_sc, c_max, c_exp, c_sink, c_p = sem("c_sc"), sem("c_max"), sem("c_exp"), sem("c_sink"), sem("c_p")
        c_pt, c_pts, c_pv, c_pvs = sem("c_pt"), sem("c_pts"), sem("c_pv"), sem("c_pvs")
        br_mm, br_used, mg_set = sem("br_mm"), sem("br_used"), sem("mg_set")
        mix_set, x3_set = sem("mix_set"), sem("x3_set")
        tap2_set, conv_set, gelu_set, f_set = (sem("tap2_set"), sem("conv_set"),
                                                      sem("gelu_set"), sem("f_set"))
        y_mm, y_set, o_set, o_out = sem("y_mm"), sem("y_set"), sem("o_set"), sem("o_out")

        class MoeSems:

            def __init__(self, pre):
                self.gather_mm, self.x_ready = sem(pre + "gather_mm"), sem(pre + "x_ready")
                self.s_ready, self.sel_ready = sem(pre + "s_ready"), sem(pre + "sel_ready")
                self.sg_ready, self.h_free = sem(pre + "sg_ready"), sem(pre + "h_free")
                self.g_ready, self.sig_ready = sem(pre + "g_ready"), sem(pre + "sig_ready")
                self.u_ready, self.a_ready = sem(pre + "u_ready"), sem(pre + "a_ready")
                self.at_mm, self.at_ready = sem(pre + "at_mm"), sem(pre + "at_ready")
                self.sgt_mm, self.sgt_ready = sem(pre + "sgt_mm"), sem(pre + "sgt_ready")
                self.y_ready, self.round_done = sem(pre + "y_ready"), sem(pre + "round_done")
                self.shifted = sem(pre + "shifted")

        MAIN, MORE = MoeSems("m_"), MoeSems("f_")
        more_full = [sem(f"more_full{i}") for i in range(RING)]

        MAIN.units, MAIN.units0, MAIN.full, MAIN.full0 = moe_units, 0, slot_full, lambda u: filled(u)
        MORE.units, MORE.units0, MORE.full, MORE.full0 = more_units, 1, more_full, lambda u: 16

        def blocks(w, c0, width):
            return w.rearrange("(k p) n -> p k n", p=P)[:, :, c0:c0 + width]

        def rows(w, k0, nk):
            return w.rearrange("(k p) n -> p k n", p=P)[:, k0:k0 + nk, :]

        w_mod, w_in, w_out = io["w_mod"][0], io["w_in"][0], io["w_out"][0]
        w_in2, w_kv, w_out2 = io["w_in_2"][0], io["w_mem_kv_2"][0], io["w_out_2"][0]
        w_up, w_down2 = io["w_ffn_up_2"][0], io["w_ffn_down_2"][0]
        w_gu, w_dn = io["w_gate_up"][0], io["w_down"][0]
        first = [blocks(w_mod, 512 * u, 512) for u in range(4)]
        U_IN = len(first)
        first += [blocks(w_in, 512 * u, 512) for u in range(4)] + [blocks(w_in, 2048, 256)]
        U_KV = len(first)
        first += [blocks(w_kv, 0, 256), blocks(w_kv, 512, 512)]
        U_MOD2 = len(first)
        first += [blocks(w_mod, 512 * u, 512) for u in range(4, 12)]
        U_OUT = len(first)
        first += [blocks(w_out, 512 * u, 512) for u in range(2)]
        U_KV2 = len(first)
        first += [blocks(w_kv, 256, 256)]
        U_MOE = len(first)
        V_IN = 0
        second = [blocks(w_in2, c0, 512) for c0 in (0, 512, 1024, 2304, 1536)] + [blocks(w_in2, 2048, 256)]
        second += [blocks(w_in2, 2816 + 512 * u, 512) for u in range(6)]
        V_BR = len(second)
        second += [rows(io[n][0], 0, 4) for n in ("w_branch_moba_2", "w_branch_swa_2", "w_branch_mem_2")]
        V_OUT = len(second)
        second += [blocks(w_out2, 512 * u, 512) for u in range(2)]
        V_UP = len(second)
        second += [blocks(w_up, 512 * u, 512) for u in range(FC // 2)]
        V_DN = len(second)
        second += [rows(w_down2, 4 * u, min(4, FC - 4 * u)) for u in range((FC + 3) // 4)]

        def unit_dst(index, src):
            n = 1
            for s in src.shape[1:]:
                n *= s
            return ring[:, index, 0:n].rearrange("p (k n) -> p k n", k=src.shape[1])

        def filled(u):
            return 16 * (u // RING + 1)

        def filled_c(c):
            before = len(range(c % RING2, U_MOE + UNITS_EXPERT * N_EXPERTS, RING))
            return 16 * (before + c // RING2 + 1)

        JOBS = ([("qa", 0), ("qa", 1)] + [("ka", i) for i in range(4)] + [("va", i) for i in range(4)]
                + [("qb", 0), ("qb", 1), ("kb", 0), ("kb", 1), ("vb", 0)])
        ROPED = [i for i, (n, _) in enumerate(JOBS) if n[0] in "qk"]
        COPIED = [i for i, (n, _) in enumerate(JOBS) if n[0] in "kv"]
        EARLY = 10

        def upto(jobs, n):
            return sum(j <= n for j in jobs)

        N_DA, N_AT = 8, 16

        def step_a(a):
            return (a // 4, a % 4) if a < N_DA else ((a - N_DA) % 2, (a - N_DA) // 2)

        def p_upto(a):
            return a + 1 if a < N_DA else N_DA + 2 * (a - N_DA + 1)

        TURNS = []
        for a in range(N_AT + 2):
            if 1 <= a <= N_AT:
                TURNS.append(("p", a - 1, 0))
                if a - 1 >= N_DA:
                    TURNS.append(("p", a - 1, 1))
            if a in (7, 11):
                TURNS.append(("y", a // 8, 0))

        def turn(kind, a, c=0):
            return TURNS.index((kind, a, c))

        ADA_STEP = 5

        KV_STEP = len(JOBS) - EARLY
        ADA_STEP = KV_STEP + 3

        KV_JOBS = (("k", 0, U_KV, 0), ("v", 0, U_KV + 1, 1), ("v", 1, U_KV + 1, 0), ("k", 1, U_KV2, 6))

        def kv_at(a):
            return a - KV_STEP if KV_STEP <= a < ADA_STEP else None

        def ada_at(a):
            return 4 + a - ADA_STEP if ADA_STEP <= a < ADA_STEP + 8 else None

        C_JOBS = ([("qmb", 0), ("qmb", 1), ("kmb", 0), ("kmb", 1), ("vmb", 0), ("vmb", 1), ("qme", 0), ("qme", 1),
                   ("qsw", 0), ("qsw", 1), ("kvsw", 0)] + [("gate", i) for i in range(12)])
        C_EARLY, N_C = 6, 24

        def c_filler(a):
            return C_EARLY + a if a < 13 else (C_EARLY + a - 5 if 18 <= a < 22 else None)

        C_UNIT = {"qmb": 0, "kmb": 1, "vmb": 2, "qme": 3, "qsw": 4, "kvsw": 5}
        PARTS = []
        for name, i in C_JOBS:
            u = V_IN + (C_UNIT[name] if name != "gate" else 6 + i // 2)
            PARTS += [(u, 2 * P if name == "kvsw" else 512, 2 * (i % 2) + c) for c in range(2)]
        J_OUT = len(PARTS) // 2
        PARTS += [(V_OUT + m // 4, 512, m % 4) for m in range(KC)]
        J_UP = len(PARTS) // 2
        PARTS += [(V_UP + n, 512, m) for n in range(FC // 2) for m in range(4)]
        J_DN = len(PARTS) // 2
        PARTS += [(V_DN + f // 4, None, f % 4) for f in range(FC)]
        N_JOBS = len(PARTS) // 2

        def part_of(n, of):
            c, width, i = PARTS[n]
            v = of[:, c % RING2, :]
            if width is None:
                return v[:, PART * i:PART * i + PART].rearrange("p (k n) -> p k n", k=KC)
            return v[:, 0:KC * width].rearrange("p (k n) -> p k n", k=KC)[:, :, P * i:P * i + P]

        def part_hi(n):
            at = PART * (n % HI_PARTS)
            return ring_r[:, RING2, at:at + PART].rearrange("p (k n) -> p k n", k=KC)

        def done(j):
            return 2 * j + 2

        def step_c(a):
            kind, j, qt = (0, 2, 1)[a // 8], a % 8 // 2, a % 2
            return kind, j, qt, (T if kind == 2 else P * (qt + 1)), (1 if kind == 2 else 2)

        NORM1, NORM_MEM, NORM2, NORM_MIX, NORM_POST, NORM_FFN, NORM_LAST = range(7)

        def chain(engine, done):
            count = [0]

            def link(ins):
                count[0] += 1
                ins.then_inc(done, 1)
                engine.wait_ge(done, count[0])
            return link

        block = ctx.enter_context(nc.Block())

        freed = [(ada_mm, n + 1) for n in range(4)]
        freed += [(proj_mm, 2), (proj_mm, 6), (proj_mm, 10), (proj_mm, 12), (proj_mm, 15)]
        freed += [(kv_mm, 1), (kv_mm, 3)]
        freed += [(ada_mm, n + 1) for n in range(4, 12)] + [(out_mm, 2), (out_mm, 4), (kv_mm, 4)]
        freed_c = [(br_mm, 4 * (c - V_BR) + 4) if V_BR <= c < V_OUT
                   else (part_mm, 1 + max(n for n, part in enumerate(PARTS) if part[0] == c))
                   for c in range(len(second))]

        @block.sync
        def _(sp):
            def load(u, dst, src):
                if u >= RING:
                    sp.wait_ge(*freed[u - RING])
                sp.dma_start(dst, src).then_inc(slot_full[u % RING], 16)

            gu_rows = w_gu.rearrange("e (k p) n -> e p k n", p=P)
            dn_rows = w_dn.rearrange("e (k p) n -> e p k n", p=P)

            def expert_unit(e, q):
                if q < 4:
                    return slot(U_MOE + q, 2), gu_rows[e, :, 2 * q:2 * q + 2, :]
                return slot(U_MOE + q, 4), dn_rows[e, :, 4 * (q - 4):4 * (q - 4) + 4, :]

            sp.dma_start(xT, io["xT"]).then_inc(x_in, 16)
            sp.dma_start(hx[:, :, T:2 * T], io["ctxT"]).then_inc(ctx_in, 16)
            sp.dma_start(memT, io["memT"]).then_inc(mem_in, 16)
            for u, src in enumerate(first):
                load(u, unit_dst(u % RING, src), src)
            for q in range(UNITS_EXPERT):
                load(U_MOE + q, *expert_unit(0, q))
            with sp.Fori(1, N_EXPERTS) as e:
                for q in range(UNITS_EXPERT):
                    sp.wait_ge(moe_units, e * UNITS_EXPERT + (q + 1 - RING))
                    sp.dma_start(*expert_unit(e, q)).then_inc(slot_full[(U_MOE + q) % RING], 16)
            sp.wait_ge(most_set, 1)
            count = sp.value_load(most_i[0:1, 0:1], min_val=0, max_val=T)
            with sp.If(count > SLOTS):
                sp.wait_ge(moe_units, UNITS_EXPERT * N_EXPERTS)
                with sp.Fori(0, ROUNDS_MORE) as r:
                    with sp.Fori(0, N_EXPERTS) as e:
                        sp.wait_ge(more_units, r * (UNITS_EXPERT * N_EXPERTS) + e * UNITS_EXPERT + 1)
                        for q in range(UNITS_EXPERT):
                            sp.dma_start(*expert_unit(e, q)).then_inc(more_full[(U_MOE + q) % RING], 16)
                sp.wait_ge(more_units, ROUNDS_MORE * UNITS_EXPERT * N_EXPERTS + 1)
            for c, src in enumerate(second):
                at = c % RING2
                if c < RING2:
                    sp.wait_ge(moe_units, UNITS_EXPERT * (N_EXPERTS - 1) + (at - U_MOE) % RING + 1)
                else:
                    sp.wait_ge(*freed_c[c - RING2])
                sp.dma_start(unit_dst(at, src), src).then_inc(slot_full[at], 16)
            for k in range(KC):
                sp.wait_ge(o_set, k + 1)
                sp.dma_start(out[:, k, :], xT[:, k, :]).then_inc(o_out, 16)
            sp.wait_ge(o_out, 16 * KC)

        def bias_loads(engine, group, landed):
            for qt in range(TT):
                keys, at = P * (qt + 1), P * qt
                for quad in range(4):
                    q_last = P * qt + 32 * quad + 31
                    src = bass.AP(bias_rows, 512 * 8 * group + T - 1 - q_last, [[1, 32], [512, 8], [1, keys]])
                    engine.dma_start(bias[32 * quad:32 * quad + 32, :, at:at + keys], src).then_inc(landed, 16)

        BIAS_LOADS = 4 * TT

        @block.gpsimd
        def _(pool):
            nc.gpsimd.memset(ones[:], 1.0).then_inc(ones_set, 1)
            nc.gpsimd.memset(cs, 0.0).then_inc(cs_zero, 1)
            pool.wait_ge(pv_mm, N_AT)
            nc.gpsimd.memset(b_gu, 0.0).then_inc(bgu_zero, 1)
            pool.wait_ge(c_max, 8)
            bias_loads(pool, 1, sw_bias_in)

        @block.tensor
        def _(pe):
            def mm(out_, lhsT, rhs, start, stop, **kw):
                return nc.tensor.matmul(out_, lhsT, rhs, start=start, stop=stop, **kw)

            pe.wait_ge(bucket_in, 16)
            for g in range(2):
                mm(ps[0:8, 6 + g, :], buckets[0:33, 1024 + 8 * g:1032 + 8 * g],
                   buckets[0:33, 512 * g:512 * g + 512], True, True).then_inc(brow_mm, 1)

            def sum_squares(norm, src, bank, width, k0=0, k1=KC):
                for k in range(k0, k1):
                    pe.wait_ge(sq_set, KC * norm + k + 1)
                    mm(ps[:, bank, 0:width], ones[:], src[:, k % 2, :], k == 0, k == KC - 1).then_inc(sq_used, 1)

            pe.wait_ge(ones_set, 1)
            pe.wait_ge(brow_set, 2)
            sum_squares(NORM1, sq, 7, 2 * T)

            def ada_rows(n, bank):
                u = n if n < 4 else U_MOD2 + n - 4
                w = slot(u, KC)
                pe.wait_ge(slot_full[u % RING], filled(u))
                if n:
                    pe.wait_ge(ada_row, n)
                for k in range(KC):
                    for j in range(4):
                        last = mm(ps[32 * j:32 * j + 32, bank, 0:P], cs[:, k, :], w[:, k, P * j:P * j + P],
                                  k == 0, k == KC - 1)
                last.then_inc(ada_mm, 1)

            def ada_turn(n, bank):
                pe.wait_ge(ada_row, n + 1)
                if n:
                    pe.wait_ge(ada_col, n)
                nc.tensor.transpose(ps[:, bank, 0:P], modrow[:, n % 2, :], ident).then_inc(ada_t, 1)

            pe.wait_ge(cs_set, 1)
            for n in range(4):
                ada_rows(n, 5)
                ada_turn(n, 6)
                if n == 0:
                    pe.wait_ge(ms_set, NORM1 + 1)
                    sum_squares(NORM_MEM, sq_m, 7, T)

            def project(n):
                name, i = JOBS[n]
                if n >= 2:
                    pe.wait_ge(proj_dve, upto(ROPED, n - 2))
                    if upto(COPIED, n - 2):
                        pe.wait_ge(proj_act, upto(COPIED, n - 2))
                bank = n % 2
                u = U_IN + {"qa": 0, "ka": 1, "va": 2, "qb": 3, "kb": 4, "vb": 4}[name]
                pe.wait_ge(slot_full[u % RING], filled(u))
                w = ring[:, u % RING, 0:2048].rearrange("p (k n) -> p k n", k=KC) if u == U_IN + 4 else slot(u, KC)

                def normed(k):
                    if n == 0:
                        pe.wait_ge(hx_x, k + 1)
                    if n == 2:
                        pe.wait_ge(hx_c, k + 1)
                if name in ("qa", "qb"):
                    for c in range(2):
                        m = 2 * i + c
                        for k in range(KC):
                            if c == 0:
                                normed(k)
                            last = mm(ps[:, bank, T * c:T * c + T], w[:, k, P * m:P * m + P], hx[:, k, 0:T],
                                      k == 0, k == KC - 1)
                elif name == "ka":
                    for k in range(KC):
                        normed(k)
                        last = mm(ps[:, bank, :], w[:, k, P * i:P * i + P], hx[:, k, :], k == 0, k == KC - 1)
                elif name == "kb":
                    for k in range(KC):
                        for half in range(2):
                            last = mm(ps[HD * half:HD * half + HD, bank, :], w[:, k, HD * i:HD * i + HD], hx[:, k, :],
                                      k == 0, k == KC - 1)
                elif name == "va":
                    for k in range(KC):
                        last = mm(ps[:, bank, :], hx[:, k, P * i:P * i + P], w[:, k, :], k == 0, k == KC - 1)
                else:
                    for t in range(4):
                        for k in range(KC):
                            last = mm(ps[:, bank, P * t:P * t + P], hx[:, k, P * t:P * t + P], w[:, k, P:2 * P],
                                      k == 0, k == KC - 1)
                last.then_inc(proj_mm, 1)

            for n in range(EARLY):
                project(n)

            def scores(a):
                qt, j = step_a(a)
                b = a % 2
                if a == 0:
                    pe.wait_ge(proj_dve, upto(ROPED, EARLY - 1))
                    pe.wait_ge(proj_act, upto(COPIED, EARLY - 1))
                    pe.wait_ge(ada_col, 4)
                    pe.wait_ge(ms_set, NORM_MEM + 1)
                if a == N_DA:
                    pe.wait_ge(proj_dve, len(ROPED))
                    pe.wait_ge(proj_act, len(COPIED))
                if a >= 2:
                    pe.wait_ge(exp_set, 2 * (a - 1))
                for c in range(2):
                    half = slice(HD * c, HD * c + HD)
                    q = (qa if a < N_DA else qb)[half, j, P * qt:P * qt + P]
                    k = ka[half, j, :] if a < N_DA else kb[half, j // 2, :]
                    last = mm(ps[:, 4 + 2 * b + c, :], q, k, True, True)
                last.then_inc(sc_mm, 1)

            def turn_bank(kind, a, c=0):
                n = turn(kind, a, c)
                if n:
                    pe.wait_ge(pt_set, n)
                src = y_da if kind == "y" else e_a[:, a % 2, c]
                if kind == "y":
                    pe.wait_ge(yda_set, a + 1)
                else:
                    pe.wait_ge(p_set, p_upto(a) if a < N_DA else p_upto(a - 1) + c + 1)
                for kt in range(4):
                    last = nc.tensor.transpose(ps[:, 2, P * kt:P * kt + P], src[:, P * kt:P * kt + P], ident)
                last.then_inc(pt_mm, 1)

            def values(a):
                qt, j = step_a(a)
                pe.wait_ge(pt_set, turn("p", a, int(a >= N_DA)) + 1)
                if a < N_DA:
                    if a == 4:
                        pe.wait_ge(ov_set, 1)
                    for kt in range(4):
                        last = mm(ps[:, 3, P * j:P * j + P], pT_a[a % 2][:, 0, kt, :], va[:, kt, P * j:P * j + P],
                                  kt == 0, kt == 3)
                else:
                    if a == N_DA:
                        pe.wait_ge(ov_set, 2)
                    else:
                        pe.wait_ge(pv_set, a - N_DA)
                    kv = j // 2
                    for kt in range(4):
                        for c in range(2):
                            last = mm(ps[HD * c:HD * c + HD, 3, 0:P], vb[:, kt, HD * kv:HD * kv + HD],
                                      pT_a[a % 2][:, c, kt, :], kt == 0, kt == 3)
                last.then_inc(pv_mm, 1)

            def memory_job(n):
                kind, i, u, bank = KV_JOBS[n]
                w = slot(u, KC) if kind == "v" else ring[:, u % RING, 0:2048].rearrange("p (k n) -> p k n", k=KC)
                if n == 0:
                    pe.wait_ge(mem_set, KC)
                    pe.wait_ge(proj_dve, len(ROPED))
                    pe.wait_ge(proj_act, len(COPIED))
                if n == 2:
                    pe.wait_ge(kv_act, 1)
                pe.wait_ge(slot_full[u % RING], filled(u))
                if kind == "k":
                    for c in range(2):
                        for k in range(KC):
                            last = mm(ps[:, bank, T * c:T * c + T], w[:, k, P * c:P * c + P], memT[:, k, :],
                                      k == 0, k == KC - 1)
                else:
                    for k in range(KC):
                        last = mm(ps[:, bank, :], memT[:, k, P * i:P * i + P], w[:, k, :], k == 0, k == KC - 1)
                last.then_inc(kv_mm, 1)

            for a in range(N_AT + 2):
                if a < N_AT:
                    scores(a)
                if EARLY + a < len(JOBS):
                    project(EARLY + a)
                if kv_at(a) is not None:
                    memory_job(kv_at(a))
                if 1 <= a <= N_AT:
                    turn_bank("p", a - 1)
                if ada_at(a) is not None:
                    if a == ADA_STEP:
                        pe.wait_ge(kv_act, 3)
                    ada_rows(ada_at(a), 1)
                if a >= 2:
                    values(a - 2)
                if ada_at(a) is not None:
                    ada_turn(ada_at(a), 0)
                if N_DA < a <= N_AT:
                    turn_bank("p", a - 1, 1)
                if a in (7, 11):
                    turn_bank("y", a // 8)

            pe.wait_ge(ada_col, 12)
            pe.wait_ge(pt_set, len(TURNS))
            pe.wait_ge(pv_set, N_AT - N_DA)
            for n in range(4):
                u = U_OUT + n // 2
                w = slot(u, KC)
                pe.wait_ge(slot_full[u % RING], filled(u))
                if n >= 2:
                    pe.wait_ge(x1_set, 2 * (n - 1))
                for c in range(2):
                    m = 2 * (n % 2) + c
                    for k in range(KC):
                        last = mm(ps[:, n % 2, T * c:T * c + T], w[:, k, P * m:P * m + P], yT[:, k, :],
                                  k == 0, k == KC - 1)
                last.then_inc(out_mm, 1)
            sum_squares(NORM2, sq2, 2, T)
            memory_job(3)
            for t in range(TT):
                for k in range(KC):
                    if t == 0:
                        pe.wait_ge(hx2_set, k + 1)
                    last = mm(ps[:, 3, 32 * t:32 * t + 32], hx2[:, k, P * t:P * t + P],
                              col("w_router")[:, 32 * k:32 * k + 32], k == 0, k == KC - 1)
                last.then_inc(log_mm, 1)
            pe.wait_ge(x1_set, KC)
            for n in range(4):
                t, half = n // 2, n % 2
                if n >= 2:
                    pe.wait_ge(tm_set, n - 1)
                for c in range(4):
                    last = nc.tensor.transpose(ps[:, n % 2, P * c:P * c + P], hx2[:, 4 * half + c, P * t:P * t + P],
                                               ident)
                last.then_inc(tm_mm, 1)
            pe.wait_ge(route_set, 1)
            for t in range(TT):
                mm(ps[:, 4, 32 * t:32 * t + 32], col("tri"), chosen[:, t, :], True, t == 0)
                if t:
                    mm(ps[:, 4, 32 * t:32 * t + 32], ones[:], chosen[:, 0, :], False, True)
            for t in range(TT):
                last = mm(ps[:, 4, 64:96], ones[:], chosen[:, t, :], t == 0, t == TT - 1)
            last.then_inc(rank_mm, 1)
            for t in range(TT):
                last = nc.tensor.transpose(ps[0:32, 5, P * t:P * t + P], gates[:, t, 0:N_EXPERTS], ident)
            last.then_inc(gt_mm, 1)
            pe.wait_ge(ms_set, NORM2 + 1)
            pe.wait_ge(tm_set, 4)
            pe.wait_ge(log_set, 1)
            pe.wait_ge(bgu_in, 16)

            def start_sums():
                pe.wait_ge(gt_set, 1)
                pe.wait_ge(bdn_in, 16)
                pe.wait_ge(most_set, 1)
                pe.wait_ge(kv_act, 4)
                for m in range(KC):
                    mm(ps[:, 4 + m // 2, T * (m % 2):T * (m % 2) + T], b_dn[0:N_EXPERTS, P * m:P * m + P], gates_t[:],
                       m % 2 == 0, False, skip_group_check=True)

            def round_pe(S, r, first):
                def gather(half):
                    for c in range(4):
                        for t in range(TT):
                            last = mm(ps[:, 2, P * c:P * c + P], hx2tm[:, t, P * (4 * half + c):P * (4 * half + c) + P],
                                      s_hot[:, t].rearrange("p a b -> p (a b)"), t == 0, t == TT - 1)
                    last.then_inc(S.gather_mm, 1)

                def combine():
                    for c in range(4):
                        for half in range(2):
                            m = 4 * half + c
                            rows_ = slice(SLOTS * half, SLOTS * half + SLOTS)
                            last = mm(ps[:, 4 + m // 2, T * (m % 2):T * (m % 2) + T], y_e[rows_, P * c:P * c + P],
                                      sgt[rows_, :], False, False, skip_group_check=True)
                    return last

                pe.wait_ge(S.s_ready, r * 17 + 1)
                gather(0)
                if first is not None:
                    first()
                pe.wait_ge(S.x_ready, r * 34 + 1)
                gather(1)
                with pe.Fori(0, N_EXPERTS // 2) as i:
                    for j in range(2):
                        e = i * 2 + j
                        pe.wait_ge(S.h_free, r * 33 + (e + 1))
                        pe.wait_ge(S.sel_ready, r * 33 + (e + 1))
                        if j == 0:
                            pe.wait_ge(S.x_ready, r * 34 + (i * 2 + 2))
                        for n in range(2):
                            for half in range(2):
                                at = 1024 * half + 512 * n
                                mm(ps[SLOTS * half:SLOTS * half + SLOTS, n, :], esel, b_gu[:, at:at + 512], True, False)
                        for q in range(4):
                            u = U_MOE + q
                            w = slot(u, 2)
                            pe.wait_ge(S.full[u % RING], (r * N_EXPERTS + e) * 16 + S.full0(u))
                            for kk in range(2):
                                k = 2 * q + kk
                                for n in range(2):
                                    for half in range(2):
                                        at = 1024 * half + 512 * n
                                        last = mm(ps[SLOTS * half:SLOTS * half + SLOTS, n, :],
                                                  xg[:, k, SLOTS * j:SLOTS * j + SLOTS], w[:, kk, at:at + 512],
                                                  False, k == KC - 1)
                            last.then_inc(S.units, 1)
                        pe.wait_ge(S.y_ready, r * 33 + (e + 1))
                        pe.wait_ge(S.sgt_ready, r * 33 + (e + 1))
                        combine()
                        pe.wait_ge(S.sg_ready, r * 33 + (e + 1))
                        for t in range(TT):
                            last = nc.tensor.transpose(ps[:, 3, P * t:P * t + P], sg_hot[:, t, :], ident)
                        last.then_inc(S.sgt_mm, 1)
                        if j == 1:
                            pe.wait_ge(S.s_ready, r * 17 + (i + 2))
                            pe.wait_ge(S.at_ready, r * 32 + e)
                            gather(0)
                            pe.wait_ge(S.x_ready, r * 34 + (i * 2 + 3))
                            gather(1)
                            pe.wait_ge(S.x_ready, r * 34 + (i * 2 + 4))
                        pe.wait_ge(S.a_ready, r * 32 + (e + 1))
                        for b in range(4):
                            last = nc.tensor.transpose(ps[:, 2, P * b:P * b + P], a_e[:, P * b:P * b + P], ident)
                        last.then_inc(S.at_mm, 1)
                        pe.wait_ge(S.at_ready, r * 32 + (e + 1))
                        pe.wait_ge(S.sgt_ready, r * 33 + (e + 2))
                        for q in range(4, UNITS_EXPERT):
                            u = U_MOE + q
                            w = slot(u, 4)
                            pe.wait_ge(S.full[u % RING], (r * N_EXPERTS + e) * 16 + S.full0(u))
                            for kk in range(4):
                                f = 4 * (q - 4) + kk
                                for half in range(2):
                                    last = mm(ps[SLOTS * half:SLOTS * half + SLOTS, 3, :],
                                              aT_e[:, f % 4, SLOTS * (f // 4):SLOTS * (f // 4) + SLOTS],
                                              w[:, kk, 512 * half:512 * half + 512], f == 0, f == KC - 1)
                            last.then_inc(S.units, 1)
                pe.wait_ge(S.y_ready, r * 33 + 33)
                pe.wait_ge(S.sgt_ready, r * 33 + 33)
                combine().then_inc(S.round_done, 1)

            def if_more(engine):
                engine.wait_ge(most_set, 1)
                return engine.If(engine.value_load(most_i[0:1, 0:1], min_val=0, max_val=T) > SLOTS)

            round_pe(MAIN, 0, start_sums)
            with if_more(pe):
                pe.sem_inc(more_units, 1)
                with pe.Fori(0, ROUNDS_MORE) as r:
                    round_pe(MORE, r, None)

            def split_product(o, hi, lo, x_hi_, x_lo_, first, last):
                mm(o, hi, x_hi_, first, False, skip_group_check=True)
                mm(o, hi, x_lo_, False, False, skip_group_check=True)
                return mm(o, lo, x_hi_, False, last, skip_group_check=True)

            def columns(n, o, hi, lo):
                w_hi, w_lo = part_hi(n), part_of(n, ring_r)
                pe.wait_ge(w_lo_set, n + 1)
                for k in range(KC):
                    if n == 0:
                        pe.wait_ge(h_lo_set, k + 1)
                    if n == 2 * J_UP:
                        pe.wait_ge(h_lo_set, KC + k + 1)
                    last = split_product(o, w_hi[:, k, :], w_lo[:, k, :], hi[:, k, :], lo[:, k, :], k == 0, k == KC - 1)
                last.then_inc(part_mm, 1)

            def rows_of(n, o, hi, lo):
                w_hi, w_lo = part_hi(n), part_of(n, ring_r)
                pe.wait_ge(w_lo_set, n + 1)
                for t in range(TT):
                    tok = slice(P * t, P * t + P)
                    for k in range(KC):
                        last = split_product(o[:, t], hi[:, k, tok], lo[:, k, tok], w_hi[:, k, :], w_lo[:, k, :], k == 0,
                                             k == KC - 1)
                last.then_inc(part_mm, 1)

            def project_c(j):
                name, i = C_JOBS[j]
                if j >= 2:
                    pe.wait_ge(c_act, j - 1)
                if name == "vmb":
                    pe.wait_ge(w_lo_set, 2 * j + 2)
                    at = PART * (2 * j % HI_PARTS)
                    w_hi = ring_r[:, RING2, at:at + 2 * PART].rearrange("p (c k n) -> p k c n", c=2, k=KC)
                    w_lo = ring_r[:, PARTS[2 * j][0] % RING2, :].rearrange("p (k n) -> p k n", k=KC)[:, :, T * i:T * i + T]
                    for t in range(TT):
                        tok = slice(P * t, P * t + P)
                        for k in range(KC):
                            last = split_product(ps[:, j % 2, T * t:T * t + T], x_hi[:, k, tok], h_lo[:, k, tok], w_hi[:, k],
                                                 w_lo[:, k], k == 0, k == KC - 1)
                    last.then_inc(part_mm, 2)
                    return
                for c in range(2):
                    n = 2 * j + c
                    if name == "kvsw" and c:
                        rows_of(n, ps[:, j % 2, T:2 * T].rearrange("p (t n) -> p t n", t=TT), x_hi, h_lo)
                    else:
                        columns(n, ps[:, j % 2, T * c:T * c + T], x_hi, h_lo)

            sum_squares(NORM_MIX, sq_mix, 2, 2 * T)
            for n in range(C_EARLY):
                project_c(n)

            def scores_c(a):
                kind, j, qt, keys, heads = step_c(a)
                b = a % 2
                if a % 8 == 0:
                    pe.wait_ge(c_act, (C_EARLY, C_EARLY + 2, C_EARLY + 5)[a // 8])
                if a >= 2:
                    pe.wait_ge(c_exp, sum(step_c(s)[4] for s in range(a - 1)))
                queries = slice(P * qt, P * qt + P)
                for c in range(heads):
                    half = slice(HD * c, HD * c + HD)
                    if kind == 0:
                        q, k = q_mb[half, j, queries], k_mb[half, j, 0:keys]
                    elif kind == 1:
                        q, k = q_sw[half, j, queries], k_sw[half, j // 2, 0:keys]
                    else:
                        q, k = q_me[:, j, queries], k_me[:, j, :]
                    last = mm(ps[:, 4 + 2 * b + c, 0:keys], q, k, True, True)
                last.then_inc(c_sc, 1)

            def turn_c(a):
                kind, j, qt, keys, heads = step_c(a)
                if a >= 1:
                    pe.wait_ge(c_pts, a)
                pe.wait_ge(c_p, a + 1)
                nk = keys // P
                for c in range(heads):
                    for kt in range(nk):
                        at = P * (nk * c + kt)
                        last = nc.tensor.transpose(ps[:, 2, at:at + P], e_c[:, a % 2, c, P * kt:P * kt + P], ident)
                last.then_inc(c_pt, 1)

            def values_c(a):
                kind, j, qt, keys, heads = step_c(a)
                nk = keys // P
                pe.wait_ge(c_pts, a + 1)
                if a >= 1:
                    pe.wait_ge(c_pvs, a)
                for kt in range(nk):
                    for c in range(heads):
                        if kind == 2:
                            o, v = ps[:, 3, 0:P], v_me[:, kt, P * j:P * j + P]
                        else:
                            o = ps[HD * c:HD * c + HD, 3, 0:P]
                            v = (v_mb[:, kt, HD * (2 * j + c):HD * (2 * j + c) + HD] if kind == 0
                                 else v_sw[:, kt, HD * (j // 2):HD * (j // 2) + HD])
                        last = mm(o, v, pT_c[a % 2][:, c, kt, :], kt == 0, kt == nk - 1)
                last.then_inc(c_pv, 1)

            pe.wait_ge(ms_set, NORM_MIX + 1)
            for a in range(N_C + 2):
                if a < N_C:
                    scores_c(a)
                if c_filler(a) is not None:
                    project_c(c_filler(a))
                if 1 <= a <= N_C:
                    turn_c(a - 1)
                if a >= 2:
                    values_c(a - 2)

            pe.wait_ge(c_pvs, N_C)
            pe.wait_ge(c_act, len(C_JOBS))
            for n in range(12):
                b, i = n // 4, n % 4
                w = ring[:, (V_BR + b) % RING2, :].rearrange("p (k n) -> p k n", k=4)
                pe.wait_ge(slot_full[(V_BR + b) % RING2], filled_c(V_BR + b))
                if n >= 2:
                    pe.wait_ge(br_used, n - 1)
                for c in range(2):
                    m = 2 * i + c
                    for k in range(4):
                        last = mm(ps[:, n % 2, T * c:T * c + T], w[:, k, P * m:P * m + P], oT[b][:, k, :],
                                  k == 0, k == 3)
                last.then_inc(br_mm, 1)
            for n in range(4):
                if n == 0:
                    pe.wait_ge(br_used, 12)
                    pe.wait_ge(mg_lo_set, 4)
                if n >= 2:
                    pe.wait_ge(mix_set, n - 1)
                for c in range(2):
                    columns(2 * (J_OUT + n) + c, ps[:, n % 2, T * c:T * c + T], x_hi, merged_lo)
                if n:
                    sum_squares(NORM_POST, sq3, 2, T, 2 * n - 2, 2 * n)
            sum_squares(NORM_POST, sq3, 2, T, KC - 2, KC)
            pe.wait_ge(ms_set, NORM_POST + 1)
            sum_squares(NORM_FFN, sq3, 2, T)
            pe.wait_ge(ms_set, NORM_FFN + 1)
            for n in range(FC // 2):
                if n >= 2:
                    pe.wait_ge(conv_set, 2 * (n - 1))
                for two in range(2):
                    for c in range(2):
                        columns(2 * (J_UP + 2 * n + two) + c, ps[:, 2 * (n % 2) + two, T * c:T * c + T], x_hi, h_lo)

            def down(f, m):
                n = 2 * J_DN + f
                return split_product(ps[:, 4 + m // 2, T * (m % 2):T * (m % 2) + T], part_hi(n)[:, m, :],
                                     part_of(n, ring_r)[:, m, :], f_hi[:, f, :], f_lo[:, f, :], f == 0 and m % 2 == 0,
                                     f == FC - 1)

            for f in range(FC - 2):
                pe.wait_ge(w_lo_set, 2 * J_DN + f + 1)
                pe.wait_ge(f_lo_set, f // 2 + 1)
                for m in range(KC):
                    last = down(f, m)
                last.then_inc(part_mm, 1)
            pe.wait_ge(w_lo_set, 2 * N_JOBS)
            pe.wait_ge(f_lo_set, FC // 2)
            pe.wait_ge(conv_set, FC)
            for m in range(KC):
                for f in (FC - 2, FC - 1):
                    last = down(f, m)
                if m % 2:
                    last.then_inc(y_mm, 1)
                if m > 1 and m % 2:
                    sum_squares(NORM_LAST, sq4, 0, T, m - 3, m - 1)
            sum_squares(NORM_LAST, sq4, 0, T, KC - 2, KC)

        @block.scalar
        def _(act):
            A = nc.scalar.activation

            tables = [0]

            def load_table(func):
                at = tables[0]
                tables[0] += 1
                A(unread[:, at:at + 1], small[0:1, 0:1], func)

            act.dma_start(small[:], io["small"]).then_inc(small_in, 16)
            act.dma_start(buckets[0:33], io["buckets"]).then_inc(bucket_in, 16)
            for g in range(2):
                act.wait_ge(brow_mm, g + 1)
                A(brow[0:8, g], ps[0:8, 6 + g, :], ACT.Copy).then_inc(brow_set, 1)
            act.wait_ge(brow_set, 2)
            act.dma_start(bias_rows.ap().rearrange("(g h) n -> h g n", g=2), brow[0:8]).then_inc(bias_out, 16)
            act.wait_ge(small_in, 16)
            A(csig[:], col("cvec"), ACT.Sigmoid).then_inc(csig_set, 1)
            act.wait_ge(lam_set, 1)
            A(lamv[:, 2:4], lamv[:, 0:2], ACT.Exp).then_inc(lame_set, 1)
            load_table(ACT.Sqrt)

            def square(norm, k, dst, src, scale=1.0):
                if k >= 2:
                    act.wait_ge(sq_used, KC * norm + k - 1)
                A(dst, src, ACT.Square, scale=scale).then_inc(sq_set, 1)

            def root(norm):
                act.wait_ge(ms_set, norm + 1)
                A(nrm[:, 1], nrm[:, 0], ACT.Sqrt).then_inc(root_set, 1)

            act.wait_ge(x_in, 16)
            act.wait_ge(ctx_in, 16)
            for k in range(KC):
                if k >= 2:
                    act.wait_ge(sq_used, k - 1)
                A(sq[:, k % 2, 0:T], xT[:, k], ACT.Square)
                A(sq[:, k % 2, T:2 * T], hx[:, k, T:2 * T], ACT.Square).then_inc(sq_set, 1)
            act.wait_ge(ms_set, 1)
            A(rope1, shuf, ACT.Sqrt).then_inc(root_set, 1)

            def ada_copy(n, bank):
                act.wait_ge(ada_mm, n + 1)
                if n >= 2:
                    act.wait_ge(ada_t, n - 1)
                A(modrow[:, n % 2], ps[:, bank, 0:P], ACT.Copy).then_inc(ada_row, 1)

            for n in range(4):
                ada_copy(n, 5)
                if n == 0:
                    act.wait_ge(mem_in, 16)
                    for k in range(KC):
                        square(NORM_MEM, k, sq_m[:, k % 2], memT[:, k])
                    root(NORM_MEM)
                    load_table(ACT.Exp)
            act.wait_ge(scaled1, 1)
            for k in range(KC):
                A(hx[:, k, T:2 * T], hx[:, k, T:2 * T], ACT.Identity, bias=modcol[:, k, 1:2],
                  scale=scale1[:, k, 1:2]).then_inc(hx_c, 1)

            def copy_job(n):
                name, i = JOBS[n]
                if n not in COPIED:
                    return
                act.wait_ge(proj_mm, n + 1)
                if name in ("ka", "kb"):
                    dst = ka if name == "ka" else kb
                    act.wait_ge(proj_dve, upto(ROPED, n))
                    A(dst[:, i, T:2 * T], ps[:, n % 2, T:2 * T], ACT.Copy).then_inc(proj_act, 1)
                elif name == "va":
                    A(va[:, i], ps[:, n % 2, :], ACT.Copy).then_inc(proj_act, 1)
                else:
                    A(vb, ps[:, n % 2, :].rearrange("p (a b) -> p a b", a=4), ACT.Copy).then_inc(proj_act, 1)

            for n in range(EARLY):
                copy_job(n)
            act.wait_ge(subln_set, 1)
            act.wait_ge(bias_out, 16)

            def copy_turn(kind, s, c=0):
                act.wait_ge(pt_mm, turn(kind, s, c) + 1)
                src = ps[:, 2, :].rearrange("p (a b) -> p a b", a=4)
                if kind == "y":
                    A(yT[:, 0:4, P * s:P * s + P], src, ACT.Copy, scale=subln_s[:, 0:1]).then_inc(pt_set, 1)
                else:
                    if s >= 2:
                        act.wait_ge(pv_mm, s - 1)
                    A(pT_a[s % 2][:, c], src, ACT.Copy).then_inc(pt_set, 1)

            def copy_memory(n):
                act.wait_ge(kv_mm, n + 1)
                kind, i, _, bank = KV_JOBS[n]
                if kind == "k":
                    A(k_me[:, 2 * i:2 * i + 2], ps[:, bank, :].rearrange("p (a b) -> p a b", a=2),
                      ACT.Copy).then_inc(kv_act, 1)
                else:
                    A(v_me[:, i], ps[:, bank, :], ACT.Copy).then_inc(kv_act, 1)

            for a in range(N_AT + 2):
                if ADA_STEP <= a <= N_AT:
                    copy_turn("p", a - 1)
                if ada_at(a) is not None:
                    ada_copy(ada_at(a), 1)
                if a < N_AT:
                    b, j = a % 2, step_a(a)[1]
                    act.wait_ge(max_set, a + 1)
                    if a >= 2:
                        act.wait_ge(pt_mm, turn("p", a - 2, int(a - 2 >= N_DA)) + 1)
                    for c in range(2):
                        A(e_a[:, b, c], ps[:, 4 + 2 * b + c, :], ACT.Exp, bias=negm[:, b, c:c + 1], scale=QK_SCALE,
                          accum_out=esum[:, b, c:c + 1]).then_inc(exp_set, 1)
                    if a >= N_DA:
                        for c in range(2):
                            A(esink[:, b, c:c + 1], col("sink")[:, 2 * j + c:2 * j + c + 1], ACT.Exp,
                              bias=negm[:, b, c:c + 1]).then_inc(sinkexp_set, 1)
                if a in (6, 10):
                    act.wait_ge(oms_set, a // 6 if a == 6 else 2)
                    A(oss[:], oss[:], ACT.Sqrt).then_inc(oroot_set, 1)
                if EARLY + a < len(JOBS):
                    copy_job(EARLY + a)
                if kv_at(a) is not None:
                    copy_memory(kv_at(a))
                if 1 <= a < ADA_STEP:
                    copy_turn("p", a - 1)
                if a - 2 in (3, 7):
                    act.wait_ge(pv_mm, a - 1)
                    if a - 2 == 7:
                        act.wait_ge(pt_mm, turn("y", 0) + 1)
                    A(y_da, ps[:, 3, :], ACT.Copy).then_inc(ov_set, 1)
                    act.wait_ge(ov_set, (a - 2) // 4 + 1)
                    A(o_sq, y_da, ACT.Square).then_inc(osq_set, 1)
                if N_DA < a <= N_AT:
                    copy_turn("p", a - 1, 1)
                if a - 2 >= N_DA:
                    qt, j = step_a(a - 2)
                    act.wait_ge(pv_mm, a - 1)
                    A(yT[:, 4 + j, P * qt:P * qt + P], ps[:, 3, 0:P], ACT.Copy).then_inc(pv_set, 1)
                if a in (7, 11):
                    copy_turn("y", a // 8)

            load_table(ACT.Sqrt)
            act.wait_ge(pv_mm, N_AT)
            act.dma_start(b_dn[0:N_EXPERTS], io["b_down"][0]).then_inc(bdn_in, 16)
            act.wait_ge(bias_out, 16)
            bias_loads(act, 0, bias_in)
            for k in range(KC):
                act.wait_ge(x1_set, k + 1)
                square(NORM2, k, sq2[:, k % 2], xT[:, k])
            root(NORM2)
            load_table(ACT.Exp)
            for k in range(KC):
                act.wait_ge(hx2_pre, k + 1)
                A(hx2[:, k], hx2[:, k], ACT.Identity, bias=modcol[:, 24 + k, 0:1]).then_inc(hx2_set, 1)
            copy_memory(3)
            act.wait_ge(bgu_zero, 1)
            act.dma_start(b_gu[0:N_EXPERTS], io["b_gate_up"][0]).then_inc(bgu_in, 16)
            for n in range(4):
                act.wait_ge(tm_mm, n + 1)
                A(hx2tm[:, n // 2, 512 * (n % 2):512 * (n % 2) + 512], ps[:, n % 2, :], ACT.Copy).then_inc(tm_set, 1)
            act.wait_ge(top_set, 1)
            for t in range(TT):
                A(top_e[:, t], top_v[:, t, 0:TOP_K], ACT.Exp, bias=top_n[:, t:t + 1],
                  accum_out=top_s[:, t:t + 1]).then_inc(tope_set, 1)
            act.wait_ge(gt_mm, 1)
            A(gates_t[:], ps[0:N_EXPERTS, 5, 0:T], ACT.Copy).then_inc(gt_set, 1)
            load_table(ACT.Sigmoid)

            def round_act(S, r):
                A(y_e, small[:, SMALL_AT["cos"][0]:SMALL_AT["cos"][0] + 512], ACT.Copy, scale=0.0).then_inc(S.y_ready, 1)
                A(sgt, cos, ACT.Copy, scale=0.0).then_inc(S.sgt_ready, 1)

                def copy_gather(half, n):
                    act.wait_ge(S.gather_mm, n)
                    A(xg[:, 4 * half:4 * half + 4, :], ps[:, 2, :].rearrange("p (a b) -> p a b", a=4),
                      ACT.Copy).then_inc(S.x_ready, 1)

                for half in range(2):
                    copy_gather(half, r * 34 + (half + 1))
                with act.Fori(0, N_EXPERTS // 2) as i:
                    for j in range(2):
                        e = i * 2 + j
                        act.wait_ge(S.g_ready, r * 32 + (e + 1))
                        A(sig_e, g_e, ACT.Sigmoid, scale=SWIGLU_ALPHA).then_inc(S.sig_ready, 1)
                        act.wait_ge(S.sgt_mm, r * 32 + (e + 1))
                        A(sgt, ps[:, 3, 0:T], ACT.Copy).then_inc(S.sgt_ready, 1)
                        if j == 1:
                            for half in range(2):
                                copy_gather(half, r * 34 + (i * 2 + (half + 3)))
                        act.wait_ge(S.at_mm, r * 32 + (e + 1))
                        A(aT_e, ps[:, 2, :].rearrange("p (a b) -> p a b", a=4), ACT.Copy).then_inc(S.at_ready, 1)
                        act.wait_ge(S.units, (r * N_EXPERTS + e) * UNITS_EXPERT + (UNITS_EXPERT + S.units0))
                        A(y_e, ps[:, 3, :], ACT.Copy).then_inc(S.y_ready, 1)
                act.wait_ge(S.round_done, r + 1)

            round_act(MAIN, 0)
            act.wait_ge(most_set, 1)
            with act.If(act.value_load(most_i[0:1, 0:1], min_val=0, max_val=T) > SLOTS):
                with act.Fori(0, ROUNDS_MORE) as r:
                    round_act(MORE, r)

            load_table(ACT.Sqrt)

            def split_hi_part(n):
                act.wait_ge(slot_full[PARTS[n][0] % RING2], filled_c(PARTS[n][0]))
                if n >= HI_PARTS:
                    act.wait_ge(part_mm, n - HI_PARTS + 1)
                A(part_hi(n), part_of(n, ring), ACT.Copy).then_inc(w_hi_set, 1)

            def split_hi(j):
                split_hi_part(2 * j)
                split_hi_part(2 * j + 1)

            def copy_c(n):
                name, i = C_JOBS[n]
                act.wait_ge(part_mm, done(n))
                src = ps[:, n % 2, :]
                pair = src.rearrange("p (a b) -> p a b", a=2)
                if name == "gate":
                    A(gate[i // 4][:, 2 * (i % 4):2 * (i % 4) + 2], pair, ACT.Tanh, scale=0.5).then_inc(c_act, 1)
                    return
                if name == "kvsw":
                    for kv in range(2):
                        for half in range(2):
                            A(k_sw[HD * half:HD * half + HD, kv], ps[HD * kv:HD * kv + HD, n % 2, 0:T], ACT.Copy)
                    dst, src = v_sw, ps[:, n % 2, T:2 * T].rearrange("p (a b) -> p a b", a=2)
                elif name == "vmb":
                    dst, src = v_mb[:, :, T * i:T * i + T], pair
                else:
                    to = {"qmb": q_mb, "kmb": k_mb, "qsw": q_sw, "qme": q_me}[name]
                    dst, src = to[:, 2 * i:2 * i + 2], pair
                A(dst, src, ACT.Copy).then_inc(c_act, 1)

            for k in range(KC):
                act.wait_ge(x2_pre, k + 1)
                if k >= 2:
                    act.wait_ge(sq_used, KC * NORM_MIX + k - 1)
                A(sq_mix[:, k % 2, 0:T], xT[:, k], ACT.Square)
                A(sq_mix[:, k % 2, T:2 * T], xT[:, k], ACT.Square, scale=col("final_g")[:, k:k + 1]).then_inc(sq_set, 1)
            split_hi_part(0)
            root(NORM_MIX)
            act.wait_ge(fin_ms, 1)
            A(fin[:, 0], fin[:, 0], ACT.Sqrt).then_inc(fin_root, 1)
            load_table(ACT.Exp)
            for k in range(KC):
                act.wait_ge(h_set, k + 1)
                A(x_hi[:, k], h[:, k], ACT.Copy).then_inc(h_hi_set, 1)
            split_hi_part(1)
            split_hi(1)
            for n in range(C_EARLY):
                copy_c(n)
                if n + 2 <= C_EARLY:
                    split_hi(n + 2)

            def copy_turn_c(s):
                kind, j, qt, keys, heads = step_c(s)
                nk = keys // P
                act.wait_ge(c_pt, s + 1)
                if s >= 2:
                    act.wait_ge(c_pv, s - 1)
                A(pT_c[s % 2][:, 0:heads, 0:nk, :], ps[:, 2, 0:P * heads * nk].rearrange("p (a b c) -> p a b c", a=heads, b=nk),
                  ACT.Copy).then_inc(c_pts, 1)

            for a in range(N_C + 2):
                if c_filler(a) is None and 1 <= a <= N_C:
                    copy_turn_c(a - 1)
                if a < N_C:
                    kind, j, qt, keys, heads = step_c(a)
                    b = a % 2
                    act.wait_ge(c_max, a + 1)
                    if a >= 2:
                        act.wait_ge(c_pt, a - 1)
                    for c in range(heads):
                        src = s_c[:, b, c, 0:keys] if kind < 2 else ps[:, 4 + 2 * b, 0:keys]
                        A(e_c[:, b, c, 0:keys], src, ACT.Exp, bias=negm[:, b, c:c + 1],
                          scale=MEM_SCALE if kind == 2 else 1.0, accum_out=esum[:, b, c:c + 1]).then_inc(c_exp, 1)
                    if kind == 1:
                        for c in range(heads):
                            A(esink[:, b, c:c + 1], col("swa_sink")[:, 2 * j + c:2 * j + c + 1], ACT.Exp,
                              bias=negm[:, b, c:c + 1]).then_inc(c_sink, 1)
                if c_filler(a) is not None:
                    split_hi(c_filler(a) + 1)
                    copy_c(c_filler(a))
                    if a >= 1:
                        copy_turn_c(a - 1)
                if a >= 2:
                    kind, j, qt, keys, heads = step_c(a - 2)
                    act.wait_ge(c_pv, a - 1)
                    A(oT[kind][:, j, P * qt:P * qt + P], ps[:, 3, 0:P], ACT.Copy).then_inc(c_pvs, 1)

            load_table(ACT.Sqrt)
            split_hi(J_OUT + 1)
            for i in range(4):
                act.wait_ge(mg_set, 4 + i + 1)
                A(x_hi[:, 2 * i:2 * i + 2], merged[:, 2 * i:2 * i + 2], ACT.Copy).then_inc(mg_hi_set, 1)
            for n in range(4):
                act.wait_ge(part_mm, done(J_OUT + n))
                for c in range(2):
                    square(NORM_POST, 2 * n + c, sq3[:, c], ps[:, n % 2, T * c:T * c + T], scale=0.5)
                A(mix[:, 2 * n:2 * n + 2], ps[:, n % 2, :].rearrange("p (a b) -> p a b", a=2),
                  ACT.Copy, scale=0.5).then_inc(mix_set, 1)
                if n < 3:
                    split_hi(J_OUT + n + 2)
            root(NORM_POST)
            split_hi(J_UP + 1)
            for k in range(KC):
                act.wait_ge(x3_set, k + 1)
                square(NORM_FFN, k, sq3[:, k % 2], xT[:, k])
            root(NORM_FFN)
            load_table(ACT.Gelu_apprx_tanh)
            for k in range(KC):
                act.wait_ge(h_set, KC + k + 1)
                A(x_hi[:, k], h[:, k], ACT.Copy).then_inc(h_hi_set, 1)

            def hidden_hi(n):
                act.wait_ge(f_set, n + 1)
                A(f_hi[:, 2 * n:2 * n + 2], fT[:, 2 * n:2 * n + 2], ACT.Copy).then_inc(f_hi_set, 1)

            for n in range(FC // 2):
                if n >= 2:
                    act.wait_ge(f_set, n - 1)
                for two in range(2):
                    act.wait_ge(part_mm, done(J_UP + 2 * n + two))
                    for c in range(2):
                        ch = FC * two + 2 * n + c
                        A((u_gate, u_val)[two][n % 2][:, c], ps[:, 2 * (n % 2) + two, T * c:T * c + T], ACT.Identity,
                          bias=col("conv_b")[:, ch:ch + 1],
                          scale=col("conv_w")[:, 88 + ch:89 + ch]).then_inc(tap2_set, 1)
                    split_hi(J_UP + 2 * n + two + 2)
                act.wait_ge(conv_set, 2 * n + 1)
                if n >= 1:
                    act.wait_ge(f_set, n)
                A(gelu, u_gate[n % 2], ACT.Gelu_apprx_tanh).then_inc(gelu_set, 1)
                if n >= 1:
                    hidden_hi(n - 1)
            hidden_hi(FC // 2 - 1)
            for j in range(J_DN + 2, N_JOBS):
                split_hi(j)
            load_table(ACT.Sqrt)
            for m in range(KC):
                if m % 2 == 0:
                    act.wait_ge(y_mm, m // 2 + 1)
                square(NORM_LAST, m, sq4[:, m % 2], ps[:, 4 + m // 2, T * (m % 2):T * (m % 2) + T])
            root(NORM_LAST)

        @block.vector
        def _(dve):
            V = nc.vector
            link = chain(dve, dve_chain)

            dve.wait_ge(small_in, 16)
            lam4 = col("lam").rearrange("p (a b d) -> p a b d", a=2, b=2)
            link(V.tensor_tensor(lamw[:], lam4[:, :, 0], lam4[:, :, 1], ALU.mult))
            V.tensor_reduce(lamv[:, 0:2], lamw[:], AX.X, ALU.add).then_inc(lam_set, 1)
            dve.wait_ge(csig_set, 1)
            dve.wait_ge(cs_zero, 1)
            cvec = col("cvec").rearrange("p (k v) -> p k v", v=2)
            V.tensor_tensor(cs[:, :, 0:2], cvec, csig[:].rearrange("p (k v) -> p k v", v=2),
                            ALU.mult).then_inc(cs_set, 1)
            V.tensor_scalar(subln_s[:], col("subln"), 1.0 - LAM_INIT, None, ALU.mult).then_inc(subln_set, 1)
            dve.wait_ge(lame_set, 1)
            link(V.tensor_tensor(lamv[:, 0:1], lamv[:, 3:4], lamv[:, 2:3], ALU.subtract))
            link(V.tensor_scalar(lamv[:, 1:2], lamv[:, 0:1], -LAM_INIT, None, ALU.add))
            neg_lam = lamv[:, 1:2]

            dve.wait_ge(sq_used, KC)
            V.tensor_scalar(shuf, ps[:, 7, :], 1.0 / D, EPS, ALU.mult, ALU.add).then_inc(ms_set, 1)
            dve.wait_ge(root_set, 1)
            link(V.reciprocal(r1, rope1))
            for k in range(KC):
                V.tensor_tensor(hx[:, k, 0:T], xT[:, k], r1[:, 0:T], ALU.mult)
                last = V.tensor_tensor(hx[:, k, T:2 * T], hx[:, k, T:2 * T], r1[:, T:2 * T], ALU.mult)
            link(last)

            rinv = nrm[:, 0]

            def inverse_rms(norm, bank):
                dve.wait_ge(sq_used, KC * (norm + 1))
                V.tensor_scalar(nrm[:, 0], ps[:, bank, 0:T], 1.0 / D, EPS, ALU.mult, ALU.add).then_inc(ms_set, 1)
                dve.wait_ge(root_set, norm + 1)
                link(V.reciprocal(rinv, nrm[:, 1]))

            def times(dst, src, g):
                return V.scalar_tensor_tensor(dst, src, g, rinv, ALU.mult, ALU.mult)

            def ada_columns(n, bank):
                dve.wait_ge(ada_t, n + 1)
                src = ps[:, bank, 0:P].rearrange("p (j v) -> p j v", j=4)[:, :, 0:2]
                b_mod = col("b_mod")[:, 4 * n:4 * n + 4].unsqueeze(2).to_broadcast([P, 4, 2])
                V.tensor_tensor(modcol[:, 4 * n:4 * n + 4, :], src, b_mod, ALU.add).then_inc(ada_col, 1)

            for n in range(4):
                ada_columns(n, 6)
                if n == 0:
                    inverse_rms(NORM_MEM, 7)
                    for k in range(KC):
                        times(memT[:, k], memT[:, k], col("mem_g")[:, k:k + 1]).then_inc(mem_set, 1)
            dve.wait_ge(ada_col, 4)
            V.scalar_tensor_tensor(scale1[:], modcol[:, 8:16, :], 1.0,
                                   col("norm1_g").unsqueeze(2).to_broadcast([P, KC, 2]), ALU.add,
                                   ALU.mult).then_inc(scaled1, 1)
            dve.wait_ge(scaled1, 1)
            for k in range(KC):
                V.tensor_scalar(hx[:, k, 0:T], hx[:, k, 0:T], scale1[:, k, 0:1], modcol[:, k, 0:1], ALU.mult,
                                ALU.add).then_inc(hx_x, 1)

            swap16 = [(i + 16) % 32 for i in range(32)]

            def rope(n):
                if n not in ROPED:
                    return
                name, i = JOBS[n]
                dve.wait_ge(proj_mm, n + 1)
                if name in ("qa", "qb"):
                    w, dst = 2 * T, (qa if name == "qa" else qb)[:, 2 * i:2 * i + 2]
                else:
                    w, dst = T, (ka if name == "ka" else kb)[:, i:i + 1, 0:T]
                nt = w // T

                def wide(x):
                    return x.rearrange("p (a b) -> p a b", a=nt)

                if n:
                    dve.wait_ge(proj_dve, upto(ROPED, n - 1))
                V.tensor_tensor(wide(rope1[:, 0:w]), wide(ps[:, n % 2, 0:w]),
                                cos.unsqueeze(1).to_broadcast([P, nt, T]), ALU.mult)
                link(V.stream_shuffle(shuf[:, 0:w], ps[:, n % 2, 0:w], swap16))
                link(V.tensor_tensor(wide(shuf[:, 0:w]), wide(shuf[:, 0:w]),
                                     sin.unsqueeze(1).to_broadcast([P, nt, T]), ALU.mult))
                V.tensor_tensor(dst, wide(rope1[:, 0:w]), wide(shuf[:, 0:w]), ALU.add).then_inc(proj_dve, 1)

            for n in range(EARLY):
                rope(n)

            def maxima(a):
                qt, j = step_a(a)
                b = a % 2
                banks = ps[:, 4 + 2 * b:6 + 2 * b, :]
                dve.wait_ge(sc_mm, a + 1)
                if a >= N_DA:
                    far = banks[:, :, P:2 * P] if qt == 0 else banks[:, :, 0:P]
                    link(V.tensor_tensor(far, far, col("wmask")[:, P * qt:P * qt + P].unsqueeze(1).to_broadcast([P, 2, P]),
                                         ALU.add))
                link(V.tensor_reduce(mx[:, b], banks, AX.X, ALU.max))
                if a < N_DA:
                    V.tensor_scalar(negm[:, b], mx[:, b], -QK_SCALE, None, ALU.mult).then_inc(max_set, 1)
                else:
                    link(V.scalar_tensor_tensor(mx[:, b], mx[:, b], QK_SCALE, col("sink")[:, 2 * j:2 * j + 2], ALU.mult,
                                                ALU.max))
                    V.tensor_scalar(negm[:, b], mx[:, b], -1.0, None, ALU.mult).then_inc(max_set, 1)

            def normalise(s):
                b = s % 2
                dve.wait_ge(exp_set, 2 * (s + 1))
                if s < N_DA:
                    link(V.reciprocal(rsum[:, b], esum[:, b]))
                    link(V.tensor_tensor(fneg[:], rsum[:, b, 1:2], neg_lam, ALU.mult))
                    link(V.tensor_scalar(e_a[:, b, 1], e_a[:, b, 1], fneg[:, 0:1], None, ALU.mult))
                    V.scalar_tensor_tensor(e_a[:, b, 0], e_a[:, b, 0], rsum[:, b, 0:1], e_a[:, b, 1], ALU.mult,
                                           ALU.add).then_inc(p_set, 1)
                else:
                    dve.wait_ge(sinkexp_set, 2 * (s - N_DA + 1))
                    link(V.tensor_tensor(tot[:], esum[:, b], esink[:, b], ALU.add))
                    link(V.reciprocal(rsum[:, b], tot[:]))
                    for c in range(2):
                        V.tensor_scalar(e_a[:, b, c], e_a[:, b, c], rsum[:, b, c:c + 1], None,
                                        ALU.mult).then_inc(p_set, 1)

            for a in range(N_AT + 1):
                if a >= 1:
                    normalise(a - 1)
                if a < N_AT:
                    maxima(a)
                if EARLY + a < len(JOBS):
                    rope(EARLY + a)
                if ada_at(a) is not None:
                    ada_columns(ada_at(a), 0)
                heads = lambda x: x.rearrange("p (a b) -> p a b", a=4)
                if a in (5, 9):
                    dve.wait_ge(osq_set, a // 4)
                    link(V.tensor_reduce(oss[:], heads(o_sq), AX.X, ALU.add))
                    V.tensor_scalar(oss[:], oss[:], 1.0 / P, EPS, ALU.mult, ALU.add).then_inc(oms_set, 1)
                if a in (6, 10):
                    dve.wait_ge(oroot_set, a // 5)
                    link(V.reciprocal(oss[:], oss[:]))
                    V.tensor_tensor(heads(y_da), heads(y_da), oss[:].unsqueeze(2).to_broadcast([P, 4, P]),
                                    ALU.mult).then_inc(yda_set, 1)

            dve.wait_ge(ada_col, 12)
            V.tensor_tensor(both_g[:], col("final_g"), col("mix_pre"), ALU.mult)
            link(V.scalar_tensor_tensor(scale2[:], modcol[:, 32:40, 0], 1.0, col("norm2_g"), ALU.add, ALU.mult))
            for m in range(KC):
                dve.wait_ge(out_mm, m // 2 + 1)
                V.scalar_tensor_tensor(xT[:, m], ps[:, m // 2 % 2, T * (m % 2):T * (m % 2) + T], modcol[:, 16 + m, 0:1],
                                       xT[:, m], ALU.mult, ALU.add).then_inc(x1_set, 1)
            inverse_rms(NORM2, 2)
            for k in range(KC):
                times(hx2[:, k], xT[:, k], scale2[:, k:k + 1]).then_inc(hx2_pre, 1)

            dve.wait_ge(log_mm, TT)
            V.tensor_tensor(logits[:], ps[:, 3, 0:64].rearrange("p (a b) -> p a b", a=TT),
                            col("b_router").unsqueeze(1).to_broadcast([P, TT, N_EXPERTS]), ALU.add).then_inc(log_set, 1)
            dve.wait_ge(log_set, 1)
            for t in range(TT):
                last = V.max(top_v[:, t], logits[:, t])
            link(last)
            V.tensor_scalar(top_n[:], top_v[:, :, 0], -1.0, None, ALU.mult).then_inc(top_set, 1)
            for t in range(TT):
                last = V.max_index(top_i[:, t], top_v[:, t], logits[:, t])
            link(last)
            link(V.tensor_copy(top_f[:], top_i[:]))
            for t in range(TT):
                last = V.tensor_tensor(pick[:, t], col("iota_expert").unsqueeze(1).to_broadcast([P, TOP_K, N_EXPERTS]),
                                       top_f[:, t, 0:TOP_K].unsqueeze(2).to_broadcast([P, TOP_K, N_EXPERTS]),
                                       ALU.is_equal)
            link(last)
            for t in range(TT):
                last = V.tensor_reduce(chosen[:, t], pick[:, t].rearrange("p k e -> p e k"), AX.X, ALU.add)
            dve.wait_ge(tope_set, TT)
            link(V.reciprocal(top_s[:], top_s[:]))
            link(V.tensor_tensor(top_e[:], top_e[:], top_s[:].unsqueeze(2).to_broadcast([P, TT, TOP_K]), ALU.mult))
            for t in range(TT):
                last = V.tensor_tensor(pick[:, t], pick[:, t],
                                       top_e[:, t].unsqueeze(2).to_broadcast([P, TOP_K, N_EXPERTS]), ALU.mult)
            link(last)
            V.memset(gates[:, :, N_EXPERTS:N_EXPERTS + 2], 0.0)
            V.memset(rank[:, :, N_EXPERTS:N_EXPERTS + 2], -1.0)
            for t in range(TT):
                last = V.tensor_reduce(gates[:, t, 0:N_EXPERTS], pick[:, t].rearrange("p k e -> p e k"), AX.X, ALU.add)
            last.then_inc(route_set, 1)
            dve.wait_ge(rank_mm, 1)
            link(V.tensor_reduce(most[:], ps[:, 4, 64:96], AX.X, ALU.max))
            link(V.scalar_tensor_tensor(rank[:, :, 0:N_EXPERTS], ps[:, 4, 0:64].rearrange("p (a b) -> p a b", a=TT), 1.0,
                                        chosen[:], ALU.add, ALU.mult))
            link(V.tensor_scalar(rank[:, :, 0:N_EXPERTS], rank[:, :, 0:N_EXPERTS], -1.0, None, ALU.add))
            V.tensor_copy(most_i[:], most[:]).then_inc(most_set, 1)

            reverse32 = [31 - i for i in range(32)]

            def round_dve(S, r, first):
                def one_hots(e0):
                    for t in range(TT):
                        for jj in range(2):
                            last = V.tensor_scalar(s_hot[:, t, jj], col("iota_slot")[:, 0:SLOTS],
                                                   rank[:, t, bass.ds(e0 + jj, 1)], None, ALU.is_equal)
                    last.then_inc(S.s_ready, 1)

                def selector(e):
                    V.tensor_copy(esel, ident[:, bass.ds(e, 1)].to_broadcast([P, SLOTS])).then_inc(S.sel_ready, 1)

                def gated(e, also=None):
                    for t in range(TT):
                        last = V.tensor_scalar(sg_hot[:, t], col("iota_slot"), rank[:, t, bass.ds(e, 1)],
                                               gates[:, t, bass.ds(e, 1)], ALU.is_equal, ALU.mult)
                        if t == 0 and also is not None:
                            last.then_inc(also, 1)
                    last.then_inc(S.sg_ready, 1)

                if S is MORE:
                    V.tensor_scalar(rank[:], rank[:], -float(SLOTS), None, ALU.add).then_inc(S.shifted, 1)
                    dve.wait_ge(S.shifted, r + 1)
                one_hots(0)
                selector(0)
                gated(0, S.h_free)
                if first is not None:
                    first()
                with dve.Fori(0, N_EXPERTS // 2) as i:
                    for j in range(2):
                        e = i * 2 + j
                        if j == 0:
                            dve.wait_ge(S.gather_mm, r * 34 + (i * 2 + 2))
                            one_hots(i * 2 + 2)
                        dve.wait_ge(S.units, (r * N_EXPERTS + e) * UNITS_EXPERT + (4 + S.units0))
                        hidden = ps[:, 0:2, :].rearrange("p n (f two) -> p n f two", two=2)
                        two_banks = lambda x: x.rearrange("p (n f) -> p n f", n=2)
                        V.tensor_scalar(two_banks(g_e), hidden[:, :, :, 0], SWIGLU_LIMIT, None,
                                        ALU.min).then_inc(S.g_ready, 1)
                        V.tensor_scalar(two_banks(lin_e), hidden[:, :, :, 1], -SWIGLU_LIMIT, SWIGLU_LIMIT, ALU.max,
                                        ALU.min).then_inc(S.h_free, 1)
                        selector(e + 1)
                        dve.wait_ge(S.h_free, r * 33 + (e + 2))
                        V.scalar_tensor_tensor(u_e, lin_e, 1.0, g_e, ALU.add, ALU.mult).then_inc(S.u_ready, 1)
                        dve.wait_ge(S.sig_ready, r * 32 + (e + 1))
                        dve.wait_ge(S.u_ready, r * 32 + (e + 1))
                        V.tensor_tensor(a_e, u_e, sig_e, ALU.mult).then_inc(S.a_ready, 1)
                        dve.wait_ge(S.sgt_mm, r * 32 + (e + 1))
                        gated(e + 1)
                dve.wait_ge(S.gather_mm, r * 34 + 34)
                dve.wait_ge(S.sg_ready, r * 33 + 33)
                dve.wait_ge(S.round_done, r + 1)

            def before_experts():
                dve.wait_ge(bias_in, 16 * BIAS_LOADS)
                flat = arena[:, AT_BIAS:AT_BIAS + 8 * 384]
                link(V.stream_shuffle(flat, flat, reverse32))

            round_dve(MAIN, 0, before_experts)
            dve.wait_ge(most_set, 1)
            with dve.If(dve.value_load(most_i[0:1, 0:1], min_val=0, max_val=T) > SLOTS):
                with dve.Fori(0, ROUNDS_MORE) as r:
                    round_dve(MORE, r, None)

            for m in range(KC):
                V.scalar_tensor_tensor(xT[:, m], ps[:, 4 + m // 2, T * (m % 2):T * (m % 2) + T], modcol[:, 40 + m, 0:1],
                                       xT[:, m], ALU.mult, ALU.add).then_inc(x2_pre, 1)
            dve.wait_ge(sq_used, KC * (NORM_MIX + 1))
            V.tensor_scalar(fin[:, 0], ps[:, 2, 0:T], 1.0 / D, EPS, ALU.mult, ALU.add).then_inc(fin_ms, 1)
            link(V.tensor_scalar(fin[:, 1], ps[:, 2, 0:T], EPS / D, EPS * EPS, ALU.mult, ALU.add))
            V.scalar_tensor_tensor(nrm[:, 0], ps[:, 2, T:2 * T], 1.0 / D, fin[:, 1], ALU.mult, ALU.add).then_inc(ms_set, 1)
            dve.wait_ge(root_set, NORM_MIX + 1)
            link(V.reciprocal(rinv, nrm[:, 1]))

            def split_lo_part(n):
                dve.wait_ge(w_hi_set, n + 1)
                V.tensor_tensor(part_of(n, ring_r), part_of(n, ring), part_hi(n).bitcast(F32),
                                ALU.subtract).then_inc(w_lo_set, 1)

            def split_lo(j):
                split_lo_part(2 * j)
                split_lo_part(2 * j + 1)

            def normed_parts(g, before):
                for k in range(KC + 2):
                    if k < KC:
                        times(h[:, k], xT[:, k], g[:, k:k + 1]).then_inc(h_set, 1)
                    if k >= 2:
                        dve.wait_ge(h_hi_set, before + k - 1)
                        V.tensor_tensor(h_lo[:, k - 2], h[:, k - 2], x_hi[:, k - 2].bitcast(F32),
                                        ALU.subtract).then_inc(h_lo_set, 1)

            split_lo_part(0)
            normed_parts(both_g, 0)
            split_lo_part(1)
            split_lo(1)
            dve.wait_ge(fin_root, 1)
            link(V.reciprocal(fin[:, 0], fin[:, 0]))
            for k in range(KC):
                V.scalar_tensor_tensor(xT[:, k], xT[:, k], col("final_g")[:, k:k + 1], fin[:, 0], ALU.mult, ALU.mult)
            for n in range(C_EARLY):
                if n + 2 <= C_EARLY:
                    split_lo(n + 2)

            def maxima_c(a):
                kind, j, qt, keys, heads = step_c(a)
                b = a % 2
                banks = ps[:, 4 + 2 * b:4 + 2 * b + heads, 0:keys]
                if a == 16:
                    dve.wait_ge(sw_bias_in, 16 * BIAS_LOADS)
                    flat = arena[:, AT_BIAS:AT_BIAS + 8 * 384]
                    link(V.stream_shuffle(flat, flat, reverse32))
                dve.wait_ge(c_sc, a + 1)
                src = banks
                if kind < 2:
                    src = s_c[:, b, :, 0:keys]
                    link(V.scalar_tensor_tensor(src, banks, QK_SCALE, bias[:, 2 * j:2 * j + 2, P * qt:P * qt + keys],
                                                ALU.mult, ALU.add))
                link(V.tensor_reduce(mx[:, b, 0:heads], src, AX.X, ALU.max))
                if kind == 1:
                    link(V.tensor_tensor(mx[:, b], mx[:, b], col("swa_sink")[:, 2 * j:2 * j + 2], ALU.max))
                V.tensor_scalar(negm[:, b, 0:heads], mx[:, b, 0:heads], -MEM_SCALE if kind == 2 else -1.0, None,
                                ALU.mult).then_inc(c_max, 1)

            def normalise_c(s):
                kind, j, qt, keys, heads = step_c(s)
                b = s % 2
                dve.wait_ge(c_exp, sum(step_c(x)[4] for x in range(s + 1)))
                total = esum[:, b, 0:heads]
                if kind == 1:
                    dve.wait_ge(c_sink, 2 * (s - 15))
                    link(V.tensor_tensor(tot[:], esum[:, b], esink[:, b], ALU.add))
                    total = tot[:]
                link(V.reciprocal(rsum[:, b, 0:heads], total))
                for c in range(heads):
                    last = V.tensor_scalar(e_c[:, b, c, 0:keys], e_c[:, b, c, 0:keys], rsum[:, b, c:c + 1], None, ALU.mult)
                last.then_inc(c_p, 1)

            for a in range(N_C + 1):
                if a >= 1:
                    normalise_c(a - 1)
                if a < N_C:
                    maxima_c(a)
                if c_filler(a) is not None:
                    split_lo(c_filler(a) + 1)

            split_lo(J_OUT + 1)
            part = [buf(AT_E2 + 512 * b, 2, T) for b in range(2)]
            for n in range(12):
                b, i = n // 4, n % 4
                chunks = slice(2 * i, 2 * i + 2)
                dve.wait_ge(br_mm, n + 1)
                src = ps[:, n % 2, :].rearrange("p (a b) -> p a b", a=2)
                if b == 0:
                    V.scalar_tensor_tensor(merged[:, chunks], gate[b][:, chunks], 1.0, src, ALU.add,
                                           ALU.mult).then_inc(br_used, 1)
                else:
                    V.scalar_tensor_tensor(part[n % 2], gate[b][:, chunks], 1.0, src, ALU.add,
                                           ALU.mult).then_inc(br_used, 1)
                    dve.wait_ge(br_used, n + 1)
                    if b == 2:
                        dve.wait_ge(mg_set, n - 7)
                    V.tensor_tensor(merged[:, chunks], merged[:, chunks], part[n % 2], ALU.add).then_inc(mg_set, 1)

            for i in range(4):
                dve.wait_ge(mg_hi_set, i + 1)
                V.tensor_tensor(merged_lo[:, 2 * i:2 * i + 2], merged[:, 2 * i:2 * i + 2],
                                x_hi[:, 2 * i:2 * i + 2].bitcast(F32), ALU.subtract).then_inc(mg_lo_set, 1)
            for n in range(3):
                split_lo(J_OUT + n + 2)
            inverse_rms(NORM_POST, 2)
            for k in range(KC + 1):
                if k < KC:
                    times(mix[:, k], mix[:, k], col("mix_post")[:, k:k + 1]).then_inc(y_set, 1)
                if k >= 1:
                    dve.wait_ge(y_set, k)
                    V.tensor_tensor(xT[:, k - 1], xT[:, k - 1], mix[:, k - 1], ALU.add).then_inc(x3_set, 1)
            inverse_rms(NORM_FFN, 2)
            normed_parts(col("ffn_pre"), KC)
            split_lo(J_UP + 1)

            def product(n):
                dve.wait_ge(gelu_set, n + 1)
                dve.wait_ge(conv_set, 2 * n + 2)
                V.tensor_tensor(fT[:, 2 * n:2 * n + 2], gelu, u_val[n % 2], ALU.mult).then_inc(f_set, 1)

            def hidden_lo(n):
                dve.wait_ge(f_hi_set, n + 1)
                V.tensor_tensor(f_lo[:, 2 * n:2 * n + 2], fT[:, 2 * n:2 * n + 2],
                                f_hi[:, 2 * n:2 * n + 2].bitcast(F32), ALU.subtract).then_inc(f_lo_set, 1)

            for n in range(FC // 2):
                for two in range(2):
                    u = (u_gate, u_val)[two][n % 2]
                    for tap, late in ((1, 1), (0, 2)):
                        for c in range(2):
                            ch = FC * two + 2 * n + c
                            src = ps[:, 2 * (n % 2) + two, T * c:T * c + T]
                            if tap:
                                dve.wait_ge(tap2_set, 4 * n + 2 * two + 2)
                            last = V.scalar_tensor_tensor(u[:, c, late:T], src[:, 0:T - late],
                                                          col("conv_w")[:, 44 * tap + ch:44 * tap + ch + 1], u[:, c, late:T],
                                                          ALU.mult, ALU.add)
                        if tap:
                            link(last)
                        else:
                            last.then_inc(conv_set, 1)
                    split_lo(J_UP + 2 * n + two + 2)
                if n >= 1:
                    product(n - 1)
                if n >= 2:
                    hidden_lo(n - 2)
            product(FC // 2 - 1)
            hidden_lo(FC // 2 - 2)
            hidden_lo(FC // 2 - 1)
            for j in range(J_DN + 2, N_JOBS):
                split_lo(j)

            inverse_rms(NORM_LAST, 0)
            y = buf(AT_UB, KC, T)
            for k in range(KC + 1):
                if k < KC:
                    times(y[:, k], ps[:, 4 + k // 2, T * (k % 2):T * (k % 2) + T],
                          col("ffn_post")[:, k:k + 1]).then_inc(y_set, 1)
                if k >= 1:
                    dve.wait_ge(y_set, KC + k)
                    V.tensor_tensor(xT[:, k - 1], xT[:, k - 1], y[:, k - 1], ALU.add).then_inc(o_set, 1)


def chunks_first(v):
    return np.asarray(v).reshape(-1, P).T


def features_first(x):
    return np.ascontiguousarray(np.asarray(x)[0].T.reshape(KC, P, T).transpose(1, 0, 2))


def everywhere(v):
    return np.broadcast_to(np.asarray(v).reshape(1, -1), (P, np.asarray(v).size))


def shape_constants():
    f = np.float32
    p = np.arange(P)
    tok = np.arange(T)
    nf = HD // 4
    inv = (f(10000.0) ** (-np.arange(nf, dtype=f) / f(nf))).astype(f)
    row = (p % HD) < HD // 2
    pos = np.where(row[:, None], (tok // GRID_W)[None], (tok % GRID_W)[None]).astype(f)
    angle = (pos * inv[p % nf][:, None]).astype(f)
    sign = np.where((p % 32) < 16, f(-1), f(1))[:, None]
    q, k = p[:, None], p[None, :]
    wmask = np.concatenate([np.where(k > q, f(MASKED), f(0)), np.where(k < q, f(MASKED), f(0))], 1)
    out = {
        "ident": np.eye(P), "tri": (q < k), "cos": np.cos(angle), "sin": np.sin(angle) * sign, "wmask": wmask,
        "iota_slot": everywhere(p % SLOTS), "iota_expert": everywhere(np.arange(N_EXPERTS)),
    }
    d = T - 1 - np.arange(2 * T)
    n = np.maximum(d, 0)
    half = NUM_BUCKETS // 2
    large = half + (np.log(np.maximum(n, 1).astype(f) / f(half)) / f(np.log(128 / half)) * f(half)).astype(np.int32)
    bucket = np.where(n < half, n, np.minimum(large, NUM_BUCKETS - 1))
    hot = (bucket[None] == np.arange(NUM_BUCKETS)[:, None])
    marks = [d < 0, (d < 0) | (d >= 128)]
    onehot = np.concatenate([np.concatenate([hot & ~m[None], m[None]], 0) for m in marks], 1).astype(f)
    return {a: np.ascontiguousarray(b, dtype=f) for a, b in out.items()}, onehot


_BIG = ["w_mod", "w_in", "w_out", "w_gate_up", "w_down", "b_gate_up", "b_down", "w_in_2", "w_mem_kv_2",
        "w_branch_moba_2", "w_branch_swa_2", "w_branch_mem_2", "w_out_2", "w_ffn_up_2", "w_ffn_down_2"]


def kernel(**inputs):
    import concourse.bacc as bacc
    from concourse.bass_utils import run_bass_kernel_spmd as run

    x = {k: np.asarray(v) for k, v in inputs.items()}
    const, onehot = shape_constants()
    cols = dict(const)
    for name, src in (("b_mod", "b_mod"), ("norm1_g", "norm1_g"), ("norm2_g", "norm2_g"), ("final_g", "final_g"),
                      ("mix_pre", "norm_mix_pre_2"), ("mix_post", "norm_mix_post_2"), ("ffn_pre", "norm_ffn_pre_2"),
                      ("ffn_post", "norm_ffn_post_2"), ("mem_g", "norm_mem_2"), ("subln", "subln_g"),
                      ("conv_w", "ffn_conv_w_2"), ("conv_b", "ffn_conv_b_2")):
        cols[name] = chunks_first(x[src])
    cols["cvec"] = np.stack([chunks_first(x["c"]), chunks_first(x["c_ctx"])], 2).reshape(P, 2 * KC)
    cols["w_router"] = x["w_router"][0].reshape(KC, P, N_EXPERTS).transpose(1, 0, 2).reshape(P, KC * N_EXPERTS)
    cols["lam"] = everywhere(np.concatenate([x[n].reshape(-1) for n in ("lam_q1", "lam_k1", "lam_q2", "lam_k2")]))
    for name, src in (("sink", "sink"), ("swa_sink", "swa_sinks_2"), ("b_router", "b_router")):
        cols[name] = everywhere(x[src])
    masked_row = np.full((1, 16), MASKED, np.float32)
    arrays = {
        "small": np.concatenate([cols[n] for n, _ in SMALL], 1),
        "buckets": np.concatenate([onehot, np.concatenate([x["rel_bias_2"], masked_row], 0)], 1),
        "xT": features_first(x["x"]), "ctxT": features_first(x["ctx"]), "memT": features_first(x["mem_2"]),
    }
    for n in _BIG:
        arrays[n] = x[n]
    arrays["w_ffn_up_2"] = x["w_ffn_up_2"].reshape(1, D, 2, FC // 2, 2 * P).transpose(0, 1, 3, 2, 4).reshape(1, D, -1)
    nc = bacc.Bacc("TRN2", target_bir_lowering=False, num_devices=1)
    io = {}
    feeds = {}
    for n, a in arrays.items():
        a = np.ascontiguousarray(a)
        feeds["in_" + n] = a
        io[n] = nc.dram_tensor("in_" + n, a.shape, mybir.dt.from_np(a.dtype), kind="ExternalInput").ap()
    out = nc.dram_tensor("out_0", (P, KC, T), F32, kind="ExternalOutput").ap()
    build(nc, io, out)
    got = run(nc, [feeds], core_ids=[0]).results[0]["out_0"]
    return np.ascontiguousarray(np.asarray(got).transpose(2, 1, 0).reshape(1, T, D))
```

```python
from contextlib import ExitStack

import numpy as np
import concourse.bass as bass
from concourse import mybir

F32 = mybir.dt.float32
F32R = mybir.dt.float32r
I32 = mybir.dt.int32
U32 = mybir.dt.uint32
ALU = mybir.AluOpType
ACT = mybir.ActivationFunctionType
AX = mybir.AxisListType

P = 128
D = 1024
KC = D // P
T = 256
TT = T // P
GRID_W = 64
EPS = 1e-6
HD = 64
QK_SCALE = HD ** -0.5
MEM_SCALE = P ** -0.5
MASKED = -1e30
LAM_INIT = 0.2
N_EXPERTS = 32
TOP_K = 4
SLOTS = 64
ROUNDS_MORE = T // SLOTS - 1
D_EXPERT = 1024
FFN = 2816
FC = FFN // P
SWIGLU_LIMIT = 7.0
SWIGLU_ALPHA = 1.702
NUM_BUCKETS = 32

RING = 6
SLOT = 4096
RING1 = RING - 2
RING2 = RING - 1
SLOT_MOE = (4, 5, 2, 3, 0, 1)
SLOT_C = (4, 2, 3, 0, 1)
PART = 1024
HI_PARTS = SLOT // PART
UNITS_EXPERT = 6

SMALL = [("ident", 128), ("tri", 128), ("cos", T), ("sin", T), ("wmask", 2 * P), ("iota_slot", 128),
         ("iota_expert", 32), ("b_mod", 48), ("norm1_g", 8), ("norm2_g", 8), ("final_g", 8),
         ("mix_pre", 8), ("mix_post", 8), ("ffn_pre", 8), ("ffn_post", 8), ("mem_g", 8), ("subln", 1),
         ("conv_w", 132), ("conv_b", 44), ("cvec", 16), ("w_router", 256), ("lam", 256), ("sink", 8),
         ("swa_sink", 8), ("b_router", 32)]
SMALL_AT = {}
SMALL_N = 0
for _name, _width in SMALL:
    SMALL_AT[_name] = (SMALL_N, _width)
    SMALL_N += _width

AT_X = 0
AT_HX = 2048
AT_YT = 6144
AT_QA, AT_KA, AT_QB, AT_KB, AT_VA, AT_VB = 8192, 9216, 11264, 12288, 13312, 15360
AT_CS, AT_ROW = 15872, 16128
AT_SQ, AT_R, AT_SH, AT_T1 = 16384, 17408, 17920, 18432
AT_E, AT_MEM, AT_PT = 18944, 20992, 23040
AT_BUCKET, AT_BROW = 18944, 23552
AT_HX2, AT_HX2TM = 2048, 8192
AT_XG, AT_SGT, AT_S, AT_SG, AT_SEL = 6144, 7168, 7424, 7680, 7936
AT_KME, AT_VME, AT_BIAS, AT_BGU, AT_BDN = 4096, 5120, 10240, 13312, 15360
AT_G, AT_LIN, AT_SIGM, AT_U, AT_A, AT_AT, AT_Y = 16384, 16896, 17408, 17920, 18432, 18944, 19456
AT_PICK, AT_GT, AT_LAM = 19968, 20224, 23040
AT_SQ2 = 24320
AT_H, AT_QMB, AT_KMB = 2048, 6144, 7168
AT_VMB, AT_VSW, AT_KSW, AT_QSW, AT_QME = 13312, 14336, 14592, 15104, 16128
AT_S2, AT_E2, AT_PT2, AT_HI = 17152, 18176, 19200, 20224
AT_GMB, AT_GSW, AT_GME = 8192, 22272, 4096
AT_MERGED, AT_MIX, AT_SQ3 = 10240, 15360, 17408
AT_FT, AT_UB, AT_GELU, AT_SQ4, AT_FHI = 4096, 9728, 11776, 12288, 13312
ARENA = 25088


def build(nc, io, out):
    ctx = ExitStack()
    with ctx:
        def sb(name, shape, dt=F32):
            return ctx.enter_context(nc.sbuf_tensor(name, shape, dt))

        def sem(name):
            return ctx.enter_context(nc.semaphore(name))

        with nc.sbuf_tensor("ring", [P, RING, SLOT], F32) as ring:
            pass
        with nc.sbuf_tensor("ring_r", [P, RING, SLOT], F32R) as ring_r:
            pass
        sb("ring_start", [P, RING1, SLOT])
        hx_hi = sb("hx_hi", [P, KC, 2 * T], F32R)
        w_high = sb("w_high", [P, HI_PARTS, KC, P], F32R)
        with nc.sbuf_tensor("arena", [P, ARENA], F32) as arena:
            pass
        with nc.sbuf_tensor("arena_r", [P, ARENA], F32R) as arena_r:
            pass
        sb("arena_start", [P, AT_HX])
        hx_lo = sb("hx_lo", [P, KC, 2 * T], F32R)
        sb("arena_rest", [P, ARENA - AT_HX - 2 * KC * T])
        small = sb("small", [P, SMALL_N])
        ones = sb("ones", [P, P])
        modcol = sb("modcol", [P, 48, 2])
        scale1 = sb("scale1", [P, KC, 2])
        scale2 = sb("scale2", [P, KC])
        csig = sb("csig", [P, 16])
        both_g = sb("both_g", [P, KC])
        lamv = sb("lamv", [P, 4])
        eps = sb("eps", [P, 1])
        subln_s = sb("subln_s", [P, 1])
        mx = sb("mx", [P, 2, 2])
        negm = sb("negm", [P, 2, 2])
        esum = sb("esum", [P, 2, 2])
        esink = sb("esink", [P, 2, 2])
        tot = sb("tot", [P, 2])
        rsum = sb("rsum", [P, 2, 2])
        fneg = sb("fneg", [P, 1])
        oss = sb("oss", [P, 4])
        nrm = sb("nrm", [P, 2, T])
        logits = sb("logits", [P, TT, N_EXPERTS])
        top_v = sb("top_v", [P, TT, 8])
        top_i = sb("top_i", [P, TT, 8], U32)
        top_f = sb("top_f", [P, TT, 8])
        top_e = sb("top_e", [P, TT, TOP_K])
        top_n = sb("top_n", [P, TT])
        top_s = sb("top_s", [P, TT])
        chosen = sb("chosen", [P, TT, N_EXPERTS])
        gates = sb("gates", [P, TT, N_EXPERTS + 2])
        rank = sb("rank", [P, TT, N_EXPERTS + 2])
        most = sb("most", [P, 1])
        unread = sb("unread", [1, 16])
        most_i = sb("most_i", [P, 1], I32)
        ps = ctx.enter_context(nc.psum_tensor("ps", [P, 8, 512], F32))
        bias_rows = nc.dram_tensor("bias_rows", [16, 512], F32)

        def col(name):
            at, width = SMALL_AT[name]
            return small[:, at:at + width]

        def buf(at, *shape, of=arena):
            n = 1
            for s in shape:
                n *= s
            v = of[:, at:at + n]
            if len(shape) == 2:
                return v.rearrange("p (a b) -> p a b", a=shape[0])
            if len(shape) == 3:
                return v.rearrange("p (a b c) -> p a b c", a=shape[0], b=shape[1])
            return v

        def slot(index, a):
            return ring[:, index, :].rearrange("p (a n) -> p a n", a=a)

        ident = col("ident")
        cos, sin = col("cos"), col("sin")
        xT = buf(AT_X, KC, T)
        hx = buf(AT_HX, KC, 2 * T)
        vb_t = buf(AT_HX, 2 * T)
        yT = buf(AT_YT, KC, T)
        qa, ka = buf(AT_QA, 4, T), buf(AT_KA, 4, 2 * T)
        qb, kb = buf(AT_QB, 4, T), buf(AT_KB, 2, 2 * T)
        va, vb = buf(AT_VA, 4, 512), buf(AT_VB, 4, P)
        cs, modrow = buf(AT_CS, KC, 32), buf(AT_ROW, 2, P)
        sq, r1 = buf(AT_SQ, 2, 512), buf(AT_R, 512)
        shuf, rope1 = buf(AT_SH, 512), buf(AT_T1, 512)
        e_a = buf(AT_E, 2, 2, 512)
        pT_a = [buf(AT_PT + 1024 * b, 2, 4, P) for b in range(2)]
        o_sq, y_da = buf(AT_SQ, 512), buf(AT_SQ + 512, 512)
        buckets, brow = buf(AT_BUCKET, 1040), buf(AT_BROW, 2, 512)
        lamw = buf(AT_LAM, 2, HD)
        pick = arena[:, AT_PICK:AT_PICK + TT * TOP_K * N_EXPERTS].rearrange("p (a b c) -> p a b c", a=TT, b=TOP_K)
        gates_t = arena[0:N_EXPERTS, AT_GT:AT_GT + T]
        hx2, hx2tm = buf(AT_HX2, KC, T), buf(AT_HX2TM, TT, D)
        xg, sgt, s_hot = buf(AT_XG, KC, 2 * SLOTS), buf(AT_SGT, T), buf(AT_S, TT, 2, SLOTS)
        sg_hot, esel = buf(AT_SG, TT, 2 * SLOTS), buf(AT_SEL, SLOTS)
        memT, bias = buf(AT_MEM, KC, T), buf(AT_BIAS, 8, 384)
        b_gu, b_dn = buf(AT_BGU, 2 * D_EXPERT), buf(AT_BDN, D)
        g_e, lin_e, sig_e, u_e, a_e = (buf(x, 512) for x in (AT_G, AT_LIN, AT_SIGM, AT_U, AT_A))
        aT_e, y_e = buf(AT_AT, 4, P), buf(AT_Y, 512)
        sq_m = buf(AT_PT + 1536, 2, T)
        sq2, sq3, sq4 = buf(AT_SQ2, 2, T), buf(AT_SQ3, 2, T), buf(AT_SQ4, 2, T)
        h, k_me, v_me = buf(AT_H, KC, T), buf(AT_KME, 4, T), buf(AT_VME, TT, 512)
        q_mb, k_mb, v_mb = buf(AT_QMB, 4, T), buf(AT_KMB, 4, T), buf(AT_VMB, TT, 512)
        q_sw, k_sw, v_sw = buf(AT_QSW, 4, T), buf(AT_KSW, 2, T), buf(AT_VSW, TT, P)
        q_me = buf(AT_QME, 4, T)
        s_c, e_c = buf(AT_S2, 2, 2, T), buf(AT_E2, 2, 2, T)
        pT_c = [buf(AT_PT2 + 512 * b, 2, 2, P) for b in range(2)]
        oT = [q_mb, q_sw, q_me]
        gate = [buf(AT_GMB, KC, T), buf(AT_GSW, KC, T), buf(AT_GME, KC, T)]
        sq_mix, fin = buf(AT_S2, 2, 2 * T), buf(AT_E2, 2, T)
        merged, mix = buf(AT_MERGED, KC, T), buf(AT_MIX, KC, T)
        fT = buf(AT_FT, FC, T)
        x_hi, h_lo = buf(AT_HI, KC, T, of=arena_r), buf(AT_H, KC, T, of=arena_r)
        merged_lo = buf(AT_MERGED, KC, T, of=arena_r)
        f_hi, f_lo = buf(AT_FHI, FC, T, of=arena_r), buf(AT_FT, FC, T, of=arena_r)
        u_gate = [buf(AT_UB + 1024 * b, 2, T) for b in range(2)]
        u_val = [buf(AT_UB + 1024 * b + 512, 2, T) for b in range(2)]
        gelu = buf(AT_GELU, 2, T)

        small_in, x_in, ctx_in, bucket_in = sem("small_in"), sem("x_in"), sem("ctx_in"), sem("bucket_in")
        slot_full = [sem(f"slot_full{i}") for i in range(RING)]
        ada_mm, moe_units, more_units = sem("ada_mm"), sem("moe_units"), sem("more_units")
        mem_in, bgu_in, bdn_in = sem("mem_in"), sem("bgu_in"), sem("bdn_in")
        bias_out, bias_in, sw_bias_in = sem("bias_out"), sem("bias_in"), sem("sw_bias_in")
        dve_chain = sem("dve_chain")
        ones_set, cs_zero, csig_set, cs_set, bgu_zero = (sem("ones_set"), sem("cs_zero"), sem("csig_set"),
                                                         sem("cs_set"), sem("bgu_zero"))
        brow_mm, brow_set = sem("brow_mm"), sem("brow_set")
        sq_set, sq_used = sem("sq_set"), sem("sq_used")
        ms_set, root_set = sem("ms_set"), sem("root_set")
        lam_set, lame_set, subln_set = sem("lam_set"), sem("lame_set"), sem("subln_set")
        ada_row, ada_t, ada_col = sem("ada_row"), sem("ada_t"), sem("ada_col")
        hx_x, hx_c, scaled1 = sem("hx_x"), sem("hx_c"), sem("scaled1")
        proj_mm, proj_dve, proj_act = sem("proj_mm"), sem("proj_dve"), sem("proj_act")
        sc_mm, max_set, exp_set, p_set = sem("sc_mm"), sem("max_set"), sem("exp_set"), sem("p_set")
        sinkexp_set = sem("sinkexp_set")
        pt_mm, pt_set, pv_mm, pv_set = sem("pt_mm"), sem("pt_set"), sem("pv_mm"), sem("pv_set")
        ov_set, osq_set, oms_set, oroot_set, yda_set = (sem("ov_set"), sem("osq_set"), sem("oms_set"),
                                                        sem("oroot_set"), sem("yda_set"))
        out_mm, x1_set = sem("out_mm"), sem("x1_set")
        hx2_pre, hx2_set = sem("hx2_pre"), sem("hx2_set")
        log_mm, log_set, top_set, tope_set, route_set = (sem("log_mm"), sem("log_set"), sem("top_set"),
                                                         sem("tope_set"), sem("route_set"))
        tm_mm, tm_set = sem("tm_mm"), sem("tm_set")
        rank_mm, most_set = sem("rank_mm"), sem("most_set")
        gt_mm, gt_set, mem_set = sem("gt_mm"), sem("gt_set"), sem("mem_set")
        x2_pre, h_set = sem("x2_pre"), sem("h_set")
        fin_ms, fin_root = sem("fin_ms"), sem("fin_root")
        w_hi_set, w_lo_set, part_mm, c_act = sem("w_hi_set"), sem("w_lo_set"), sem("part_mm"), sem("c_act")
        h_hi_set, h_lo_set = sem("h_hi_set"), sem("h_lo_set")
        mg_hi_set, mg_lo_set, f_hi_set, f_lo_set = (sem("mg_hi_set"), sem("mg_lo_set"), sem("f_hi_set"),
                                                    sem("f_lo_set"))
        kv_mm, kv_act = sem("kv_mm"), sem("kv_act")
        c_sc, c_max, c_exp, c_sink, c_p = sem("c_sc"), sem("c_max"), sem("c_exp"), sem("c_sink"), sem("c_p")
        c_pt, c_pts, c_pv, c_pvs = sem("c_pt"), sem("c_pts"), sem("c_pv"), sem("c_pvs")
        br_mm, br_used, mg_set = sem("br_mm"), sem("br_used"), sem("mg_set")
        mix_set, x3_set = sem("mix_set"), sem("x3_set")
        tap2_set, conv_set, gelu_set, f_set = (sem("tap2_set"), sem("conv_set"),
                                                      sem("gelu_set"), sem("f_set"))
        y_mm, y_set, o_set, o_out = sem("y_mm"), sem("y_set"), sem("o_set"), sem("o_out")

        class MoeSems:

            def __init__(self, pre):
                self.gather_mm, self.x_ready = sem(pre + "gather_mm"), sem(pre + "x_ready")
                self.s_ready, self.sel_ready = sem(pre + "s_ready"), sem(pre + "sel_ready")
                self.sg_ready, self.h_free = sem(pre + "sg_ready"), sem(pre + "h_free")
                self.g_ready, self.sig_ready = sem(pre + "g_ready"), sem(pre + "sig_ready")
                self.u_ready, self.a_ready = sem(pre + "u_ready"), sem(pre + "a_ready")
                self.at_mm, self.at_ready = sem(pre + "at_mm"), sem(pre + "at_ready")
                self.sgt_mm, self.sgt_ready = sem(pre + "sgt_mm"), sem(pre + "sgt_ready")
                self.y_ready, self.round_done = sem(pre + "y_ready"), sem(pre + "round_done")
                self.shifted = sem(pre + "shifted")

        MAIN, MORE = MoeSems("m_"), MoeSems("f_")
        more_full = [sem(f"more_full{i}") for i in range(RING)]

        MAIN.units, MAIN.units0, MAIN.full, MAIN.full0 = moe_units, 0, slot_full, lambda q: filled_moe(q)
        MORE.units, MORE.units0, MORE.full, MORE.full0 = more_units, 1, more_full, lambda q: 16

        def blocks(w, c0, width):
            return w.rearrange("(k p) n -> p k n", p=P)[:, :, c0:c0 + width]

        def rows(w, k0, nk):
            return w.rearrange("(k p) n -> p k n", p=P)[:, k0:k0 + nk, :]

        w_mod, w_in, w_out = io["w_mod"][0], io["w_in"][0], io["w_out"][0]
        w_in2, w_kv, w_out2 = io["w_in_2"][0], io["w_mem_kv_2"][0], io["w_out_2"][0]
        w_up, w_down2 = io["w_ffn_up_2"][0], io["w_ffn_down_2"][0]
        w_gu, w_dn = io["w_gate_up"][0], io["w_down"][0]
        first = [blocks(w_mod, 512 * u, 512) for u in range(4)]
        U_IN = len(first)
        first += [blocks(w_in, 512 * u, 512) for u in range(4)] + [blocks(w_in, 2048, 256)]
        U_KV = len(first)
        first += [blocks(w_kv, 0, 256), blocks(w_kv, 512, 512)]
        U_MOD2 = len(first)
        first += [blocks(w_mod, 512 * u, 512) for u in range(4, 12)]
        U_OUT = len(first)
        first += [blocks(w_out, 512 * u, 512) for u in range(2)]
        U_KV2 = len(first)
        first += [blocks(w_kv, 256, 256)]
        U_MOE = len(first)
        V_IN = 0
        second = [blocks(w_in2, c0, 512) for c0 in (0, 512, 1024, 2304, 1536)] + [blocks(w_in2, 2048, 256)]
        second += [blocks(w_in2, 2816 + 512 * u, 512) for u in range(6)]
        V_BR = len(second)
        second += [rows(io[n][0], 0, 4) for n in ("w_branch_moba_2", "w_branch_swa_2", "w_branch_mem_2")]
        V_OUT = len(second)
        second += [blocks(w_out2, 512 * u, 512) for u in range(2)]
        V_UP = len(second)
        second += [blocks(w_up, 512 * u, 512) for u in range(FC // 2)]
        V_DN = len(second)
        second += [rows(w_down2, 4 * u, min(4, FC - 4 * u)) for u in range((FC + 3) // 4)]

        def unit_dst(index, src):
            n = 1
            for s in src.shape[1:]:
                n *= s
            return ring[:, index, 0:n].rearrange("p (k n) -> p k n", k=src.shape[1])

        def filled(u):
            return 16 * (u // RING1 + 1)

        def fills1(at):
            return len(range(at, U_MOE, RING1)) if at < RING1 else 0

        def filled_moe(q):
            return 16 * (fills1(SLOT_MOE[q]) + 1)

        def filled_c(c):
            return 16 * (fills1(SLOT_C[c % RING2]) + N_EXPERTS + c // RING2 + 1)

        JOBS = ([("qa", 0), ("qa", 1)] + [("ka", i) for i in range(4)] + [("va", i) for i in range(4)]
                + [("qb", 0), ("qb", 1), ("kb", 0), ("vb", 0), ("vt", 0)])
        ROPED = [i for i, (n, _) in enumerate(JOBS) if n[0] in "qk"]
        COPIED = [i for i, (n, _) in enumerate(JOBS) if n[0] in "kv"]
        EARLY = 10
        MEM_JOB = 4
        BIAS_JOB = 2
        COL_BANKS = (6, 4, 3, 2)
        ROW_BANKS = (5, 7)

        PARTS1 = [(U_IN + u, 512, m) for u in range(4) for m in range(4)] + [(U_IN + 4, 2 * P, m) for m in range(2)]
        N_PARTS1 = len(PARTS1)
        JOB_PARTS = ([(0, 1), (2, 3)] + [(4 + i,) for i in range(4)] + [(8 + i // 2 * 2, 9 + i // 2 * 2) for i in range(4)]
                     + [(12, 13), (14, 15), (16,), (17,), ()])
        LAST_JOB = [max(n for n, parts in enumerate(JOB_PARTS) if p in parts) for p in range(N_PARTS1)]

        def part1(p, of):
            u, width, m = PARTS1[p]
            return of[:, u % RING1, 0:KC * width].rearrange("p (k n) -> p k n", k=KC)[:, :, P * m:P * m + P]

        def split_after(n):
            free = [p for p in range(HI_PARTS, N_PARTS1) if LAST_JOB[p - HI_PARTS] == n]
            return free

        def upto(jobs, n):
            return sum(j <= n for j in jobs)

        N_DA, N_AT = 8, 16

        def step_a(a):
            return (a // 4, a % 4) if a < N_DA else ((a - N_DA) % 2, (a - N_DA) // 2)

        def p_upto(a):
            return a + 1 if a < N_DA else N_DA + 2 * (a - N_DA + 1)

        TURNS = []
        for a in range(N_AT + 2):
            if 1 <= a <= N_AT:
                TURNS.append(("p", a - 1, 0))
                if a - 1 >= N_DA:
                    TURNS.append(("p", a - 1, 1))
            if a in (7, 11):
                TURNS.append(("y", a // 8, 0))

        def turn(kind, a, c=0):
            return TURNS.index((kind, a, c))

        ADA_STEP = 5

        KV_STEP = len(JOBS) - EARLY
        ADA_STEP = KV_STEP + 3

        KV_JOBS = (("k", 0, U_KV, 0), ("v", 0, U_KV + 1, 1), ("v", 1, U_KV + 1, 0), ("k", 1, U_KV2, 6))

        def kv_at(a):
            return a - KV_STEP if KV_STEP <= a < ADA_STEP else None

        def ada_at(a):
            return 4 + a - ADA_STEP if ADA_STEP <= a < ADA_STEP + 8 else None

        C_JOBS = ([("qmb", 0), ("qmb", 1), ("kmb", 0), ("kmb", 1), ("vmb", 0), ("vmb", 1), ("qme", 0), ("qme", 1),
                   ("qsw", 0), ("qsw", 1), ("kvsw", 0)] + [("gate", i) for i in range(12)])
        C_EARLY, N_C = 6, 24
        BIAS_STEP = 13
        BR_STEP = 22

        def c_filler(a):
            return C_EARLY + a if a < 13 else (C_EARLY + a - 5 if 18 <= a < 22 else None)

        C_UNIT = {"qmb": 0, "kmb": 1, "vmb": 2, "qme": 3, "qsw": 4, "kvsw": 5}
        PARTS = []
        for name, i in C_JOBS:
            u = V_IN + (C_UNIT[name] if name != "gate" else 6 + i // 2)
            PARTS += [(u, 2 * P if name == "kvsw" else 512, 2 * (i % 2) + c) for c in range(2)]
        J_OUT = len(PARTS) // 2
        PARTS += [(V_OUT + m // 4, 512, m % 4) for m in range(KC)]
        J_UP = len(PARTS) // 2
        PARTS += [(V_UP + n, 512, m) for n in range(FC // 2) for m in range(4)]
        J_DN = len(PARTS) // 2
        PARTS += [(V_DN + f // 4, None, f % 4) for f in range(FC)]
        N_JOBS = len(PARTS) // 2

        def part_of(n, of):
            c, width, i = PARTS[n]
            v = of[:, SLOT_C[c % RING2], :]
            if width is None:
                return v[:, PART * i:PART * i + PART].rearrange("p (k n) -> p k n", k=KC)
            return v[:, 0:KC * width].rearrange("p (k n) -> p k n", k=KC)[:, :, P * i:P * i + P]

        def part_hi(n):
            return w_high[:, n % HI_PARTS]

        def done(j):
            return 2 * j + 2

        def step_c(a):
            kind, j, qt = (0, 2, 1)[a // 8], a % 8 // 2, a % 2
            return kind, j, qt, (T if kind == 2 else P * (qt + 1)), (1 if kind == 2 else 2)

        NORM1, NORM_MEM, NORM2, NORM_MIX, NORM_POST, NORM_FFN, NORM_LAST = range(7)

        def chain(engine, done):
            count = [0]

            def link(ins):
                count[0] += 1
                ins.then_inc(done, 1)
                engine.wait_ge(done, count[0])
            return link

        block = ctx.enter_context(nc.Block())

        freed = [(ada_mm, n + 1) for n in range(4)]
        freed += [(proj_mm, 1 + max(LAST_JOB[p] for p in range(N_PARTS1) if PARTS1[p][0] == U_IN + u)) for u in range(5)]
        freed += [(kv_mm, 1), (kv_mm, 3)]
        freed += [(ada_mm, n + 1) for n in range(4, 12)] + [(out_mm, 2), (out_mm, 4), (kv_mm, 4)]
        freed_c = [(br_mm, 4 * (c - V_BR) + 4) if V_BR <= c < V_OUT
                   else (part_mm, 1 + max(n for n, part in enumerate(PARTS) if part[0] == c))
                   for c in range(len(second))]

        @block.sync
        def _(sp):
            def load(u, dst, src):
                if u >= RING1:
                    sp.wait_ge(*freed[u - RING1])
                sp.dma_start(dst, src).then_inc(slot_full[u % RING1], 16)

            gu_rows = w_gu.rearrange("e (k p) n -> e p k n", p=P)
            dn_rows = w_dn.rearrange("e (k p) n -> e p k n", p=P)

            def expert_unit(e, q):
                if q < 4:
                    return slot(SLOT_MOE[q], 2), gu_rows[e, :, 2 * q:2 * q + 2, :]
                return slot(SLOT_MOE[q], 4), dn_rows[e, :, 4 * (q - 4):4 * (q - 4) + 4, :]

            sp.dma_start(xT, io["xT"]).then_inc(x_in, 16)
            sp.dma_start(hx[:, :, T:2 * T], io["ctxT"]).then_inc(ctx_in, 16)
            for u, src in enumerate(first):
                if u == U_IN + 4:
                    sp.dma_start(memT, io["memT"]).then_inc(mem_in, 16)
                load(u, unit_dst(u % RING1, src), src)
                if u == U_MOD2 + 1:
                    sp.wait_ge(proj_mm, JOBS.index(("vb", 0)) + 1)
                    for q in range(2):
                        sp.dma_start(*expert_unit(0, q)).then_inc(slot_full[SLOT_MOE[q]], 16)
            for q in range(2, UNITS_EXPERT):
                sp.wait_ge(*freed[max(range(SLOT_MOE[q], U_MOE, RING1))])
                sp.dma_start(*expert_unit(0, q)).then_inc(slot_full[SLOT_MOE[q]], 16)
            with sp.Fori(1, N_EXPERTS) as e:
                for q in range(UNITS_EXPERT):
                    sp.wait_ge(moe_units, e * UNITS_EXPERT + (q + 1 - RING))
                    sp.dma_start(*expert_unit(e, q)).then_inc(slot_full[SLOT_MOE[q]], 16)
            sp.wait_ge(most_set, 1)
            count = sp.value_load(most_i[0:1, 0:1], min_val=0, max_val=T)
            with sp.If(count > SLOTS):
                sp.wait_ge(moe_units, UNITS_EXPERT * N_EXPERTS)
                with sp.Fori(0, ROUNDS_MORE) as r:
                    with sp.Fori(0, N_EXPERTS) as e:
                        sp.wait_ge(more_units, r * (UNITS_EXPERT * N_EXPERTS) + e * UNITS_EXPERT + 1)
                        for q in range(UNITS_EXPERT):
                            sp.dma_start(*expert_unit(e, q)).then_inc(more_full[SLOT_MOE[q]], 16)
                sp.wait_ge(more_units, ROUNDS_MORE * UNITS_EXPERT * N_EXPERTS + 1)
            for c, src in enumerate(second):
                at = SLOT_C[c % RING2]
                if c < RING2:
                    sp.wait_ge(moe_units, UNITS_EXPERT * (N_EXPERTS - 1) + SLOT_MOE.index(at) + 1)
                else:
                    sp.wait_ge(*freed_c[c - RING2])
                sp.dma_start(unit_dst(at, src), src).then_inc(slot_full[at], 16)
            for k in range(KC):
                sp.wait_ge(o_set, k + 1)
                sp.dma_start(out[:, k, :], xT[:, k, :]).then_inc(o_out, 16)
            sp.wait_ge(o_out, 16 * KC)

        def bias_loads(engine, group, landed):
            for qt in range(TT):
                keys, at = P * (qt + 1), P * qt
                for quad in range(4):
                    q_last = P * qt + 32 * quad + 31
                    src = bass.AP(bias_rows, 512 * 8 * group + T - 1 - q_last, [[1, 32], [512, 8], [1, keys]])
                    engine.dma_start(bias[32 * quad:32 * quad + 32, :, at:at + keys], src).then_inc(landed, 16)

        BIAS_LOADS = 4 * TT

        @block.gpsimd
        def _(pool):
            nc.gpsimd.memset(eps[:], EPS).then_inc(ones_set, 1)
            nc.gpsimd.memset(ones[:], 1.0).then_inc(ones_set, 1)
            nc.gpsimd.memset(cs, 0.0).then_inc(cs_zero, 1)
            pool.wait_ge(pv_mm, N_AT)
            nc.gpsimd.memset(b_gu, 0.0).then_inc(bgu_zero, 1)
            pool.wait_ge(c_max, 8)
            bias_loads(pool, 1, sw_bias_in)

        @block.tensor
        def _(pe):
            def mm(out_, lhsT, rhs, start, stop, **kw):
                return nc.tensor.matmul(out_, lhsT, rhs, start=start, stop=stop, **kw)

            def sum_squares(norm, src, bank, width, k0=0, k1=KC):
                for k in range(k0, k1):
                    pe.wait_ge(sq_set, KC * norm + k + 1)
                    mm(ps[:, bank, 0:width], ones[:], src[:, k % 2, :], k == 0, k == KC - 1).then_inc(sq_used, 1)

            pe.wait_ge(ones_set, 2)
            sum_squares(NORM1, sq, 7, 2 * T)

            def ada_rows(n, bank):
                u = n if n < 4 else U_MOD2 + n - 4
                w = slot(u % RING1, KC)
                pe.wait_ge(slot_full[u % RING1], filled(u))
                if n:
                    pe.wait_ge(ada_row, n)
                for k in range(KC):
                    for j in range(4):
                        last = mm(ps[32 * j:32 * j + 32, bank, 0:P], cs[:, k, :], w[:, k, P * j:P * j + P],
                                  k == 0, k == KC - 1)
                last.then_inc(ada_mm, 1)

            def ada_turn(n, bank):
                pe.wait_ge(ada_row, n + 1)
                if n > 4:
                    pe.wait_ge(ada_col, n)
                nc.tensor.transpose(ps[:, bank, 0:P], modrow[:, n % 2, :], ident).then_inc(ada_t, 1)

            pe.wait_ge(cs_set, 1)
            for n in range(4):
                ada_rows(n, 5)
                ada_turn(n, COL_BANKS[n])

            def split_product(o, hi, lo, x_hi_, x_lo_, first, last):
                mm(o, hi, x_hi_, first, False, skip_group_check=True)
                mm(o, hi, x_lo_, False, False, skip_group_check=True)
                return mm(o, lo, x_hi_, False, last, skip_group_check=True)

            def project(n):
                name, i = JOBS[n]
                if n >= 2:
                    pe.wait_ge(proj_dve, upto(ROPED, n - 2))
                    if upto(COPIED, n - 2):
                        pe.wait_ge(proj_act, upto(COPIED, n - 2))
                bank = ps[:, n % 2, :]
                if name == "vt":
                    pe.wait_ge(proj_act, upto(COPIED, n - 1))
                    for t in range(4):
                        last = nc.tensor.transpose(bank[:, P * t:P * t + P], vb_t[:, P * t:P * t + P], ident)
                    last.then_inc(proj_mm, 1)
                    return
                if name == "va":
                    p = JOB_PARTS[n][0]
                    pe.wait_ge(w_lo_set, p + 2)
                    u, _, m = PARTS1[p]
                    w_hi = w_high[:, p % HI_PARTS:p % HI_PARTS + 2].rearrange("p c k n -> p k c n")
                    w_lo = ring_r[:, u % RING1, :].rearrange("p (k n) -> p k n", k=KC)[:, :, P * m:P * m + 2 * P]
                    for c in range(2):
                        t = 2 * (i % 2) + c
                        tok = slice(P * t, P * t + P)
                        for k in range(KC):
                            last = split_product(bank[:, T * c:T * c + T], hx_hi[:, k, tok], hx_lo[:, k, tok], w_hi[:, k],
                                                 w_lo[:, k], k == 0, k == KC - 1)
                else:
                    wide = T if name[0] == "q" else 2 * T
                    for c, p in enumerate(JOB_PARTS[n]):
                        w_hi, w_lo = part_hi(p), part1(p, ring_r)
                        pe.wait_ge(w_lo_set, p + 1)
                        for k in range(KC):
                            if n == 0 and c == 0:
                                pe.wait_ge(h_lo_set, k + 1)
                            if n == 2:
                                pe.wait_ge(h_lo_set, KC + k + 1)
                            last = split_product(bank[:, T * c:T * c + wide], w_hi[:, k, :], w_lo[:, k, :],
                                                 hx_hi[:, k, 0:wide], hx_lo[:, k, 0:wide], k == 0, k == KC - 1)
                last.then_inc(proj_mm, 1)

            for n in range(EARLY):
                project(n)
                if n == BIAS_JOB:
                    pe.wait_ge(bucket_in, 16)
                    pe.wait_ge(ada_row, 4)
                    pe.wait_ge(root_set, NORM1 + 1)
                    for g in range(2):
                        mm(ps[0:8, ROW_BANKS[g], :], buckets[0:33, 1024 + 8 * g:1032 + 8 * g],
                           buckets[0:33, 512 * g:512 * g + 512], True, True).then_inc(brow_mm, 1)
                if MEM_JOB < n <= MEM_JOB + 4:
                    k = 2 * (n - MEM_JOB - 1)
                    pe.wait_ge(brow_set, 2)
                    sum_squares(NORM_MEM, sq_m, 7, T, k, k + 2)

            def scores(a):
                qt, j = step_a(a)
                b = a % 2
                if a == 0:
                    pe.wait_ge(proj_dve, upto(ROPED, EARLY - 1))
                    pe.wait_ge(proj_act, upto(COPIED, EARLY - 1))
                    pe.wait_ge(ada_col, 4)
                    pe.wait_ge(brow_set, 2)
                    pe.wait_ge(root_set, NORM_MEM + 1)
                if a == N_DA:
                    pe.wait_ge(proj_dve, len(ROPED))
                    pe.wait_ge(proj_act, len(COPIED))
                if a >= 2:
                    pe.wait_ge(exp_set, 2 * (a - 1))
                for c in range(2):
                    half = slice(HD * c, HD * c + HD)
                    q = (qa if a < N_DA else qb)[half, j, P * qt:P * qt + P]
                    k = ka[half, j, :] if a < N_DA else kb[half, j // 2, :]
                    last = mm(ps[:, 4 + 2 * b + c, :], q, k, True, True)
                last.then_inc(sc_mm, 1)

            def turn_bank(kind, a, c=0):
                n = turn(kind, a, c)
                if n:
                    pe.wait_ge(pt_set, n)
                src = y_da if kind == "y" else e_a[:, a % 2, c]
                if kind == "y":
                    pe.wait_ge(yda_set, a + 1)
                else:
                    pe.wait_ge(p_set, p_upto(a) if a < N_DA else p_upto(a - 1) + c + 1)
                for kt in range(4):
                    last = nc.tensor.transpose(ps[:, 2, P * kt:P * kt + P], src[:, P * kt:P * kt + P], ident)
                last.then_inc(pt_mm, 1)

            def values(a):
                qt, j = step_a(a)
                pe.wait_ge(pt_set, turn("p", a, int(a >= N_DA)) + 1)
                if a < N_DA:
                    if a == 4:
                        pe.wait_ge(ov_set, 1)
                    for kt in range(4):
                        last = mm(ps[:, 3, P * j:P * j + P], pT_a[a % 2][:, 0, kt, :], va[:, kt, P * j:P * j + P],
                                  kt == 0, kt == 3)
                else:
                    if a == N_DA:
                        pe.wait_ge(ov_set, 2)
                    else:
                        pe.wait_ge(pv_set, a - N_DA)
                    kv = j // 2
                    for kt in range(4):
                        for c in range(2):
                            last = mm(ps[HD * c:HD * c + HD, 3, 0:P], vb[:, kt, HD * kv:HD * kv + HD],
                                      pT_a[a % 2][:, c, kt, :], kt == 0, kt == 3)
                last.then_inc(pv_mm, 1)

            def memory_job(n):
                kind, i, u, bank = KV_JOBS[n]
                w = slot(u % RING1, KC) if kind == "v" else ring[:, u % RING1, 0:2048].rearrange("p (k n) -> p k n", k=KC)
                if n == 0:
                    pe.wait_ge(mem_set, KC)
                    pe.wait_ge(proj_dve, len(ROPED))
                    pe.wait_ge(proj_act, len(COPIED))
                if n == 2:
                    pe.wait_ge(kv_act, 1)
                pe.wait_ge(slot_full[u % RING1], filled(u))
                if kind == "k":
                    for c in range(2):
                        for k in range(KC):
                            last = mm(ps[:, bank, T * c:T * c + T], w[:, k, P * c:P * c + P], memT[:, k, :],
                                      k == 0, k == KC - 1)
                else:
                    for k in range(KC):
                        last = mm(ps[:, bank, :], memT[:, k, P * i:P * i + P], w[:, k, :], k == 0, k == KC - 1)
                last.then_inc(kv_mm, 1)

            for a in range(N_AT + 2):
                if a < N_AT:
                    scores(a)
                if EARLY + a < len(JOBS):
                    project(EARLY + a)
                if kv_at(a) is not None:
                    memory_job(kv_at(a))
                if 1 <= a <= N_AT:
                    turn_bank("p", a - 1)
                if ada_at(a) is not None:
                    if a == ADA_STEP:
                        pe.wait_ge(kv_act, 3)
                    ada_rows(ada_at(a), 1)
                if a >= 2:
                    values(a - 2)
                if N_DA < a <= N_AT:
                    turn_bank("p", a - 1, 1)
                if ada_at(a) is not None:
                    ada_turn(ada_at(a), 0)
                if a in (7, 11):
                    turn_bank("y", a // 8)

            pe.wait_ge(ada_col, 12)
            pe.wait_ge(pt_set, len(TURNS))
            pe.wait_ge(pv_set, N_AT - N_DA)
            for n in range(4):
                u = U_OUT + n // 2
                w = slot(u % RING1, KC)
                pe.wait_ge(slot_full[u % RING1], filled(u))
                if n >= 2:
                    pe.wait_ge(x1_set, 2 * (n - 1))
                for c in range(2):
                    m = 2 * (n % 2) + c
                    for k in range(KC):
                        last = mm(ps[:, n % 2, T * c:T * c + T], w[:, k, P * m:P * m + P], yT[:, k, :],
                                  k == 0, k == KC - 1)
                last.then_inc(out_mm, 1)
            sum_squares(NORM2, sq2, 2, T)
            memory_job(3)
            for t in range(TT):
                for k in range(KC):
                    if t == 0:
                        pe.wait_ge(hx2_set, k + 1)
                    last = mm(ps[:, 3, 32 * t:32 * t + 32], hx2[:, k, P * t:P * t + P],
                              col("w_router")[:, 32 * k:32 * k + 32], k == 0, k == KC - 1)
                last.then_inc(log_mm, 1)
            pe.wait_ge(x1_set, KC)
            for n in range(4):
                t, half = n // 2, n % 2
                if n >= 2:
                    pe.wait_ge(tm_set, n - 1)
                for c in range(4):
                    last = nc.tensor.transpose(ps[:, n % 2, P * c:P * c + P], hx2[:, 4 * half + c, P * t:P * t + P],
                                               ident)
                last.then_inc(tm_mm, 1)
            pe.wait_ge(route_set, 1)
            for t in range(TT):
                mm(ps[:, 4, 32 * t:32 * t + 32], col("tri"), chosen[:, t, :], True, t == 0)
                if t:
                    mm(ps[:, 4, 32 * t:32 * t + 32], ones[:], chosen[:, 0, :], False, True)
            for t in range(TT):
                last = mm(ps[:, 4, 64:96], ones[:], chosen[:, t, :], t == 0, t == TT - 1)
            last.then_inc(rank_mm, 1)
            for t in range(TT):
                last = nc.tensor.transpose(ps[0:32, 5, P * t:P * t + P], gates[:, t, 0:N_EXPERTS], ident)
            last.then_inc(gt_mm, 1)
            pe.wait_ge(root_set, NORM2 + 1)
            pe.wait_ge(tm_set, 4)
            pe.wait_ge(log_set, 1)
            pe.wait_ge(bgu_in, 16)

            def start_sums(chunks):
                for m in chunks:
                    mm(ps[:, 4 + m // 2, T * (m % 2):T * (m % 2) + T], b_dn[0:N_EXPERTS, P * m:P * m + P], gates_t[:],
                       m % 2 == 0, False, skip_group_check=True)

            pe.wait_ge(gt_set, 1)
            pe.wait_ge(bdn_in, 16)
            pe.wait_ge(kv_act, 4)
            start_sums(range(4, KC))
            pe.wait_ge(most_set, 1)

            def round_pe(S, r, first):
                def gather(half):
                    for c in range(4):
                        for t in range(TT):
                            last = mm(ps[:, 2, P * c:P * c + P], hx2tm[:, t, P * (4 * half + c):P * (4 * half + c) + P],
                                      s_hot[:, t].rearrange("p a b -> p (a b)"), t == 0, t == TT - 1)
                    last.then_inc(S.gather_mm, 1)

                def combine():
                    for c in range(4):
                        for half in range(2):
                            m = 4 * half + c
                            rows_ = slice(SLOTS * half, SLOTS * half + SLOTS)
                            last = mm(ps[:, 4 + m // 2, T * (m % 2):T * (m % 2) + T], y_e[rows_, P * c:P * c + P],
                                      sgt[rows_, :], False, False, skip_group_check=True)
                    return last

                pe.wait_ge(S.s_ready, r * 17 + 1)
                gather(0)
                if first is not None:
                    first(range(4))
                pe.wait_ge(S.x_ready, r * 34 + 1)
                gather(1)
                with pe.Fori(0, N_EXPERTS // 2) as i:
                    for j in range(2):
                        e = i * 2 + j
                        pe.wait_ge(S.h_free, r * 33 + (e + 1))
                        pe.wait_ge(S.sel_ready, r * 33 + (e + 1))
                        if j == 0:
                            pe.wait_ge(S.x_ready, r * 34 + (i * 2 + 2))
                        for n in range(2):
                            for half in range(2):
                                at = 1024 * half + 512 * n
                                mm(ps[SLOTS * half:SLOTS * half + SLOTS, n, :], esel, b_gu[:, at:at + 512], True, False)
                        for q in range(4):
                            w = slot(SLOT_MOE[q], 2)
                            pe.wait_ge(S.full[SLOT_MOE[q]], (r * N_EXPERTS + e) * 16 + S.full0(q))
                            for kk in range(2):
                                k = 2 * q + kk
                                for n in range(2):
                                    for half in range(2):
                                        at = 1024 * half + 512 * n
                                        last = mm(ps[SLOTS * half:SLOTS * half + SLOTS, n, :],
                                                  xg[:, k, SLOTS * j:SLOTS * j + SLOTS], w[:, kk, at:at + 512],
                                                  False, k == KC - 1)
                            last.then_inc(S.units, 1)
                        pe.wait_ge(S.y_ready, r * 33 + (e + 1))
                        pe.wait_ge(S.sgt_ready, r * 33 + (e + 1))
                        combine()
                        pe.wait_ge(S.sg_ready, r * 33 + (e + 1))
                        for t in range(TT):
                            last = nc.tensor.transpose(ps[:, 3, P * t:P * t + P], sg_hot[:, t, :], ident)
                        last.then_inc(S.sgt_mm, 1)
                        if j == 1:
                            pe.wait_ge(S.s_ready, r * 17 + (i + 2))
                            pe.wait_ge(S.at_ready, r * 32 + e)
                            gather(0)
                            pe.wait_ge(S.x_ready, r * 34 + (i * 2 + 3))
                            gather(1)
                            pe.wait_ge(S.x_ready, r * 34 + (i * 2 + 4))
                        pe.wait_ge(S.a_ready, r * 32 + (e + 1))
                        for b in range(4):
                            last = nc.tensor.transpose(ps[:, 2, P * b:P * b + P], a_e[:, P * b:P * b + P], ident)
                        last.then_inc(S.at_mm, 1)
                        pe.wait_ge(S.at_ready, r * 32 + (e + 1))
                        pe.wait_ge(S.sgt_ready, r * 33 + (e + 2))
                        for q in range(4, UNITS_EXPERT):
                            w = slot(SLOT_MOE[q], 4)
                            pe.wait_ge(S.full[SLOT_MOE[q]], (r * N_EXPERTS + e) * 16 + S.full0(q))
                            for kk in range(4):
                                f = 4 * (q - 4) + kk
                                for half in range(2):
                                    last = mm(ps[SLOTS * half:SLOTS * half + SLOTS, 3, :],
                                              aT_e[:, f % 4, SLOTS * (f // 4):SLOTS * (f // 4) + SLOTS],
                                              w[:, kk, 512 * half:512 * half + 512], f == 0, f == KC - 1)
                            last.then_inc(S.units, 1)
                pe.wait_ge(S.y_ready, r * 33 + 33)
                pe.wait_ge(S.sgt_ready, r * 33 + 33)
                combine().then_inc(S.round_done, 1)

            def if_more(engine):
                engine.wait_ge(most_set, 1)
                return engine.If(engine.value_load(most_i[0:1, 0:1], min_val=0, max_val=T) > SLOTS)

            round_pe(MAIN, 0, start_sums)
            with if_more(pe):
                pe.sem_inc(more_units, 1)
                with pe.Fori(0, ROUNDS_MORE) as r:
                    round_pe(MORE, r, None)

            def columns(n, o, hi, lo):
                w_hi, w_lo = part_hi(n), part_of(n, ring_r)
                pe.wait_ge(w_lo_set, N_PARTS1 + n + 1)
                for k in range(KC):
                    if n == 0:
                        pe.wait_ge(h_lo_set, 2 * KC + k + 1)
                    if n == 2 * J_OUT and k % 2 == 0:
                        pe.wait_ge(mg_lo_set, k // 2 + 1)
                    if n == 2 * J_UP:
                        pe.wait_ge(h_lo_set, 3 * KC + k + 1)
                    last = split_product(o, w_hi[:, k, :], w_lo[:, k, :], hi[:, k, :], lo[:, k, :], k == 0, k == KC - 1)
                last.then_inc(part_mm, 1)

            def rows_of(n, o, hi, lo):
                w_hi, w_lo = part_hi(n), part_of(n, ring_r)
                pe.wait_ge(w_lo_set, N_PARTS1 + n + 1)
                for t in range(TT):
                    tok = slice(P * t, P * t + P)
                    for k in range(KC):
                        last = split_product(o[:, t], hi[:, k, tok], lo[:, k, tok], w_hi[:, k, :], w_lo[:, k, :], k == 0,
                                             k == KC - 1)
                last.then_inc(part_mm, 1)

            def project_c(j):
                name, i = C_JOBS[j]
                if j >= 2:
                    pe.wait_ge(c_act, j - 1)
                if name == "vmb":
                    pe.wait_ge(w_lo_set, N_PARTS1 + 2 * j + 2)
                    b = 2 * j % HI_PARTS
                    w_hi = w_high[:, b:b + 2].rearrange("p c k n -> p k c n")
                    w_lo = ring_r[:, SLOT_C[PARTS[2 * j][0] % RING2], :].rearrange("p (k n) -> p k n", k=KC)[:, :, T * i:T * i + T]
                    for t in range(TT):
                        tok = slice(P * t, P * t + P)
                        for k in range(KC):
                            last = split_product(ps[:, j % 2, T * t:T * t + T], x_hi[:, k, tok], h_lo[:, k, tok], w_hi[:, k],
                                                 w_lo[:, k], k == 0, k == KC - 1)
                    last.then_inc(part_mm, 2)
                    return
                for c in range(2):
                    n = 2 * j + c
                    if name == "kvsw" and c:
                        rows_of(n, ps[:, j % 2, T:2 * T].rearrange("p (t n) -> p t n", t=TT), x_hi, h_lo)
                    else:
                        columns(n, ps[:, j % 2, T * c:T * c + T], x_hi, h_lo)

            sum_squares(NORM_MIX, sq_mix, 2, 2 * T)
            for n in range(C_EARLY):
                project_c(n)

            def scores_c(a):
                kind, j, qt, keys, heads = step_c(a)
                b = a % 2
                if a % 8 == 0:
                    pe.wait_ge(c_act, (C_EARLY, C_EARLY + 2, C_EARLY + 5)[a // 8])
                if a >= 2:
                    pe.wait_ge(c_exp, sum(step_c(s)[4] for s in range(a - 1)))
                queries = slice(P * qt, P * qt + P)
                for c in range(heads):
                    half = slice(HD * c, HD * c + HD)
                    if kind == 0:
                        q, k = q_mb[half, j, queries], k_mb[half, j, 0:keys]
                    elif kind == 1:
                        q, k = q_sw[half, j, queries], k_sw[half, j // 2, 0:keys]
                    else:
                        q, k = q_me[:, j, queries], k_me[:, j, :]
                    last = mm(ps[:, 4 + 2 * b + c, 0:keys], q, k, True, True)
                last.then_inc(c_sc, 1)

            def turn_c(a):
                kind, j, qt, keys, heads = step_c(a)
                if a >= 1:
                    pe.wait_ge(c_pts, a)
                pe.wait_ge(c_p, a + 1)
                nk = keys // P
                for c in range(heads):
                    for kt in range(nk):
                        at = P * (nk * c + kt)
                        last = nc.tensor.transpose(ps[:, 2, at:at + P], e_c[:, a % 2, c, P * kt:P * kt + P], ident)
                last.then_inc(c_pt, 1)

            def values_c(a):
                kind, j, qt, keys, heads = step_c(a)
                nk = keys // P
                pe.wait_ge(c_pts, a + 1)
                if a >= 1:
                    pe.wait_ge(c_pvs, a)
                for kt in range(nk):
                    for c in range(heads):
                        if kind == 2:
                            o, v = ps[:, 3, 0:P], v_me[:, kt, P * j:P * j + P]
                        else:
                            o = ps[HD * c:HD * c + HD, 3, 0:P]
                            v = (v_mb[:, kt, HD * (2 * j + c):HD * (2 * j + c) + HD] if kind == 0
                                 else v_sw[:, kt, HD * (j // 2):HD * (j // 2) + HD])
                        last = mm(o, v, pT_c[a % 2][:, c, kt, :], kt == 0, kt == nk - 1)
                last.then_inc(c_pv, 1)

            def branch(n):
                b, i = n // 4, n % 4
                if n == 0:
                    pe.wait_ge(c_pvs, N_C // 3)
                    pe.wait_ge(c_act, len(C_JOBS))
                w = ring[:, SLOT_C[(V_BR + b) % RING2], :].rearrange("p (k n) -> p k n", k=4)
                pe.wait_ge(slot_full[SLOT_C[(V_BR + b) % RING2]], filled_c(V_BR + b))
                if n >= 2:
                    pe.wait_ge(br_used, n - 1)
                for c in range(2):
                    m = 2 * i + c
                    for k in range(4):
                        last = mm(ps[:, n % 2, T * c:T * c + T], w[:, k, P * m:P * m + P], oT[b][:, k, :],
                                  k == 0, k == 3)
                last.then_inc(br_mm, 1)

            pe.wait_ge(root_set, NORM_MIX + 1)
            for a in range(N_C + 2):
                if a < N_C:
                    scores_c(a)
                if c_filler(a) is not None:
                    project_c(c_filler(a))
                if a >= BR_STEP:
                    branch(a - BR_STEP)
                if 1 <= a <= N_C:
                    turn_c(a - 1)
                if a >= 2:
                    values_c(a - 2)

            pe.wait_ge(c_pvs, N_C)
            for n in range(4, 12):
                branch(n)
            for n in range(4):
                if n == 0:
                    pe.wait_ge(br_used, 12)
                if n >= 2:
                    pe.wait_ge(mix_set, n - 1)
                for c in range(2):
                    columns(2 * (J_OUT + n) + c, ps[:, n % 2, T * c:T * c + T], x_hi, merged_lo)
                if n:
                    sum_squares(NORM_POST, sq3, 2, T, 2 * n - 2, 2 * n)
            sum_squares(NORM_POST, sq3, 2, T, KC - 2, KC)
            pe.wait_ge(root_set, NORM_POST + 1)
            sum_squares(NORM_FFN, sq3, 2, T)
            pe.wait_ge(root_set, NORM_FFN + 1)
            for n in range(FC // 2):
                if n >= 2:
                    pe.wait_ge(conv_set, 2 * (n - 1))
                for two in range(2):
                    for c in range(2):
                        columns(2 * (J_UP + 2 * n + two) + c, ps[:, 2 * (n % 2) + two, T * c:T * c + T], x_hi, h_lo)

            def down(f, m):
                n = 2 * J_DN + f
                return split_product(ps[:, 4 + m // 2, T * (m % 2):T * (m % 2) + T], part_hi(n)[:, m, :],
                                     part_of(n, ring_r)[:, m, :], f_hi[:, f, :], f_lo[:, f, :], f == 0 and m % 2 == 0,
                                     f == FC - 1)

            for f in range(FC - 2):
                pe.wait_ge(w_lo_set, N_PARTS1 + 2 * J_DN + f + 1)
                pe.wait_ge(f_lo_set, f // 2 + 1)
                for m in range(KC):
                    last = down(f, m)
                last.then_inc(part_mm, 1)
            pe.wait_ge(w_lo_set, N_PARTS1 + 2 * N_JOBS)
            pe.wait_ge(f_lo_set, FC // 2)
            pe.wait_ge(conv_set, FC)
            for m in range(KC):
                for f in (FC - 2, FC - 1):
                    last = down(f, m)
                if m % 2:
                    last.then_inc(y_mm, 1)
                if m > 1 and m % 2:
                    sum_squares(NORM_LAST, sq4, 0, T, m - 3, m - 1)
            sum_squares(NORM_LAST, sq4, 0, T, KC - 2, KC)

        @block.scalar
        def _(act):
            A = nc.scalar.activation

            tables = [0]

            def load_table(func):
                at = tables[0]
                tables[0] += 1
                A(unread[:, at:at + 1], eps[0:1, 0:1], func)

            act.dma_start(small[:], io["small"]).then_inc(small_in, 16)
            act.dma_start(buckets[0:33], io["buckets"]).then_inc(bucket_in, 16)
            def square(norm, k, dst, src, scale=1.0):
                if k >= 2:
                    act.wait_ge(sq_used, KC * norm + k - 1)
                A(dst, src, ACT.Square, scale=scale).then_inc(sq_set, 1)

            def root(norm, bank):
                act.wait_ge(sq_used, KC * (norm + 1))
                A(nrm[:, 1], ps[:, bank, 0:T], ACT.Sqrt, bias=eps[:, 0:1], scale=1.0 / D).then_inc(root_set, 1)

            act.wait_ge(ones_set, 2)
            load_table(ACT.Sqrt)
            act.wait_ge(x_in, 16)
            act.wait_ge(ctx_in, 16)
            for k in range(KC):
                if k >= 2:
                    act.wait_ge(sq_used, k - 1)
                A(sq[:, k % 2, 0:T], xT[:, k], ACT.Square)
                A(sq[:, k % 2, T:2 * T], hx[:, k, T:2 * T], ACT.Square).then_inc(sq_set, 1)
            act.wait_ge(small_in, 16)
            A(csig[:], col("cvec"), ACT.Sigmoid).then_inc(csig_set, 1)
            load_table(ACT.Sqrt)
            act.wait_ge(sq_used, KC)
            A(rope1, ps[:, 7, :], ACT.Sqrt, bias=eps[:, 0:1], scale=1.0 / D).then_inc(root_set, 1)

            def ada_copy(n, bank):
                act.wait_ge(ada_mm, n + 1)
                if n >= 2:
                    act.wait_ge(ada_t, n - 1)
                A(modrow[:, n % 2], ps[:, bank, 0:P], ACT.Copy).then_inc(ada_row, 1)

            for n in range(4):
                ada_copy(n, 5)

            def split_hi1(p):
                u = PARTS1[p][0]
                act.wait_ge(slot_full[u % RING1], filled(u))
                if p >= HI_PARTS:
                    act.wait_ge(proj_mm, LAST_JOB[p - HI_PARTS] + 1)
                A(part_hi(p), part1(p, ring), ACT.Copy).then_inc(w_hi_set, 1)

            split_hi1(0)
            for k in range(KC):
                act.wait_ge(hx_x, k + 1)
                A(hx_hi[:, k, 0:T], hx[:, k, 0:T], ACT.Copy).then_inc(h_hi_set, 1)
            for p in range(1, HI_PARTS):
                split_hi1(p)
            for k in range(KC):
                act.wait_ge(hx_c, k + 1)
                A(hx_hi[:, k, T:2 * T], hx[:, k, T:2 * T], ACT.Copy).then_inc(h_hi_set, 1)

            def copy_job(n):
                name, i = JOBS[n]
                src = ps[:, n % 2, :]
                if n in COPIED:
                    act.wait_ge(proj_mm, n + 1)
                if name in ("ka", "kb"):
                    act.wait_ge(proj_dve, upto(ROPED, n))
                if name == "ka":
                    last = A(ka[:, i, T:2 * T], src[:, T:2 * T], ACT.Copy)
                elif name == "kb":
                    for kv in range(2):
                        for half in range(2):
                            last = A(kb[HD * half:HD * half + HD, kv, T:2 * T], src[HD * kv:HD * kv + HD, T:2 * T], ACT.Copy)
                elif name == "va":
                    t, c0 = 2 * (i % 2), T * (i // 2)
                    last = A(va[:, t:t + 2, c0:c0 + T], src.rearrange("p (a b) -> p a b", a=2), ACT.Copy)
                elif name == "vb":
                    last = A(vb_t, src, ACT.Copy)
                elif name == "vt":
                    last = A(vb, src.rearrange("p (a b) -> p a b", a=4), ACT.Copy)
                if n in COPIED:
                    last.then_inc(proj_act, 1)
                for p in split_after(n):
                    split_hi1(p)

            for n in range(EARLY):
                copy_job(n)
                if n == BIAS_JOB:
                    for g in range(2):
                        act.wait_ge(brow_mm, g + 1)
                        A(brow[0:8, g], ps[0:8, ROW_BANKS[g], :], ACT.Copy).then_inc(brow_set, 1)
                    act.wait_ge(brow_set, 2)
                    act.dma_start(bias_rows.ap().rearrange("(g h) n -> h g n", g=2), brow[0:8]).then_inc(bias_out, 16)
                if MEM_JOB <= n < MEM_JOB + 4:
                    act.wait_ge(mem_in, 16)
                    for k in range(2 * (n - MEM_JOB), 2 * (n - MEM_JOB) + 2):
                        square(NORM_MEM, k, sq_m[:, k % 2], memT[:, k])
                if n == MEM_JOB + 4:
                    root(NORM_MEM, 7)
            act.wait_ge(lam_set, 1)
            A(lamv[:, 2:4], lamv[:, 0:2], ACT.Exp).then_inc(lame_set, 1)
            act.wait_ge(subln_set, 1)
            act.wait_ge(bias_out, 16)

            def copy_turn(kind, s, c=0):
                act.wait_ge(pt_mm, turn(kind, s, c) + 1)
                src = ps[:, 2, :].rearrange("p (a b) -> p a b", a=4)
                if kind == "y":
                    A(yT[:, 0:4, P * s:P * s + P], src, ACT.Copy, scale=subln_s[:, 0:1]).then_inc(pt_set, 1)
                else:
                    if s >= 2:
                        act.wait_ge(pv_mm, s - 1)
                    A(pT_a[s % 2][:, c], src, ACT.Copy).then_inc(pt_set, 1)

            def copy_memory(n):
                act.wait_ge(kv_mm, n + 1)
                kind, i, _, bank = KV_JOBS[n]
                if kind == "k":
                    A(k_me[:, 2 * i:2 * i + 2], ps[:, bank, :].rearrange("p (a b) -> p a b", a=2),
                      ACT.Copy).then_inc(kv_act, 1)
                else:
                    A(v_me[:, i], ps[:, bank, :], ACT.Copy).then_inc(kv_act, 1)

            for a in range(N_AT + 2):
                if ADA_STEP <= a <= N_AT:
                    copy_turn("p", a - 1)
                if a < N_AT:
                    b, j = a % 2, step_a(a)[1]
                    act.wait_ge(max_set, a + 1)
                    if a >= 2:
                        act.wait_ge(pt_mm, turn("p", a - 2, int(a - 2 >= N_DA)) + 1)
                    for c in range(2):
                        A(e_a[:, b, c], ps[:, 4 + 2 * b + c, :], ACT.Exp, bias=negm[:, b, c:c + 1], scale=QK_SCALE,
                          accum_out=esum[:, b, c:c + 1]).then_inc(exp_set, 1)
                    if a >= N_DA:
                        for c in range(2):
                            A(esink[:, b, c:c + 1], col("sink")[:, 2 * j + c:2 * j + c + 1], ACT.Exp,
                              bias=negm[:, b, c:c + 1]).then_inc(sinkexp_set, 1)
                if ada_at(a) is not None:
                    ada_copy(ada_at(a), 1)
                if a in (6, 10):
                    act.wait_ge(oms_set, a // 6 if a == 6 else 2)
                    A(oss[:], oss[:], ACT.Sqrt).then_inc(oroot_set, 1)
                if EARLY + a < len(JOBS):
                    copy_job(EARLY + a)
                if kv_at(a) is not None:
                    copy_memory(kv_at(a))
                if 1 <= a < ADA_STEP:
                    copy_turn("p", a - 1)
                if a - 2 in (3, 7):
                    act.wait_ge(pv_mm, a - 1)
                    if a - 2 == 7:
                        act.wait_ge(pt_mm, turn("y", 0) + 1)
                    A(y_da, ps[:, 3, :], ACT.Copy).then_inc(ov_set, 1)
                    act.wait_ge(ov_set, (a - 2) // 4 + 1)
                    A(o_sq, y_da, ACT.Square).then_inc(osq_set, 1)
                if N_DA < a <= N_AT:
                    copy_turn("p", a - 1, 1)
                if a - 2 >= N_DA:
                    qt, j = step_a(a - 2)
                    act.wait_ge(pv_mm, a - 1)
                    A(yT[:, 4 + j, P * qt:P * qt + P], ps[:, 3, 0:P], ACT.Copy).then_inc(pv_set, 1)
                if a in (7, 11):
                    copy_turn("y", a // 8)

            load_table(ACT.Sqrt)
            act.wait_ge(pv_mm, N_AT)
            act.dma_start(b_dn[0:N_EXPERTS], io["b_down"][0]).then_inc(bdn_in, 16)
            act.wait_ge(bias_out, 16)
            bias_loads(act, 0, bias_in)
            for k in range(KC):
                act.wait_ge(x1_set, k + 1)
                square(NORM2, k, sq2[:, k % 2], xT[:, k])
            root(NORM2, 2)
            load_table(ACT.Exp)
            for k in range(KC):
                act.wait_ge(hx2_pre, k + 1)
                A(hx2[:, k], hx2[:, k], ACT.Identity, bias=modcol[:, 24 + k, 0:1]).then_inc(hx2_set, 1)
            copy_memory(3)
            act.wait_ge(bgu_zero, 1)
            act.dma_start(b_gu[0:N_EXPERTS], io["b_gate_up"][0]).then_inc(bgu_in, 16)
            for n in range(4):
                act.wait_ge(tm_mm, n + 1)
                A(hx2tm[:, n // 2, 512 * (n % 2):512 * (n % 2) + 512], ps[:, n % 2, :], ACT.Copy).then_inc(tm_set, 1)
                if n == 1:
                    act.wait_ge(top_set, 1)
                    for t in range(TT):
                        A(top_e[:, t], top_v[:, t, 0:TOP_K], ACT.Exp, bias=top_n[:, t:t + 1],
                          accum_out=top_s[:, t:t + 1]).then_inc(tope_set, 1)
            act.wait_ge(gt_mm, 1)
            A(gates_t[:], ps[0:N_EXPERTS, 5, 0:T], ACT.Copy).then_inc(gt_set, 1)
            load_table(ACT.Sigmoid)

            def round_act(S, r):
                A(y_e, small[:, SMALL_AT["cos"][0]:SMALL_AT["cos"][0] + 512], ACT.Copy, scale=0.0).then_inc(S.y_ready, 1)
                A(sgt, cos, ACT.Copy, scale=0.0).then_inc(S.sgt_ready, 1)

                def copy_gather(half, n):
                    act.wait_ge(S.gather_mm, n)
                    A(xg[:, 4 * half:4 * half + 4, :], ps[:, 2, :].rearrange("p (a b) -> p a b", a=4),
                      ACT.Copy).then_inc(S.x_ready, 1)

                for half in range(2):
                    copy_gather(half, r * 34 + (half + 1))
                with act.Fori(0, N_EXPERTS // 2) as i:
                    for j in range(2):
                        e = i * 2 + j
                        act.wait_ge(S.g_ready, r * 32 + (e + 1))
                        A(sig_e, g_e, ACT.Sigmoid, scale=SWIGLU_ALPHA).then_inc(S.sig_ready, 1)
                        act.wait_ge(S.sgt_mm, r * 32 + (e + 1))
                        A(sgt, ps[:, 3, 0:T], ACT.Copy).then_inc(S.sgt_ready, 1)
                        if j == 1:
                            for half in range(2):
                                copy_gather(half, r * 34 + (i * 2 + (half + 3)))
                        act.wait_ge(S.at_mm, r * 32 + (e + 1))
                        A(aT_e, ps[:, 2, :].rearrange("p (a b) -> p a b", a=4), ACT.Copy).then_inc(S.at_ready, 1)
                        act.wait_ge(S.units, (r * N_EXPERTS + e) * UNITS_EXPERT + (UNITS_EXPERT + S.units0))
                        A(y_e, ps[:, 3, :], ACT.Copy).then_inc(S.y_ready, 1)

            round_act(MAIN, 0)
            act.wait_ge(most_set, 1)
            with act.If(act.value_load(most_i[0:1, 0:1], min_val=0, max_val=T) > SLOTS):
                act.wait_ge(MAIN.round_done, 1)
                with act.Fori(0, ROUNDS_MORE) as r:
                    round_act(MORE, r)
                    act.wait_ge(MORE.round_done, r + 1)

            load_table(ACT.Sqrt)

            def split_hi_part(n):
                act.wait_ge(slot_full[SLOT_C[PARTS[n][0] % RING2]], filled_c(PARTS[n][0]))
                if n >= HI_PARTS:
                    act.wait_ge(part_mm, n - HI_PARTS + 1)
                A(part_hi(n), part_of(n, ring), ACT.Copy).then_inc(w_hi_set, 1)

            def split_hi(j):
                split_hi_part(2 * j)
                split_hi_part(2 * j + 1)

            def copy_c(n):
                name, i = C_JOBS[n]
                act.wait_ge(part_mm, done(n))
                src = ps[:, n % 2, :]
                pair = src.rearrange("p (a b) -> p a b", a=2)
                if name == "gate":
                    A(gate[i // 4][:, 2 * (i % 4):2 * (i % 4) + 2], pair, ACT.Tanh, scale=0.5).then_inc(c_act, 1)
                    return
                if name == "kvsw":
                    for kv in range(2):
                        for half in range(2):
                            A(k_sw[HD * half:HD * half + HD, kv], ps[HD * kv:HD * kv + HD, n % 2, 0:T], ACT.Copy)
                    dst, src = v_sw, ps[:, n % 2, T:2 * T].rearrange("p (a b) -> p a b", a=2)
                elif name == "vmb":
                    dst, src = v_mb[:, :, T * i:T * i + T], pair
                else:
                    to = {"qmb": q_mb, "kmb": k_mb, "qsw": q_sw, "qme": q_me}[name]
                    dst, src = to[:, 2 * i:2 * i + 2], pair
                A(dst, src, ACT.Copy).then_inc(c_act, 1)

            for n in range(HI_PARTS):
                split_hi_part(n)
            for k in range(KC):
                act.wait_ge(x2_pre, k + 1)
                if k >= 2:
                    act.wait_ge(sq_used, KC * NORM_MIX + k - 1)
                A(sq_mix[:, k % 2, 0:T], xT[:, k], ACT.Square)
                A(sq_mix[:, k % 2, T:2 * T], xT[:, k], ACT.Square, scale=col("final_g")[:, k:k + 1]).then_inc(sq_set, 1)
            act.wait_ge(ms_set, 1)
            A(nrm[:, 1], nrm[:, 0], ACT.Sqrt).then_inc(root_set, 1)
            act.wait_ge(fin_ms, 1)
            A(fin[:, 0], fin[:, 0], ACT.Sqrt).then_inc(fin_root, 1)
            load_table(ACT.Exp)
            for k in range(KC):
                act.wait_ge(h_set, k + 1)
                A(x_hi[:, k], h[:, k], ACT.Copy).then_inc(h_hi_set, 1)
            for n in range(C_EARLY):
                copy_c(n)
                if n + 2 <= C_EARLY:
                    split_hi(n + 2)

            def copy_turn_c(s):
                kind, j, qt, keys, heads = step_c(s)
                nk = keys // P
                act.wait_ge(c_pt, s + 1)
                if s >= 2:
                    act.wait_ge(c_pv, s - 1)
                A(pT_c[s % 2][:, 0:heads, 0:nk, :], ps[:, 2, 0:P * heads * nk].rearrange("p (a b c) -> p a b c", a=heads, b=nk),
                  ACT.Copy).then_inc(c_pts, 1)

            for a in range(N_C + 2):
                if c_filler(a) is None and 1 <= a <= N_C:
                    copy_turn_c(a - 1)
                if a < N_C:
                    kind, j, qt, keys, heads = step_c(a)
                    b = a % 2
                    act.wait_ge(c_max, a + 1)
                    if a >= 2:
                        act.wait_ge(c_pt, a - 1)
                    for c in range(heads):
                        src = s_c[:, b, c, 0:keys] if kind < 2 else ps[:, 4 + 2 * b, 0:keys]
                        A(e_c[:, b, c, 0:keys], src, ACT.Exp, bias=negm[:, b, c:c + 1],
                          scale=MEM_SCALE if kind == 2 else 1.0, accum_out=esum[:, b, c:c + 1]).then_inc(c_exp, 1)
                    if kind == 1:
                        for c in range(heads):
                            A(esink[:, b, c:c + 1], col("swa_sink")[:, 2 * j + c:2 * j + c + 1], ACT.Exp,
                              bias=negm[:, b, c:c + 1]).then_inc(c_sink, 1)
                if c_filler(a) is not None:
                    split_hi(c_filler(a) + 1)
                    copy_c(c_filler(a))
                    if a >= 1:
                        copy_turn_c(a - 1)
                if a >= 2:
                    kind, j, qt, keys, heads = step_c(a - 2)
                    act.wait_ge(c_pv, a - 1)
                    A(oT[kind][:, j, P * qt:P * qt + P], ps[:, 3, 0:P], ACT.Copy).then_inc(c_pvs, 1)

            load_table(ACT.Sqrt)
            split_hi(J_OUT + 1)
            for i in range(4):
                act.wait_ge(mg_set, 4 + i + 1)
                A(x_hi[:, 2 * i:2 * i + 2], merged[:, 2 * i:2 * i + 2], ACT.Copy).then_inc(mg_hi_set, 1)
            for n in range(4):
                act.wait_ge(part_mm, done(J_OUT + n))
                for c in range(2):
                    square(NORM_POST, 2 * n + c, sq3[:, c], ps[:, n % 2, T * c:T * c + T], scale=0.5)
                A(mix[:, 2 * n:2 * n + 2], ps[:, n % 2, :].rearrange("p (a b) -> p a b", a=2),
                  ACT.Copy, scale=0.5).then_inc(mix_set, 1)
                if n < 3:
                    split_hi(J_OUT + n + 2)
            root(NORM_POST, 2)
            split_hi(J_UP + 1)
            for k in range(KC):
                act.wait_ge(x3_set, k + 1)
                square(NORM_FFN, k, sq3[:, k % 2], xT[:, k])
            root(NORM_FFN, 2)
            load_table(ACT.Gelu_apprx_tanh)
            for k in range(KC):
                act.wait_ge(h_set, KC + k + 1)
                A(x_hi[:, k], h[:, k], ACT.Copy).then_inc(h_hi_set, 1)

            def hidden_hi(n):
                act.wait_ge(f_set, n + 1)
                A(f_hi[:, 2 * n:2 * n + 2], fT[:, 2 * n:2 * n + 2], ACT.Copy).then_inc(f_hi_set, 1)

            for n in range(FC // 2):
                if n >= 2:
                    act.wait_ge(f_set, n - 1)
                for two in range(2):
                    act.wait_ge(part_mm, done(J_UP + 2 * n + two))
                    for c in range(2):
                        ch = FC * two + 2 * n + c
                        A((u_gate, u_val)[two][n % 2][:, c], ps[:, 2 * (n % 2) + two, T * c:T * c + T], ACT.Identity,
                          bias=col("conv_b")[:, ch:ch + 1],
                          scale=col("conv_w")[:, 88 + ch:89 + ch]).then_inc(tap2_set, 1)
                    split_hi(J_UP + 2 * n + two + 2)
                act.wait_ge(conv_set, 2 * n + 1)
                if n >= 1:
                    act.wait_ge(f_set, n)
                A(gelu, u_gate[n % 2], ACT.Gelu_apprx_tanh).then_inc(gelu_set, 1)
                if n >= 1:
                    hidden_hi(n - 1)
            hidden_hi(FC // 2 - 1)
            for j in range(J_DN + 2, N_JOBS):
                split_hi(j)
            load_table(ACT.Sqrt)
            for m in range(KC):
                if m % 2 == 0:
                    act.wait_ge(y_mm, m // 2 + 1)
                square(NORM_LAST, m, sq4[:, m % 2], ps[:, 4 + m // 2, T * (m % 2):T * (m % 2) + T])
            root(NORM_LAST, 0)

        @block.vector
        def _(dve):
            V = nc.vector
            link = chain(dve, dve_chain)

            dve.wait_ge(small_in, 16)
            lam4 = col("lam").rearrange("p (a b d) -> p a b d", a=2, b=2)
            link(V.tensor_tensor(lamw[:], lam4[:, :, 0], lam4[:, :, 1], ALU.mult))
            V.tensor_reduce(lamv[:, 0:2], lamw[:], AX.X, ALU.add).then_inc(lam_set, 1)
            dve.wait_ge(csig_set, 1)
            dve.wait_ge(cs_zero, 1)
            cvec = col("cvec").rearrange("p (k v) -> p k v", v=2)
            V.tensor_tensor(cs[:, :, 0:2], cvec, csig[:].rearrange("p (k v) -> p k v", v=2),
                            ALU.mult).then_inc(cs_set, 1)
            V.tensor_scalar(subln_s[:], col("subln"), 1.0 - LAM_INIT, None, ALU.mult).then_inc(subln_set, 1)
            neg_lam = lamv[:, 1:2]

            dve.wait_ge(root_set, 1)
            link(V.reciprocal(r1, rope1))
            for k in range(KC):
                V.tensor_tensor(hx[:, k, 0:T], xT[:, k], r1[:, 0:T], ALU.mult)
                last = V.tensor_tensor(hx[:, k, T:2 * T], hx[:, k, T:2 * T], r1[:, T:2 * T], ALU.mult)
            link(last)

            rinv = nrm[:, 0]

            def inverse_rms(norm):
                dve.wait_ge(root_set, norm + 1)
                link(V.reciprocal(rinv, nrm[:, 1]))

            def times(dst, src, g):
                return V.scalar_tensor_tensor(dst, src, g, rinv, ALU.mult, ALU.mult)

            def ada_columns(n, bank):
                dve.wait_ge(ada_t, n + 1)
                src = ps[:, bank, 0:P].rearrange("p (j v) -> p j v", j=4)[:, :, 0:2]
                b_mod = col("b_mod")[:, 4 * n:4 * n + 4].unsqueeze(2).to_broadcast([P, 4, 2])
                V.tensor_tensor(modcol[:, 4 * n:4 * n + 4, :], src, b_mod, ALU.add).then_inc(ada_col, 1)

            for n in range(4):
                ada_columns(n, COL_BANKS[n])
            dve.wait_ge(ada_col, 4)
            V.scalar_tensor_tensor(scale1[:], modcol[:, 8:16, :], 1.0,
                                   col("norm1_g").unsqueeze(2).to_broadcast([P, KC, 2]), ALU.add,
                                   ALU.mult).then_inc(scaled1, 1)
            dve.wait_ge(scaled1, 1)
            def split_lo1(p):
                dve.wait_ge(w_hi_set, p + 1)
                V.tensor_tensor(part1(p, ring_r), part1(p, ring), part_hi(p).bitcast(F32),
                                ALU.subtract).then_inc(w_lo_set, 1)

            def normed_lo(k, half):
                at = slice(T * half, T * half + T)
                dve.wait_ge(h_hi_set, KC * half + k + 1)
                V.tensor_tensor(hx_lo[:, k, at], hx[:, k, at], hx_hi[:, k, at].bitcast(F32),
                                ALU.subtract).then_inc(h_lo_set, 1)

            def modulated(k, half):
                at = slice(T * half, T * half + T)
                V.tensor_scalar(hx[:, k, at], hx[:, k, at], scale1[:, k, half:half + 1], modcol[:, k, half:half + 1],
                                ALU.mult, ALU.add).then_inc((hx_x, hx_c)[half], 1)

            for k in range(3):
                modulated(k, 0)
            split_lo1(0)
            for k in range(KC):
                normed_lo(k, 0)
                if k + 3 < KC:
                    modulated(k + 3, 0)
            split_lo1(1)
            for k in range(KC):
                modulated(k, 1)
            split_lo1(2)
            split_lo1(3)
            for k in range(KC):
                normed_lo(k, 1)

            swap16 = [(i + 16) % 32 for i in range(32)]

            def rope(n):
                if n in ROPED:
                    name, i = JOBS[n]
                    dve.wait_ge(proj_mm, n + 1)
                    nt = 2 if name[0] == "q" else 1
                    w = nt * T

                    def wide(x):
                        return x.rearrange("p (a b) -> p a b", a=nt)

                    if n:
                        dve.wait_ge(proj_dve, upto(ROPED, n - 1))
                    V.tensor_tensor(wide(rope1[:, 0:w]), wide(ps[:, n % 2, 0:w]),
                                    cos.unsqueeze(1).to_broadcast([P, nt, T]), ALU.mult)
                    link(V.stream_shuffle(shuf[:, 0:w], ps[:, n % 2, 0:w], swap16))
                    link(V.tensor_tensor(wide(shuf[:, 0:w]), wide(shuf[:, 0:w]),
                                         sin.unsqueeze(1).to_broadcast([P, nt, T]), ALU.mult))
                    if name == "kb":
                        for kv in range(2):
                            rows_ = slice(HD * kv, HD * kv + HD)
                            for half in range(2):
                                last = V.tensor_tensor(kb[HD * half:HD * half + HD, kv, 0:T], rope1[rows_, 0:T],
                                                       shuf[rows_, 0:T], ALU.add)
                    else:
                        dst = (qa if name == "qa" else qb)[:, 2 * i:2 * i + 2] if nt == 2 else ka[:, i:i + 1, 0:T]
                        last = V.tensor_tensor(dst, wide(rope1[:, 0:w]), wide(shuf[:, 0:w]), ALU.add)
                    last.then_inc(proj_dve, 1)
                for p in split_after(n):
                    split_lo1(p)

            for n in range(EARLY):
                rope(n)
                if n == MEM_JOB + 4:
                    inverse_rms(NORM_MEM)
                    for k in range(KC):
                        times(memT[:, k], memT[:, k], col("mem_g")[:, k:k + 1]).then_inc(mem_set, 1)

            def maxima(a):
                qt, j = step_a(a)
                b = a % 2
                banks = ps[:, 4 + 2 * b:6 + 2 * b, :]
                dve.wait_ge(sc_mm, a + 1)
                if a >= N_DA:
                    far = banks[:, :, P:2 * P] if qt == 0 else banks[:, :, 0:P]
                    link(V.tensor_tensor(far, far, col("wmask")[:, P * qt:P * qt + P].unsqueeze(1).to_broadcast([P, 2, P]),
                                         ALU.add))
                link(V.tensor_reduce(mx[:, b], banks, AX.X, ALU.max))
                if a < N_DA:
                    V.tensor_scalar(negm[:, b], mx[:, b], -QK_SCALE, None, ALU.mult).then_inc(max_set, 1)
                else:
                    link(V.scalar_tensor_tensor(mx[:, b], mx[:, b], QK_SCALE, col("sink")[:, 2 * j:2 * j + 2], ALU.mult,
                                                ALU.max))
                    V.tensor_scalar(negm[:, b], mx[:, b], -1.0, None, ALU.mult).then_inc(max_set, 1)

            def normalise(s):
                b = s % 2
                dve.wait_ge(exp_set, 2 * (s + 1))
                if s < N_DA:
                    link(V.reciprocal(rsum[:, b], esum[:, b]))
                    link(V.tensor_tensor(fneg[:], rsum[:, b, 1:2], neg_lam, ALU.mult))
                    link(V.tensor_scalar(e_a[:, b, 1], e_a[:, b, 1], fneg[:, 0:1], None, ALU.mult))
                    V.scalar_tensor_tensor(e_a[:, b, 0], e_a[:, b, 0], rsum[:, b, 0:1], e_a[:, b, 1], ALU.mult,
                                           ALU.add).then_inc(p_set, 1)
                else:
                    dve.wait_ge(sinkexp_set, 2 * (s - N_DA + 1))
                    link(V.tensor_tensor(tot[:], esum[:, b], esink[:, b], ALU.add))
                    link(V.reciprocal(rsum[:, b], tot[:]))
                    for c in range(2):
                        V.tensor_scalar(e_a[:, b, c], e_a[:, b, c], rsum[:, b, c:c + 1], None,
                                        ALU.mult).then_inc(p_set, 1)

            for a in range(N_AT + 1):
                if a >= 1:
                    normalise(a - 1)
                if a < N_AT:
                    maxima(a)
                if a == 0:
                    dve.wait_ge(lame_set, 1)
                    link(V.tensor_tensor(lamv[:, 0:1], lamv[:, 3:4], lamv[:, 2:3], ALU.subtract))
                    link(V.tensor_scalar(lamv[:, 1:2], lamv[:, 0:1], -LAM_INIT, None, ALU.add))
                if EARLY + a < len(JOBS):
                    rope(EARLY + a)
                if ada_at(a - 1) is not None:
                    ada_columns(ada_at(a - 1), 0)
                heads = lambda x: x.rearrange("p (a b) -> p a b", a=4)
                if a in (5, 9):
                    dve.wait_ge(osq_set, a // 4)
                    link(V.tensor_reduce(oss[:], heads(o_sq), AX.X, ALU.add))
                    V.tensor_scalar(oss[:], oss[:], 1.0 / P, EPS, ALU.mult, ALU.add).then_inc(oms_set, 1)
                if a in (6, 10):
                    dve.wait_ge(oroot_set, a // 5)
                    link(V.reciprocal(oss[:], oss[:]))
                    V.tensor_tensor(heads(y_da), heads(y_da), oss[:].unsqueeze(2).to_broadcast([P, 4, P]),
                                    ALU.mult).then_inc(yda_set, 1)

            dve.wait_ge(ada_col, 12)
            V.tensor_tensor(both_g[:], col("final_g"), col("mix_pre"), ALU.mult)
            link(V.scalar_tensor_tensor(scale2[:], modcol[:, 32:40, 0], 1.0, col("norm2_g"), ALU.add, ALU.mult))
            for m in range(KC):
                dve.wait_ge(out_mm, m // 2 + 1)
                V.scalar_tensor_tensor(xT[:, m], ps[:, m // 2 % 2, T * (m % 2):T * (m % 2) + T], modcol[:, 16 + m, 0:1],
                                       xT[:, m], ALU.mult, ALU.add).then_inc(x1_set, 1)
            inverse_rms(NORM2)
            for k in range(KC):
                times(hx2[:, k], xT[:, k], scale2[:, k:k + 1]).then_inc(hx2_pre, 1)

            dve.wait_ge(log_mm, TT)
            V.tensor_tensor(logits[:], ps[:, 3, 0:64].rearrange("p (a b) -> p a b", a=TT),
                            col("b_router").unsqueeze(1).to_broadcast([P, TT, N_EXPERTS]), ALU.add).then_inc(log_set, 1)
            dve.wait_ge(log_set, 1)
            for t in range(TT):
                last = V.max(top_v[:, t], logits[:, t])
            link(last)
            V.tensor_scalar(top_n[:], top_v[:, :, 0], -1.0, None, ALU.mult).then_inc(top_set, 1)
            for t in range(TT):
                last = V.max_index(top_i[:, t], top_v[:, t], logits[:, t])
            link(last)
            link(V.tensor_copy(top_f[:], top_i[:]))
            for t in range(TT):
                last = V.tensor_tensor(pick[:, t], col("iota_expert").unsqueeze(1).to_broadcast([P, TOP_K, N_EXPERTS]),
                                       top_f[:, t, 0:TOP_K].unsqueeze(2).to_broadcast([P, TOP_K, N_EXPERTS]),
                                       ALU.is_equal)
            link(last)
            for t in range(TT):
                last = V.tensor_reduce(chosen[:, t], pick[:, t].rearrange("p k e -> p e k"), AX.X, ALU.add)
            dve.wait_ge(tope_set, TT)
            link(V.reciprocal(top_s[:], top_s[:]))
            link(V.tensor_tensor(top_e[:], top_e[:], top_s[:].unsqueeze(2).to_broadcast([P, TT, TOP_K]), ALU.mult))
            for t in range(TT):
                last = V.tensor_tensor(pick[:, t], pick[:, t],
                                       top_e[:, t].unsqueeze(2).to_broadcast([P, TOP_K, N_EXPERTS]), ALU.mult)
            link(last)
            V.memset(gates[:, :, N_EXPERTS:N_EXPERTS + 2], 0.0)
            V.memset(rank[:, :, N_EXPERTS:N_EXPERTS + 2], -1.0)
            for t in range(TT):
                last = V.tensor_reduce(gates[:, t, 0:N_EXPERTS], pick[:, t].rearrange("p k e -> p e k"), AX.X, ALU.add)
            last.then_inc(route_set, 1)
            dve.wait_ge(rank_mm, 1)
            link(V.tensor_reduce(most[:], ps[:, 4, 64:96], AX.X, ALU.max))
            link(V.scalar_tensor_tensor(rank[:, :, 0:N_EXPERTS], ps[:, 4, 0:64].rearrange("p (a b) -> p a b", a=TT), 1.0,
                                        chosen[:], ALU.add, ALU.mult))
            link(V.tensor_scalar(rank[:, :, 0:N_EXPERTS], rank[:, :, 0:N_EXPERTS], -1.0, None, ALU.add))
            V.tensor_copy(most_i[:], most[:]).then_inc(most_set, 1)

            reverse32 = [31 - i for i in range(32)]

            def round_dve(S, r, first):
                def one_hots(e0):
                    for t in range(TT):
                        for jj in range(2):
                            last = V.tensor_scalar(s_hot[:, t, jj], col("iota_slot")[:, 0:SLOTS],
                                                   rank[:, t, bass.ds(e0 + jj, 1)], None, ALU.is_equal)
                    last.then_inc(S.s_ready, 1)

                def selector(e):
                    V.tensor_copy(esel, ident[:, bass.ds(e, 1)].to_broadcast([P, SLOTS])).then_inc(S.sel_ready, 1)

                def gated(e, also=None):
                    for t in range(TT):
                        last = V.tensor_scalar(sg_hot[:, t], col("iota_slot"), rank[:, t, bass.ds(e, 1)],
                                               gates[:, t, bass.ds(e, 1)], ALU.is_equal, ALU.mult)
                        if t == 0 and also is not None:
                            last.then_inc(also, 1)
                    last.then_inc(S.sg_ready, 1)

                if S is MORE:
                    V.tensor_scalar(rank[:], rank[:], -float(SLOTS), None, ALU.add).then_inc(S.shifted, 1)
                    dve.wait_ge(S.shifted, r + 1)
                one_hots(0)
                selector(0)
                gated(0, S.h_free)
                if first is not None:
                    first()
                with dve.Fori(0, N_EXPERTS // 2) as i:
                    for j in range(2):
                        e = i * 2 + j
                        if j == 0:
                            dve.wait_ge(S.gather_mm, r * 34 + (i * 2 + 2))
                            one_hots(i * 2 + 2)
                        dve.wait_ge(S.units, (r * N_EXPERTS + e) * UNITS_EXPERT + (4 + S.units0))
                        hidden = ps[:, 0:2, :].rearrange("p n (f two) -> p n f two", two=2)
                        two_banks = lambda x: x.rearrange("p (n f) -> p n f", n=2)
                        V.tensor_scalar(two_banks(g_e), hidden[:, :, :, 0], SWIGLU_LIMIT, None,
                                        ALU.min).then_inc(S.g_ready, 1)
                        V.tensor_scalar(two_banks(lin_e), hidden[:, :, :, 1], -SWIGLU_LIMIT, SWIGLU_LIMIT, ALU.max,
                                        ALU.min).then_inc(S.h_free, 1)
                        selector(e + 1)
                        dve.wait_ge(S.h_free, r * 33 + (e + 2))
                        V.scalar_tensor_tensor(u_e, lin_e, 1.0, g_e, ALU.add, ALU.mult).then_inc(S.u_ready, 1)
                        dve.wait_ge(S.sig_ready, r * 32 + (e + 1))
                        dve.wait_ge(S.u_ready, r * 32 + (e + 1))
                        V.tensor_tensor(a_e, u_e, sig_e, ALU.mult).then_inc(S.a_ready, 1)
                        dve.wait_ge(S.sgt_mm, r * 32 + (e + 1))
                        gated(e + 1)
                dve.wait_ge(S.gather_mm, r * 34 + 34)
                dve.wait_ge(S.sg_ready, r * 33 + 33)
                dve.wait_ge(S.round_done, r + 1)

            def before_experts():
                dve.wait_ge(bias_in, 16 * BIAS_LOADS)
                flat = arena[:, AT_BIAS:AT_BIAS + 8 * 384]
                link(V.stream_shuffle(flat, flat, reverse32))

            round_dve(MAIN, 0, before_experts)
            dve.wait_ge(most_set, 1)
            with dve.If(dve.value_load(most_i[0:1, 0:1], min_val=0, max_val=T) > SLOTS):
                with dve.Fori(0, ROUNDS_MORE) as r:
                    round_dve(MORE, r, None)

            for m in range(KC):
                V.scalar_tensor_tensor(xT[:, m], ps[:, 4 + m // 2, T * (m % 2):T * (m % 2) + T], modcol[:, 40 + m, 0:1],
                                       xT[:, m], ALU.mult, ALU.add).then_inc(x2_pre, 1)
            def split_lo_part(n):
                dve.wait_ge(w_hi_set, N_PARTS1 + n + 1)
                V.tensor_tensor(part_of(n, ring_r), part_of(n, ring), part_hi(n).bitcast(F32),
                                ALU.subtract).then_inc(w_lo_set, 1)

            def split_lo(j):
                split_lo_part(2 * j)
                split_lo_part(2 * j + 1)

            for n in range(HI_PARTS):
                split_lo_part(n)
            dve.wait_ge(sq_used, KC * (NORM_MIX + 1))
            V.tensor_scalar(fin[:, 0], ps[:, 2, 0:T], 1.0 / D, EPS, ALU.mult, ALU.add).then_inc(fin_ms, 1)
            link(V.tensor_scalar(fin[:, 1], ps[:, 2, 0:T], EPS / D, EPS * EPS, ALU.mult, ALU.add))
            V.scalar_tensor_tensor(nrm[:, 0], ps[:, 2, T:2 * T], 1.0 / D, fin[:, 1], ALU.mult, ALU.add).then_inc(ms_set, 1)
            dve.wait_ge(root_set, NORM_MIX + 1)
            link(V.reciprocal(rinv, nrm[:, 1]))

            def normed_parts(g, before):
                for k in range(KC + 2):
                    if k < KC:
                        times(h[:, k], xT[:, k], g[:, k:k + 1]).then_inc(h_set, 1)
                    if k >= 2:
                        dve.wait_ge(h_hi_set, before + k - 1)
                        V.tensor_tensor(h_lo[:, k - 2], h[:, k - 2], x_hi[:, k - 2].bitcast(F32),
                                        ALU.subtract).then_inc(h_lo_set, 1)

            normed_parts(both_g, 2 * KC)
            dve.wait_ge(fin_root, 1)
            link(V.reciprocal(fin[:, 0], fin[:, 0]))
            for k in range(KC):
                V.scalar_tensor_tensor(xT[:, k], xT[:, k], col("final_g")[:, k:k + 1], fin[:, 0], ALU.mult, ALU.mult)
            for n in range(C_EARLY):
                if n + 2 <= C_EARLY:
                    split_lo(n + 2)

            def maxima_c(a):
                kind, j, qt, keys, heads = step_c(a)
                b = a % 2
                banks = ps[:, 4 + 2 * b:4 + 2 * b + heads, 0:keys]
                if a == BIAS_STEP:
                    dve.wait_ge(sw_bias_in, 16 * BIAS_LOADS)
                    flat = arena[:, AT_BIAS:AT_BIAS + 8 * 384]
                    link(V.stream_shuffle(flat, flat, reverse32))
                dve.wait_ge(c_sc, a + 1)
                src = banks
                if kind < 2:
                    src = s_c[:, b, :, 0:keys]
                    link(V.scalar_tensor_tensor(src, banks, QK_SCALE, bias[:, 2 * j:2 * j + 2, P * qt:P * qt + keys],
                                                ALU.mult, ALU.add))
                link(V.tensor_reduce(mx[:, b, 0:heads], src, AX.X, ALU.max))
                if kind == 1:
                    link(V.tensor_tensor(mx[:, b], mx[:, b], col("swa_sink")[:, 2 * j:2 * j + 2], ALU.max))
                V.tensor_scalar(negm[:, b, 0:heads], mx[:, b, 0:heads], -MEM_SCALE if kind == 2 else -1.0, None,
                                ALU.mult).then_inc(c_max, 1)

            def normalise_c(s):
                kind, j, qt, keys, heads = step_c(s)
                b = s % 2
                dve.wait_ge(c_exp, sum(step_c(x)[4] for x in range(s + 1)))
                total = esum[:, b, 0:heads]
                if kind == 1:
                    dve.wait_ge(c_sink, 2 * (s - 15))
                    link(V.tensor_tensor(tot[:], esum[:, b], esink[:, b], ALU.add))
                    total = tot[:]
                link(V.reciprocal(rsum[:, b, 0:heads], total))
                for c in range(heads):
                    last = V.tensor_scalar(e_c[:, b, c, 0:keys], e_c[:, b, c, 0:keys], rsum[:, b, c:c + 1], None, ALU.mult)
                last.then_inc(c_p, 1)

            part = [buf(AT_E2 + 512 * b, 2, T) for b in range(2)]

            def merge(n):
                b, i = n // 4, n % 4
                chunks = slice(2 * i, 2 * i + 2)
                dve.wait_ge(br_mm, n + 1)
                src = ps[:, n % 2, :].rearrange("p (a b) -> p a b", a=2)
                dst = gate[0][:, chunks] if b == 0 else part[n % 2]
                V.scalar_tensor_tensor(dst, gate[b][:, chunks], 1.0, src, ALU.add, ALU.mult).then_inc(br_used, 1)
                if b:
                    dve.wait_ge(br_used, n + 1)
                    if b == 2:
                        dve.wait_ge(mg_set, n - 7)
                    V.tensor_tensor(merged[:, chunks], (gate[0] if b == 1 else merged)[:, chunks], part[n % 2],
                                    ALU.add).then_inc(mg_set, 1)

            def merged_low(i):
                dve.wait_ge(mg_hi_set, i + 1)
                V.tensor_tensor(merged_lo[:, 2 * i:2 * i + 2], merged[:, 2 * i:2 * i + 2],
                                x_hi[:, 2 * i:2 * i + 2].bitcast(F32), ALU.subtract).then_inc(mg_lo_set, 1)

            for a in range(N_C + 1):
                if a >= 1:
                    normalise_c(a - 1)
                if a < N_C:
                    maxima_c(a)
                if c_filler(a) is not None:
                    split_lo(c_filler(a) + 1)
                if a >= BR_STEP:
                    merge(a - BR_STEP)

            for n in range(N_C + 1 - BR_STEP, 12):
                merge(n)
                if n == 5:
                    split_lo(J_OUT + 1)
                if n >= 9:
                    merged_low(n - 9)
            merged_low(3)
            for n in range(3):
                split_lo(J_OUT + n + 2)
            inverse_rms(NORM_POST)
            for k in range(KC + 1):
                if k < KC:
                    times(mix[:, k], mix[:, k], col("mix_post")[:, k:k + 1]).then_inc(y_set, 1)
                if k >= 1:
                    dve.wait_ge(y_set, k)
                    V.tensor_tensor(xT[:, k - 1], xT[:, k - 1], mix[:, k - 1], ALU.add).then_inc(x3_set, 1)
            inverse_rms(NORM_FFN)
            normed_parts(col("ffn_pre"), 3 * KC)
            split_lo(J_UP + 1)

            def product(n):
                dve.wait_ge(gelu_set, n + 1)
                dve.wait_ge(conv_set, 2 * n + 2)
                V.tensor_tensor(fT[:, 2 * n:2 * n + 2], gelu, u_val[n % 2], ALU.mult).then_inc(f_set, 1)

            def hidden_lo(n):
                dve.wait_ge(f_hi_set, n + 1)
                V.tensor_tensor(f_lo[:, 2 * n:2 * n + 2], fT[:, 2 * n:2 * n + 2],
                                f_hi[:, 2 * n:2 * n + 2].bitcast(F32), ALU.subtract).then_inc(f_lo_set, 1)

            for n in range(FC // 2):
                for two in range(2):
                    u = (u_gate, u_val)[two][n % 2]
                    for tap, late in ((1, 1), (0, 2)):
                        for c in range(2):
                            ch = FC * two + 2 * n + c
                            src = ps[:, 2 * (n % 2) + two, T * c:T * c + T]
                            if tap:
                                dve.wait_ge(tap2_set, 4 * n + 2 * two + 2)
                            last = V.scalar_tensor_tensor(u[:, c, late:T], src[:, 0:T - late],
                                                          col("conv_w")[:, 44 * tap + ch:44 * tap + ch + 1], u[:, c, late:T],
                                                          ALU.mult, ALU.add)
                        if tap:
                            link(last)
                        else:
                            last.then_inc(conv_set, 1)
                    split_lo(J_UP + 2 * n + two + 2)
                if n >= 1:
                    product(n - 1)
                if n >= 2:
                    hidden_lo(n - 2)
            product(FC // 2 - 1)
            hidden_lo(FC // 2 - 2)
            hidden_lo(FC // 2 - 1)
            for j in range(J_DN + 2, N_JOBS):
                split_lo(j)

            inverse_rms(NORM_LAST)
            y = buf(AT_UB, KC, T)
            for k in range(KC + 1):
                if k < KC:
                    times(y[:, k], ps[:, 4 + k // 2, T * (k % 2):T * (k % 2) + T],
                          col("ffn_post")[:, k:k + 1]).then_inc(y_set, 1)
                if k >= 1:
                    dve.wait_ge(y_set, KC + k)
                    V.tensor_tensor(xT[:, k - 1], xT[:, k - 1], y[:, k - 1], ALU.add).then_inc(o_set, 1)


def chunks_first(v):
    return np.asarray(v).reshape(-1, P).T


def features_first(x):
    return np.ascontiguousarray(np.asarray(x)[0].T.reshape(KC, P, T).transpose(1, 0, 2))


def everywhere(v):
    return np.broadcast_to(np.asarray(v).reshape(1, -1), (P, np.asarray(v).size))


def shape_constants():
    f = np.float32
    p = np.arange(P)
    tok = np.arange(T)
    nf = HD // 4
    inv = (f(10000.0) ** (-np.arange(nf, dtype=f) / f(nf))).astype(f)
    row = (p % HD) < HD // 2
    pos = np.where(row[:, None], (tok // GRID_W)[None], (tok % GRID_W)[None]).astype(f)
    angle = (pos * inv[p % nf][:, None]).astype(f)
    sign = np.where((p % 32) < 16, f(-1), f(1))[:, None]
    q, k = p[:, None], p[None, :]
    wmask = np.concatenate([np.where(k > q, f(MASKED), f(0)), np.where(k < q, f(MASKED), f(0))], 1)
    out = {
        "ident": np.eye(P), "tri": (q < k), "cos": np.cos(angle), "sin": np.sin(angle) * sign, "wmask": wmask,
        "iota_slot": everywhere(p % SLOTS), "iota_expert": everywhere(np.arange(N_EXPERTS)),
    }
    d = T - 1 - np.arange(2 * T)
    n = np.maximum(d, 0)
    half = NUM_BUCKETS // 2
    large = half + (np.log(np.maximum(n, 1).astype(f) / f(half)) / f(np.log(128 / half)) * f(half)).astype(np.int32)
    bucket = np.where(n < half, n, np.minimum(large, NUM_BUCKETS - 1))
    hot = (bucket[None] == np.arange(NUM_BUCKETS)[:, None])
    marks = [d < 0, (d < 0) | (d >= 128)]
    onehot = np.concatenate([np.concatenate([hot & ~m[None], m[None]], 0) for m in marks], 1).astype(f)
    return {a: np.ascontiguousarray(b, dtype=f) for a, b in out.items()}, onehot


_BIG = ["w_mod", "w_in", "w_out", "w_gate_up", "w_down", "b_gate_up", "b_down", "w_in_2", "w_mem_kv_2",
        "w_branch_moba_2", "w_branch_swa_2", "w_branch_mem_2", "w_out_2", "w_ffn_up_2", "w_ffn_down_2"]


def kernel(**inputs):
    import concourse.bacc as bacc
    from concourse.bass_utils import run_bass_kernel_spmd as run

    x = {k: np.asarray(v) for k, v in inputs.items()}
    const, onehot = shape_constants()
    cols = dict(const)
    for name, src in (("b_mod", "b_mod"), ("norm1_g", "norm1_g"), ("norm2_g", "norm2_g"), ("final_g", "final_g"),
                      ("mix_pre", "norm_mix_pre_2"), ("mix_post", "norm_mix_post_2"), ("ffn_pre", "norm_ffn_pre_2"),
                      ("ffn_post", "norm_ffn_post_2"), ("mem_g", "norm_mem_2"), ("subln", "subln_g"),
                      ("conv_w", "ffn_conv_w_2"), ("conv_b", "ffn_conv_b_2")):
        cols[name] = chunks_first(x[src])
    cols["cvec"] = np.stack([chunks_first(x["c"]), chunks_first(x["c_ctx"])], 2).reshape(P, 2 * KC)
    cols["w_router"] = x["w_router"][0].reshape(KC, P, N_EXPERTS).transpose(1, 0, 2).reshape(P, KC * N_EXPERTS)
    cols["lam"] = everywhere(np.concatenate([x[n].reshape(-1) for n in ("lam_q1", "lam_k1", "lam_q2", "lam_k2")]))
    for name, src in (("sink", "sink"), ("swa_sink", "swa_sinks_2"), ("b_router", "b_router")):
        cols[name] = everywhere(x[src])
    masked_row = np.full((1, 16), MASKED, np.float32)
    arrays = {
        "small": np.concatenate([cols[n] for n, _ in SMALL], 1),
        "buckets": np.concatenate([onehot, np.concatenate([x["rel_bias_2"], masked_row], 0)], 1),
        "xT": features_first(x["x"]), "ctxT": features_first(x["ctx"]), "memT": features_first(x["mem_2"]),
    }
    for n in _BIG:
        arrays[n] = x[n]
    arrays["w_ffn_up_2"] = x["w_ffn_up_2"].reshape(1, D, 2, FC // 2, 2 * P).transpose(0, 1, 3, 2, 4).reshape(1, D, -1)
    nc = bacc.Bacc("TRN2", target_bir_lowering=False, num_devices=1)
    io = {}
    feeds = {}
    for n, a in arrays.items():
        a = np.ascontiguousarray(a)
        feeds["in_" + n] = a
        io[n] = nc.dram_tensor("in_" + n, a.shape, mybir.dt.from_np(a.dtype), kind="ExternalInput").ap()
    out = nc.dram_tensor("out_0", (P, KC, T), F32, kind="ExternalOutput").ap()
    build(nc, io, out)
    got = run(nc, [feeds], core_ids=[0]).results[0]["out_0"]
    return np.ascontiguousarray(np.asarray(got).transpose(2, 1, 0).reshape(1, T, D))
```
